# Optimizing a Trainium2 kernel written in Bass

```python
import jax, jax.numpy as jnp
from jax import lax
import numpy as np
import math

D_MODEL = 1024
BATCH = 1
SEQ = 256
DEPTH = 1

MLSTM_HEADS = 4
MLSTM_HEAD_DIM = D_MODEL // 8
MLSTM_WIDTH = MLSTM_HEADS * MLSTM_HEAD_DIM
HGRN_HEADS = 4
HGRN_HEAD_DIM = D_MODEL // 8
HGRN_WIDTH = HGRN_HEADS * HGRN_HEAD_DIM
MIX_WIDTH = MLSTM_WIDTH + HGRN_WIDTH
CONV_WIDTH = 4
MLSTM_CHUNK = 64
HGRN_CHUNK = 16
D_FF = ((8 * D_MODEL // 3 + 255) // 256) * 256
FFN_RESIDUAL_WEIGHT = 0.5
EPS = 1e-6
N_MOD = 9
M_NEG = -1e30
PROJ_SPLITS = [MLSTM_WIDTH, MLSTM_WIDTH, MLSTM_WIDTH, MLSTM_WIDTH, 2 * MLSTM_HEADS,
               HGRN_WIDTH, HGRN_WIDTH, HGRN_WIDTH, HGRN_WIDTH]
PROJ_WIDTH = sum(PROJ_SPLITS)
PROJ_IDX = list(np.cumsum(PROJ_SPLITS)[:-1])


def rmsnorm(x, g):
    xf = x.astype(jnp.float32)
    y = xf * lax.rsqrt(jnp.mean(xf * xf, axis=-1, keepdims=True) + EPS)
    return (y * g.astype(jnp.float32)).astype(x.dtype)

def head_rmsnorm(h, g, n_heads):
    B, S, W = h.shape
    hf = h.astype(jnp.float32).reshape(B, S, n_heads, W // n_heads)
    hf = hf * lax.rsqrt(jnp.mean(hf * hf, axis=-1, keepdims=True) + EPS)
    return hf.reshape(B, S, W) * g.astype(jnp.float32)

def split_heads(a, n_heads):
    B, S, W = a.shape
    return a.reshape(B, S, n_heads, W // n_heads).transpose(0, 2, 1, 3)

def merge_heads(a):
    B, H, S, dh = a.shape
    return a.transpose(0, 2, 1, 3).reshape(B, S, H * dh)

def to_chunks(a, L):
    B, H, S = a.shape[:3]
    return jnp.moveaxis(a.reshape(B, H, S // L, L, *a.shape[3:]), 2, 0)

def from_chunks(a):
    nc, B, H, L, d = a.shape
    return jnp.moveaxis(a, 0, 2).reshape(B, H, nc * L, d)

def causal_dwconv(x, w, b):
    C = x.shape[-1]
    y = lax.conv_general_dilated(x, w.astype(x.dtype)[:, None, :], window_strides=(1,),
                                 padding=[(CONV_WIDTH - 1, 0)],
                                 dimension_numbers=('NWC', 'WIO', 'NWC'),
                                 feature_group_count=C)
    return y + b.astype(x.dtype)

def mlstm_chunkwise(q, k, v, log_i, log_f):
    B, H, S, dh = q.shape
    L = MLSTM_CHUNK
    causal = jnp.tril(jnp.ones((L, L), dtype=bool))
    xs = (to_chunks(q, L), to_chunks(k, L), to_chunks(v, L), to_chunks(log_i, L), to_chunks(log_f, L))

    def step(carry, inp):
        C, n, m = carry
        qb, kb, vb, li, lf = inp
        bcum = jnp.cumsum(lf, axis=-1)
        d = bcum[..., :, None] - bcum[..., None, :] + li[..., None, :]
        d = jnp.where(causal, d, -jnp.inf)
        inter = bcum + m[..., None]
        m_t = jnp.maximum(inter, jnp.max(d, axis=-1))
        w = jnp.exp(d - m_t[..., None])
        a = jnp.exp(inter - m_t)
        s = jnp.einsum('bhtd,bhsd->bhts', qb, kb) * w
        num = a[..., None] * jnp.einsum('bhtd,bhde->bhte', qb, C) + jnp.einsum('bhts,bhse->bhte', s, vb)
        den = a * jnp.einsum('bhtd,bhd->bht', qb, n) + jnp.sum(s, axis=-1)
        h = num / jnp.maximum(jnp.abs(den), jnp.exp(-m_t))[..., None]
        m_new = m_t[..., -1]
        g = jnp.exp(bcum[..., -1:] - bcum + li - m_new[..., None])
        decay = jnp.exp(bcum[..., -1] + m - m_new)
        C_new = decay[..., None, None] * C + jnp.einsum('bhs,bhsd,bhse->bhde', g, kb, vb)
        n_new = decay[..., None] * n + jnp.einsum('bhs,bhsd->bhd', g, kb)
        return (C_new, n_new, m_new), h

    init = (jnp.zeros((B, H, dh, dh), jnp.float32), jnp.zeros((B, H, dh), jnp.float32),
            jnp.full((B, H), M_NEG, jnp.float32))
    _, hs = lax.scan(step, init, xs)
    return from_chunks(hs)

def hgrn2_chunkwise(q, k, v, log_f):
    B, H, S, dk = q.shape
    dv = v.shape[-1]
    L = HGRN_CHUNK
    causal = jnp.tril(jnp.ones((L, L), dtype=bool))[:, :, None]
    xs = (to_chunks(q, L), to_chunks(k, L), to_chunks(v, L), to_chunks(log_f, L))

    def step(Sst, inp):
        qb, kb, vb, gb = inp
        bc = jnp.cumsum(gb, axis=2)
        inter = jnp.einsum('bhtc,bhce->bhte', qb * jnp.exp(bc), Sst)
        dec = jnp.exp(jnp.where(causal, bc[:, :, :, None, :] - bc[:, :, None, :, :], -jnp.inf))
        att = jnp.einsum('bhtc,bhsc,bhtsc->bhts', qb, kb, dec)
        o = inter + jnp.einsum('bhts,bhse->bhte', att, vb)
        S_new = jnp.exp(bc[:, :, -1])[..., None] * Sst + jnp.einsum(
            'bhsc,bhse->bhce', kb * jnp.exp(bc[:, :, -1:] - bc), vb)
        return S_new, o

    _, os = lax.scan(step, jnp.zeros((B, H, dk, dv), jnp.float32), xs)
    return from_chunks(os)

def swiglu(y, w_gate, w_up, w_down):
    return (jax.nn.silu(y @ w_gate) * (y @ w_up)) @ w_down

def token_mix(y, w_in, conv_w, conv_b, gate_b, mnorm_g, lb, hnorm_g, w_out):
    f32 = jnp.float32
    p = y @ w_in
    mq, mk, mv, mo, mif, hq, hf, hi, hg = jnp.split(p, PROJ_IDX, axis=-1)

    qk = jax.nn.silu(causal_dwconv(jnp.concatenate([mq, mk], axis=-1), conv_w, conv_b))
    mq, mk = jnp.split(qk, 2, axis=-1)
    q = split_heads(mq, MLSTM_HEADS).astype(f32)
    k = split_heads(mk, MLSTM_HEADS).astype(f32) * (MLSTM_HEAD_DIM ** -0.5)
    v = split_heads(mv, MLSTM_HEADS).astype(f32)
    gates = (mif.astype(f32) + gate_b.astype(f32)).transpose(0, 2, 1)
    log_i = gates[:, :MLSTM_HEADS]
    log_f = jax.nn.log_sigmoid(gates[:, MLSTM_HEADS:])
    hm = merge_heads(mlstm_chunkwise(q, k, v, log_i, log_f))
    out_m = head_rmsnorm(hm, mnorm_g, MLSTM_HEADS) * jax.nn.sigmoid(mo.astype(f32))

    fgate = lb.astype(f32) + (1.0 - lb.astype(f32)) * jax.nn.sigmoid(hf.astype(f32))
    hq_ = split_heads(jax.nn.silu(hq.astype(f32)), HGRN_HEADS)
    hk_ = split_heads(1.0 - fgate, HGRN_HEADS)
    hv_ = split_heads(hi.astype(f32), HGRN_HEADS)
    hlf = split_heads(jnp.log(fgate), HGRN_HEADS)
    ho = merge_heads(hgrn2_chunkwise(hq_, hk_, hv_, hlf))
    out_h = head_rmsnorm(ho, hnorm_g, HGRN_HEADS) * jax.nn.silu(hg.astype(f32))

    merged = jnp.concatenate([out_m, out_h], axis=-1).astype(y.dtype)
    return merged @ w_out

def first_inputs(seed: int = 0) -> dict:
    key = jax.random.key(seed)
    ks = jax.random.split(key, 32)
    nrm = jax.random.normal
    D, F = D_MODEL, D_FF

    def gain(k, n):
        return 1.0 + 0.05 * nrm(k, (DEPTH, n), jnp.float32)

    forget_bias = jnp.linspace(3.0, 6.0, MLSTM_HEADS, dtype=jnp.float32)[None, :] \
        + 0.1 * nrm(ks[14], (DEPTH, MLSTM_HEADS), jnp.float32)
    input_bias = 0.1 * nrm(ks[15], (DEPTH, MLSTM_HEADS), jnp.float32)
    return {
        "x": nrm(ks[0], (BATCH, SEQ, D), jnp.float32),
        "c": nrm(ks[1], (BATCH, D), jnp.float32),
        "ada_w": 0.5 * (D ** -0.5) * nrm(ks[2], (DEPTH, D, N_MOD * D), jnp.float32),
        "ada_b": 0.02 * nrm(ks[3], (DEPTH, N_MOD * D), jnp.float32),
        "ffn1_pre_g": gain(ks[4], D),
        "ffn1_post_g": gain(ks[5], D),
        "ffn1_w_gate": (D ** -0.5) * nrm(ks[6], (DEPTH, D, F), jnp.float32),
        "ffn1_w_up": (D ** -0.5) * nrm(ks[7], (DEPTH, D, F), jnp.float32),
        "ffn1_w_down": (F ** -0.5) * nrm(ks[8], (DEPTH, F, D), jnp.float32),
        "mix_pre_g": gain(ks[9], D),
        "mix_post_g": gain(ks[10], D),
        "w_in": (D ** -0.5) * nrm(ks[11], (DEPTH, D, PROJ_WIDTH), jnp.float32),
        "mlstm_conv_w": (CONV_WIDTH ** -0.5) * nrm(ks[12], (DEPTH, CONV_WIDTH, 2 * MLSTM_WIDTH), jnp.float32),
        "mlstm_conv_b": 0.02 * nrm(ks[13], (DEPTH, 2 * MLSTM_WIDTH), jnp.float32),
        "mlstm_gate_b": jnp.concatenate([input_bias, forget_bias], axis=-1),
        "mlstm_norm_g": gain(ks[16], MLSTM_WIDTH),
        "hgrn_lb_logits": nrm(ks[17], (DEPTH + 1, HGRN_WIDTH), jnp.float32),
        "hgrn_norm_g": gain(ks[18], HGRN_WIDTH),
        "w_out": (MIX_WIDTH ** -0.5) * nrm(ks[19], (DEPTH, MIX_WIDTH, D), jnp.float32),
        "ffn2_pre_g": gain(ks[20], D),
        "ffn2_post_g": gain(ks[21], D),
        "ffn2_w_gate": (D ** -0.5) * nrm(ks[22], (DEPTH, D, F), jnp.float32),
        "ffn2_w_up": (D ** -0.5) * nrm(ks[23], (DEPTH, D, F), jnp.float32),
        "ffn2_w_down": (F ** -0.5) * nrm(ks[24], (DEPTH, F, D), jnp.float32),
    }

def first_block(x, c, ada_w, ada_b, ffn1_pre_g, ffn1_post_g, ffn1_w_gate, ffn1_w_up, ffn1_w_down,
              mix_pre_g, mix_post_g, w_in, mlstm_conv_w, mlstm_conv_b, mlstm_gate_b, mlstm_norm_g,
              hgrn_lb_logits, hgrn_norm_g, w_out, ffn2_pre_g, ffn2_post_g, ffn2_w_gate, ffn2_w_up,
              ffn2_w_down):
    lb_all = jnp.cumsum(jax.nn.softmax(hgrn_lb_logits.astype(jnp.float32), axis=0), axis=0)
    sc = jax.nn.silu(c)
    h = x
    for l in range(DEPTH):
        mod = (sc @ ada_w[l] + ada_b[l])[:, None, :]
        (sh1, sc1, g1, sh2, sc2, g2, sh3, sc3, g3) = jnp.split(mod, N_MOD, axis=-1)

        y = rmsnorm(h, ffn1_pre_g[l]) * (1.0 + sc1) + sh1
        y = swiglu(y, ffn1_w_gate[l], ffn1_w_up[l], ffn1_w_down[l])
        h = h + FFN_RESIDUAL_WEIGHT * g1 * rmsnorm(y, ffn1_post_g[l])

        y = rmsnorm(h, mix_pre_g[l]) * (1.0 + sc2) + sh2
        y = token_mix(y, w_in[l], mlstm_conv_w[l], mlstm_conv_b[l], mlstm_gate_b[l], mlstm_norm_g[l],
                      lb_all[l], hgrn_norm_g[l], w_out[l])
        h = h + g2 * rmsnorm(y, mix_post_g[l])

        y = rmsnorm(h, ffn2_pre_g[l]) * (1.0 + sc3) + sh3
        y = swiglu(y, ffn2_w_gate[l], ffn2_w_up[l], ffn2_w_down[l])
        h = h + FFN_RESIDUAL_WEIGHT * g3 * rmsnorm(y, ffn2_post_g[l])
    return h


CHUNK = 64
Q_BLOCK = 128
FOX_HEADS = 8
FOX_HEAD_DIM = 64
FOX_WIDTH = FOX_HEADS * FOX_HEAD_DIM
RWKV_HEADS = 8
RWKV_HEAD_DIM = 64
RWKV_WIDTH = RWKV_HEADS * RWKV_HEAD_DIM
W_LORA = 64
A_LORA = 64
G_LORA = 128
GN_EPS = 64e-5
PEER_HEADS = 8
PEER_N_KEYS = 128
PEER_N_EXPERTS = PEER_N_KEYS * PEER_N_KEYS
PEER_HALF = 128
PEER_TOPK = 16
PEER_TOKEN_BLOCK = 128
DN_ALPHA = (2 * DEPTH) ** 0.25
DN_BETA = (8 * DEPTH) ** -0.25
LN_EPS = 1e-5
FOX_SPLITS = (FOX_WIDTH, FOX_WIDTH, FOX_WIDTH, FOX_HEADS)
RWKV_SPLITS = (RWKV_WIDTH, RWKV_WIDTH, RWKV_WIDTH, W_LORA, A_LORA, G_LORA)
FOX_COLS = 3 * FOX_WIDTH + FOX_HEADS
RWKV_COLS = 3 * RWKV_WIDTH + W_LORA + A_LORA + G_LORA
IN_WIDTH = FOX_COLS + RWKV_COLS + 2 * D_MODEL


def _split(t, sizes):
    out = []
    start = 0
    for n in sizes:
        out.append(t[..., start:start + n])
        start += n
    return out

def _layer_norm(x, g, b):
    xf = x.astype(jnp.float32)
    mu = jnp.mean(xf, axis=-1, keepdims=True)
    var = jnp.mean(jnp.square(xf - mu), axis=-1, keepdims=True)
    return ((xf - mu) * lax.rsqrt(var + LN_EPS) * g + b).astype(x.dtype)

def _token_shift(p, mu):
    prev = jnp.pad(p, ((0, 0), (1, 0), (0, 0)))[:, :-1]
    return p + mu * (prev - p)

def _forgetting_attention(q, k, v, f_logit):
    B, S = q.shape[0], q.shape[1]
    heads = lambda t: t.reshape(B, S, FOX_HEADS, FOX_HEAD_DIM).transpose(0, 2, 1, 3)
    q, k, v = heads(q), heads(k), heads(v)
    log_f = jax.nn.log_sigmoid(f_logit.astype(jnp.float32))
    c = jnp.cumsum(log_f, axis=1).transpose(0, 2, 1)
    scale = FOX_HEAD_DIM ** -0.5
    outs = []
    for blk in range(S // Q_BLOCK):
        q0 = blk * Q_BLOCK
        q1 = q0 + Q_BLOCK
        s = jnp.einsum('bhqd,bhkd->bhqk', q[:, :, q0:q1], k[:, :, :q1]).astype(jnp.float32) * scale
        s = s + c[:, :, q0:q1, None] - c[:, :, None, :q1]
        causal = jnp.arange(q0, q1)[:, None] >= jnp.arange(q1)[None, :]
        s = jnp.where(causal, s, -jnp.inf)
        p = jax.nn.softmax(s, axis=-1).astype(v.dtype)
        outs.append(jnp.einsum('bhqk,bhkd->bhqd', p, v[:, :, :q1]))
    o = jnp.concatenate(outs, axis=2)
    return o.transpose(0, 2, 1, 3).reshape(B, S, FOX_WIDTH)

def _rwkv7_time_mix(r, k, v, w_lora, a_lora, g_lora, w0, w2, a0, a2, g2, k_k, k_a, r_k, ln_g, ln_b):
    B, S = r.shape[0], r.shape[1]
    f32 = jnp.float32
    H, N = RWKV_HEADS, RWKV_HEAD_DIM
    w_pre = (w0 + jnp.tanh(w_lora) @ w2).astype(f32)
    decay = jnp.exp(-jnp.exp(-jax.nn.softplus(-w_pre) - 0.5))
    a = jax.nn.sigmoid((a0 + a_lora @ a2).astype(f32))
    g = jax.nn.sigmoid(g_lora) @ g2
    heads = lambda t: t.astype(f32).reshape(B, S, H, N)
    kk = heads(k * k_k)
    kk = kk / jnp.maximum(jnp.sqrt(jnp.sum(kk * kk, axis=-1, keepdims=True)), 1e-12)
    k_mod = k.astype(f32) * (1.0 + (a - 1.0) * k_a.astype(f32))
    r_h, k_h, v_h, w_h, a_h = heads(r), heads(k_mod), heads(v), heads(decay), heads(a)

    def to_chunks(t):
        return t.transpose(1, 0, 2, 3).reshape(S // CHUNK, CHUNK, B, H, N)

    def frame_step(state, inp):
        r_t, w_t, k_t, v_t, kk_t, a_t = inp
        sa = jnp.einsum('bhij,bhj->bhi', state, -kk_t)
        state = (state * w_t[:, :, None, :] + sa[..., None] * (kk_t * a_t)[:, :, None, :]
                 + v_t[..., None] * k_t[:, :, None, :])
        return state, jnp.einsum('bhij,bhj->bhi', state, r_t)

    def chunk_step(state, chunk_inp):
        return lax.scan(frame_step, state, chunk_inp)

    state0 = jnp.zeros((B, H, N, N), f32)
    xs = (to_chunks(r_h), to_chunks(w_h), to_chunks(k_h), to_chunks(v_h), to_chunks(kk), to_chunks(a_h))
    _, y = lax.scan(chunk_step, state0, xs)
    y = y.reshape(S, B, H, N).transpose(1, 0, 2, 3)
    mu = jnp.mean(y, axis=-1, keepdims=True)
    var = jnp.mean(jnp.square(y - mu), axis=-1, keepdims=True)
    y = ((y - mu) * lax.rsqrt(var + GN_EPS)).reshape(B, S, RWKV_WIDTH) * ln_g + ln_b
    bonus = jnp.sum(r_h * k_h * r_k.astype(f32).reshape(H, N), axis=-1, keepdims=True) * v_h
    y = (y + bonus.reshape(B, S, RWKV_WIDTH)) * g
    return y.astype(r.dtype)

def _peer(x, w_q, sub_keys, u_table, v_table):
    B, S, D = x.shape
    xt = x.reshape((B * S) // PEER_TOKEN_BLOCK, PEER_TOKEN_BLOCK, D)
    K = PEER_TOPK

    def block(xb):
        t = xb.shape[0]
        q = (xb @ w_q).reshape(t, PEER_HEADS, 2, PEER_HALF)
        s = jnp.einsum('thpd,hpkd->thpk', q, sub_keys).astype(jnp.float32)
        top_s, top_i = lax.top_k(s, K)
        cand_s = top_s[:, :, 0, :, None] + top_s[:, :, 1, None, :]
        cand_i = top_i[:, :, 0, :, None] * PEER_N_KEYS + top_i[:, :, 1, None, :]
        best_s, best_pos = lax.top_k(cand_s.reshape(t, PEER_HEADS, K * K), K)
        idx = jnp.take_along_axis(cand_i.reshape(t, PEER_HEADS, K * K), best_pos, axis=-1)
        gate = jax.nn.softmax(best_s, axis=-1).astype(xb.dtype)
        h = jax.nn.gelu(jnp.einsum('thkd,td->thk', u_table[idx], xb), approximate=False)
        return jnp.einsum('thk,thkd->td', gate * h, v_table[idx])

    return lax.map(block, xt).reshape(B, S, D)

def second_inputs(seed: int = 0) -> dict:
    key = jax.random.key(seed)
    ks = jax.random.split(key, 32)
    L = DEPTH
    nrm = lambda k, shape, scale: jax.random.normal(k, shape, jnp.float32) * scale
    return {
        "x": nrm(ks[0], (BATCH, SEQ, D_MODEL), 1.0),
        "w_in": nrm(ks[1], (L, D_MODEL, IN_WIDTH), D_MODEL ** -0.5),
        "fox_f_bias": 3.0 + nrm(ks[2], (L, FOX_HEADS), 0.5),
        "rwkv_mu": jax.random.uniform(ks[3], (L, RWKV_COLS), jnp.float32),
        "rwkv_w0": nrm(ks[4], (L, RWKV_WIDTH), 1.0),
        "rwkv_w2": nrm(ks[5], (L, W_LORA, RWKV_WIDTH), 0.1 * W_LORA ** -0.5),
        "rwkv_a0": nrm(ks[6], (L, RWKV_WIDTH), 0.5),
        "rwkv_a2": nrm(ks[7], (L, A_LORA, RWKV_WIDTH), A_LORA ** -0.5),
        "rwkv_g2": nrm(ks[8], (L, G_LORA, RWKV_WIDTH), G_LORA ** -0.5),
        "rwkv_k_k": 0.85 + nrm(ks[9], (L, RWKV_WIDTH), 0.05),
        "rwkv_k_a": 1.0 + nrm(ks[10], (L, RWKV_WIDTH), 0.05),
        "rwkv_r_k": nrm(ks[11], (L, RWKV_WIDTH), 0.1),
        "rwkv_ln_g": 1.0 + nrm(ks[12], (L, RWKV_WIDTH), 0.05),
        "rwkv_ln_b": nrm(ks[13], (L, RWKV_WIDTH), 0.01),
        "p_fox": nrm(ks[14], (L, FOX_WIDTH, D_MODEL), FOX_WIDTH ** -0.5),
        "p_rwkv": nrm(ks[15], (L, RWKV_WIDTH, D_MODEL), RWKV_WIDTH ** -0.5),
        "w_o": nrm(ks[16], (L, D_MODEL, D_MODEL), DN_BETA * D_MODEL ** -0.5),
        "ln1_g": 1.0 + nrm(ks[17], (L, D_MODEL), 0.05),
        "ln1_b": nrm(ks[18], (L, D_MODEL), 0.01),
        "peer_w_q": nrm(ks[19], (L, D_MODEL, PEER_HEADS * 2 * PEER_HALF), D_MODEL ** -0.5),
        "peer_sub_keys": nrm(ks[20], (L, PEER_HEADS, 2, PEER_N_KEYS, PEER_HALF), PEER_HALF ** -0.5),
        "peer_u": nrm(ks[21], (L, PEER_N_EXPERTS, D_MODEL), D_MODEL ** -0.5),
        "peer_v": nrm(ks[22], (L, PEER_N_EXPERTS, D_MODEL), DN_BETA * PEER_HEADS ** -0.5),
        "ln2_g": 1.0 + nrm(ks[23], (L, D_MODEL), 0.05),
        "ln2_b": nrm(ks[24], (L, D_MODEL), 0.01),
    }

def second_block(x, w_in, fox_f_bias, rwkv_mu, rwkv_w0, rwkv_w2, rwkv_a0, rwkv_a2, rwkv_g2,
              rwkv_k_k, rwkv_k_a, rwkv_r_k, rwkv_ln_g, rwkv_ln_b, p_fox, p_rwkv, w_o,
              ln1_g, ln1_b, peer_w_q, peer_sub_keys, peer_u, peer_v, ln2_g, ln2_b):
    for l in range(DEPTH):
        p = x @ w_in[l]
        fox_cols = p[..., :FOX_COLS]
        rwkv_cols = _token_shift(p[..., FOX_COLS:FOX_COLS + RWKV_COLS], rwkv_mu[l])
        gate_cols = p[..., FOX_COLS + RWKV_COLS:]
        q, k, v, f_logit = _split(fox_cols, FOX_SPLITS)
        r_r, r_k, r_v, r_wl, r_al, r_gl = _split(rwkv_cols, RWKV_SPLITS)
        gate_fox, gate_rwkv = _split(gate_cols, (D_MODEL, D_MODEL))

        y_fox = _forgetting_attention(q, k, v, f_logit + fox_f_bias[l])
        y_rwkv = _rwkv7_time_mix(r_r, r_k, r_v, r_wl, r_al, r_gl,
                                 rwkv_w0[l], rwkv_w2[l], rwkv_a0[l], rwkv_a2[l], rwkv_g2[l],
                                 rwkv_k_k[l], rwkv_k_a[l], rwkv_r_k[l], rwkv_ln_g[l], rwkv_ln_b[l])
        merged = (jax.nn.sigmoid(gate_fox) * (y_fox @ p_fox[l])
                  + jax.nn.sigmoid(gate_rwkv) * (y_rwkv @ p_rwkv[l]))
        x = _layer_norm(DN_ALPHA * x + merged @ w_o[l], ln1_g[l], ln1_b[l])
        x = _layer_norm(DN_ALPHA * x + _peer(x, peer_w_q[l], peer_sub_keys[l], peer_u[l], peer_v[l]),
                        ln2_g[l], ln2_b[l])
    return x


def setup_inputs(seed=0):
    out = dict(first_inputs(seed))
    for name, value in second_inputs(seed + 1).items():
        if name != "x":
            out[name + "_2"] = value
    return out


def reference(
    x, c, ada_w, ada_b, ffn1_pre_g, ffn1_post_g, ffn1_w_gate, ffn1_w_up, ffn1_w_down, mix_pre_g,
    mix_post_g, w_in, mlstm_conv_w, mlstm_conv_b, mlstm_gate_b, mlstm_norm_g, hgrn_lb_logits,
    hgrn_norm_g, w_out, ffn2_pre_g, ffn2_post_g, ffn2_w_gate, ffn2_w_up, ffn2_w_down, w_in_2,
    fox_f_bias_2, rwkv_mu_2, rwkv_w0_2, rwkv_w2_2, rwkv_a0_2, rwkv_a2_2, rwkv_g2_2, rwkv_k_k_2,
    rwkv_k_a_2, rwkv_r_k_2, rwkv_ln_g_2, rwkv_ln_b_2, p_fox_2, p_rwkv_2, w_o_2, ln1_g_2,
    ln1_b_2, peer_w_q_2, peer_sub_keys_2, peer_u_2, peer_v_2, ln2_g_2, ln2_b_2,
):
    x = first_block(
        x, c, ada_w, ada_b, ffn1_pre_g, ffn1_post_g, ffn1_w_gate, ffn1_w_up, ffn1_w_down,
        mix_pre_g, mix_post_g, w_in, mlstm_conv_w, mlstm_conv_b, mlstm_gate_b, mlstm_norm_g,
        hgrn_lb_logits, hgrn_norm_g, w_out, ffn2_pre_g, ffn2_post_g, ffn2_w_gate, ffn2_w_up,
        ffn2_w_down,
    )
    return second_block(
        x, w_in_2, fox_f_bias_2, rwkv_mu_2, rwkv_w0_2, rwkv_w2_2, rwkv_a0_2, rwkv_a2_2,
        rwkv_g2_2, rwkv_k_k_2, rwkv_k_a_2, rwkv_r_k_2, rwkv_ln_g_2, rwkv_ln_b_2, p_fox_2,
        p_rwkv_2, w_o_2, ln1_g_2, ln1_b_2, peer_w_q_2, peer_sub_keys_2, peer_u_2, peer_v_2,
        ln2_g_2, ln2_b_2,
    )


_drawn_inputs = setup_inputs


def setup_inputs(seed=0):
    import zlib

    import numpy as np

    out = dict(_drawn_inputs(seed))
    spreads = {}
    factors = {'ffn1_pre_g': 3.673,
     'ffn1_post_g': 4.79,
     'mix_post_g': 2.893,
     'mlstm_conv_b': 8.0,
     'mlstm_norm_g': 3.788,
     'hgrn_norm_g': 3.726,
     'ffn2_pre_g': 4.123,
     'ffn2_post_g': 5.045,
     'fox_f_bias_2': 35.128,
     'rwkv_w2_2': 8.0,
     'rwkv_k_k_2': 44.794,
     'rwkv_k_a_2': 4.348,
     'rwkv_ln_g_2': 5.377,
     'rwkv_ln_b_2': 45.225,
     'ln1_b_2': 3.945,
     'ln2_b_2': 5.685}
    for name, (base, spread) in spreads.items():
        noise = np.random.default_rng([zlib.crc32(name.encode()), seed]).standard_normal(out[name].shape)
        drawn = base * np.exp(spread * noise) if base else spread * noise
        out[name] = __import__('jax').numpy.asarray(drawn.astype(out[name].dtype))
    for name, factor in factors.items():
        out[name] = (out[name] * factor).astype(out[name].dtype)
    return out
```

```python
from contextlib import ExitStack

import concourse.bass as bass
import numpy as np
from concourse import mybir

ALU = mybir.AluOpType
ACT = mybir.ActivationFunctionType
F32 = mybir.dt.float32
U32 = mybir.dt.uint32
AX_X = mybir.AxisListType.X

P = 128
S, D, F = 256, 1024, 2816
TT, KT, FT = S // P, D // P, F // P
N_MOD = 9
HEADS, W1 = 4, 512
FOX_H, RW_H, DH = 8, 8, 64
PAIRS = RW_H // 2
CH = 16
NCH = S // CH
PH, NKEY, TOPK = 8, 128, 16
EPS, LN_EPS, GN_EPS = 1e-6, 1e-5, 64e-5
ALPHA = 2.0 ** 0.25
SLOTS, CHUNK = 4, 2048
LEVELS = [64, 32, 16, 8, 4, 2, 1]
NEG = -3.0e38



def w_form(w):
    k, n = w.shape
    v = w.reshape(k // P, P, n // 256, 256).transpose(2, 1, 0, 3)
    return np.ascontiguousarray(v).reshape(-1, P, CHUNK)


def a_form(w):
    k, n = w.shape
    v = w.reshape(k // 512, 4, P, n // 512, 512).transpose(3, 0, 2, 1, 4)
    return np.ascontiguousarray(v).reshape(-1, P, CHUNK)


def gate_up(wg, wu):
    v = np.stack([wg.reshape(KT, P, FT, P), wu.reshape(KT, P, FT, P)], axis=3)
    return np.ascontiguousarray(v.transpose(2, 1, 0, 3, 4)).reshape(-1, P, CHUNK)


def down(w):
    v = w.reshape(FT // 2, 2, P, D).transpose(0, 2, 1, 3)
    return np.ascontiguousarray(v).reshape(-1, P, CHUNK)


def narrow(w):
    return np.ascontiguousarray(w.reshape(KT, P, -1).transpose(1, 0, 2)).reshape(P, -1)


def columns(v):
    v = np.atleast_2d(v)
    return np.ascontiguousarray(v.reshape(v.shape[0], -1, P).transpose(2, 0, 1)).reshape(P, -1)


def spread(v):
    return np.ascontiguousarray(np.broadcast_to(v.reshape(1, -1), (P, v.size)))


def constants():
    u, t = np.arange(P)[:, None], np.arange(P)[None, :]
    out = {"ident": u == t, "ones": np.ones((P, P)), "tri": u <= t, "after": u > t}
    out["par_ones"] = u // DH == t // DH
    decay, keep = [], []
    for m in LEVELS:
        half = (t // m) % 2 == 1
        start = t // (2 * m) * (2 * m)
        decay.append(np.where(half, (u >= start + m) & (u <= t), (u > t) & (u < start + m)))
        keep.append((u // (2 * m) == t // (2 * m)) & ((u // m) % 2 == 0) & half)
    out["decay"] = np.concatenate(decay, 1)
    out["keep"] = np.concatenate(keep + [u == t], 1)
    out["causal"] = np.where(t <= u, 0.0, NEG)
    out["id64"] = u % DH == np.arange(DH)[None, :]
    q, r = np.arange(P)[:, None] % DH, np.arange(DH)[None, :]
    same = q // CH == r // CH
    out["s_t"] = np.concatenate([same & (q < r), same & (q <= r)], 1)
    out["t_s"] = same & (r < q)
    out["pairs"] = q // CH == np.arange(PAIRS)[None, :]
    out["starts"] = np.broadcast_to(np.arange(S)[None, :] % CH != 0, (P, S))
    out["digits"] = np.broadcast_to(np.arange(TOPK)[None, :], (P, TOPK))
    return {k: np.ascontiguousarray(v, dtype=np.float32) for k, v in out.items()}


def pack(parts):
    at, where = 0, {}
    for name, a in parts.items():
        where[name] = (at, at + a.shape[1])
        at += a.shape[1]
    return np.ascontiguousarray(np.concatenate(list(parts.values()), axis=1)), where



class Count:

    def __init__(self):
        self.n, self.term = 0, None

    def at(self, n):
        return n if self.term is None else self.term + n


class Banks:

    def __init__(self, banks, done, free):
        self.banks, self.done, self.free = banks, done, free
        self.filled, self.emptied = Count(), Count()

    def take(self, pe):
        c = self.filled
        pe.wait_ge(self.free, c.at(c.n + 1))
        c.n += 1
        return self.banks[(c.n - 1) % 4]

    def evacuated(self, pe):
        c = self.filled
        pe.wait_ge(self.free, c.at(c.n + 4))

    def evacuated_but(self, pe, n):
        c = self.filled
        pe.wait_ge(self.free, c.at(c.n + 4 - n))

    def get(self, eng):
        c = self.emptied
        eng.wait_ge(self.done, c.at(c.n + 1))
        c.n += 1
        return self.banks[(c.n - 1) % 4]

    def through(self, eng):
        c = self.emptied
        eng.wait_ge(self.free, c.at(c.n + 4))


def loop(eng, total, unroll, body, counts):
    passes = total // unroll
    if passes > 1:
        starts = [c.n for c, _ in counts]
        with eng.Fori(0, passes) as i:
            for c, per in counts:
                c.term = i * per
            for j in range(unroll):
                body(i * unroll + j, j)
        for (c, per), start in zip(counts, starts):
            assert c.n - start == per
            c.n, c.term = start + per * passes, None
    else:
        passes = 0
    for g in range(passes * unroll, total):
        body(g, g)



def program(nc, dram, out, where):
    ctx = ExitStack()
    with ctx:
        sems = {}

        def sem(name):
            if name not in sems:
                sems[name] = ctx.enter_context(nc.semaphore(name))
            return sems[name]

        def sb(name, shape, dt=F32):
            return ctx.enter_context(nc.sbuf_tensor(name, shape, dt))

        ring = sb("ring", [P, SLOTS, CHUNK])
        n_const = max(b for _, b in where["const"].values())
        const = sb("const", [P, n_const])

        def cst(name):
            a, b = where["const"][name]
            return const[:, a:b]

        n_cols = max(b for _, b in where["cols"].values())
        cols = sb("cols", [P, n_cols])

        def col(name):
            a, b = where["cols"][name]
            return cols[:, a:b]

        xh = sb("xh", [P, TT, D])
        yb = sb("yb", [P, TT, D])
        yT = sb("yT", [P, KT, S])
        small = sb("small", [P, 512])
        arena1 = sb("arena1", [P, N_MOD * D])
        arena2 = sb("arena2", [P, 6 * D])
        arena3 = sb("arena3", [P, FT * S])
        arena4 = sb("arena4", [P, 6 * D])

        banks = [ctx.enter_context(nc.psum_tensor(f"bank{i}", [P, 512], F32)) for i in range(8)]
        A = Banks(banks[:4], sem("act_bank_filled"), sem("act_bank_free"))
        V = Banks(banks[4:], sem("dve_bank_filled"), sem("dve_bank_free"))

        mod = arena1[:, :].rearrange("p (m d) -> p m d", m=N_MOD)
        gains = arena2[:, :].rearrange("p (m d) -> p m d", m=6)
        hT = arena3[:, :].rearrange("p (f s) -> p f s", s=S)
        sgate = arena4[:, 0:4 * S].rearrange("p (j s) -> p j s", j=4)
        junk = arena2[:, 0:2 * D].rearrange("p (t d) -> p t d", t=TT)
        SH1, SC1, G1, SH2, SC2, G2, SH3, SC3, G3 = range(N_MOD)

        ident = cst("ident")

        landed = [sem(f"chunk_landed{j}") for j in range(SLOTS)]
        begun = sem("chunk_begun")
        chunks = Count()
        v_steps, a_steps, g_steps = Count(), Count(), Count()
        root_asked, root_done = sem("root_asked"), sem("root_done")
        roots = {"dve": 0, "act": 0}

        def v(ins):
            v_steps.n += 1
            ins.then_inc(sem("dve_step"), 1)
            nc.vector.wait_ge(sem("dve_step"), v_steps.at(v_steps.n))

        def a(ins):
            a_steps.n += 1
            ins.then_inc(sem("act_step"), 1)
            nc.scalar.wait_ge(sem("act_step"), a_steps.at(a_steps.n))

        def next_chunk(pe):
            g = chunks.n
            n = 16 * (g // SLOTS + 1)
            pe.wait_ge(landed[g % SLOTS], n if chunks.term is None else chunks.term * (16 // SLOTS) + n)
            chunks.n += 1
            return ring[:, g % SLOTS, :]


        def root_act(n):
            roots["act"] += 1
            nc.scalar.wait_ge(root_asked, roots["act"])
            nc.scalar.activation(small[:, 64:64 + n], small[:, 0:n], ACT.Sqrt).then_inc(root_done, 1)

        def rstd_dve(dst, ss, n, scale, eps):
            roots["dve"] += 1
            nc.vector.tensor_scalar(small[:, 0:n], ss, scale, eps, ALU.mult, ALU.add).then_inc(root_asked, 1)
            nc.vector.wait_ge(root_done, roots["dve"])
            v(nc.vector.reciprocal(dst, small[:, 64:64 + n]))

        def square_sums(src, n):
            for i in range(n):
                ins = nc.vector.tensor_tensor_reduce(junk[:, i, 0:src.shape[2]], src[:, i, :], src[:, i, :], 1.0, 0.0,
                                                     ALU.mult, ALU.add, small[:, 128 + i:129 + i])
            v(ins)

        def modulated_norm_dve(sc, sh, tag):
            square_sums(xh, TT)
            rstd_dve(small[:, 130:132], small[:, 128:130], TT, 1.0 / D, EPS)
            for t in range(TT):
                v(nc.vector.scalar_tensor_tensor(yb[:, t, :], xh[:, t, :], small[:, 130 + t:131 + t],
                                                 mod[:, sc, :], ALU.mult, ALU.mult))
                nc.vector.tensor_tensor(yb[:, t, :], yb[:, t, :], mod[:, sh, :],
                                        ALU.add).then_inc(sem(f"y_{tag}"), 1)

        def turn_pe(pe, src, tag, by_tile=True):
            for t in range(TT):
                pe.wait_ge(sem(f"y_{tag}"), t + 1)
                for k in range(0, KT, 4):
                    bank = A.take(pe)
                    for j in range(4):
                        ins = pe.transpose(bank[:, j * P:(j + 1) * P], src[:, t, (k + j) * P:(k + j + 1) * P],
                                           ident)
                    ins.then_inc(A.done, 1)

        def turn_act(act):
            for t in range(TT):
                for k in range(0, KT, 4):
                    bank = A.get(act)
                    nc.scalar.copy(yT[:, k:k + 4, t * P:(t + 1) * P],
                                   bank[:, :].rearrange("p (j s) -> p j s", j=4)).then_inc(A.free, 1)

        def moving_pe(pe, queue, k_tiles=KT, src=None):
            src = yT if src is None else src
            two = [queue.take(pe), queue.take(pe)]
            for c in range(0, k_tiles, 4):
                w = next_chunk(pe)[:, :].rearrange("p (k n) -> p k n", k=4)
                for t in range(TT):
                    for k in range(4):
                        ins = pe.matmul(two[t][:, :], src[:, c + k, t * P:(t + 1) * P], w[:, k, :],
                                        start=(c + k == 0), stop=(c + k == k_tiles - 1))
                        if t == 0 and k == 0:
                            ins.then_inc(begun, 1)
                    if c + k == k_tiles - 1:
                        ins.then_inc(queue.done, 1)

        def staying_pe(pe, queue, src=None):
            src = yT if src is None else src
            bank = queue.take(pe)
            w = next_chunk(pe)[:, :].rearrange("p (k n) -> p k n", k=KT)
            for j in range(2):
                for k in range(KT):
                    ins = pe.matmul(bank[:, j * S:(j + 1) * S], w[:, k, j * P:(j + 1) * P], src[:, k, :],
                                    start=(k == 0), stop=(k == KT - 1))
                    if j == 0 and k == 0:
                        ins.then_inc(begun, 1)
            ins.then_inc(queue.done, 1)

        def add_residual_dve(g):
            square_sums(yb, TT)
            rstd_dve(small[:, 130:132], small[:, 128:130], TT, 1.0 / D, EPS)
            for t in range(TT):
                v(nc.vector.scalar_tensor_tensor(yb[:, t, :], yb[:, t, :], small[:, 130 + t:131 + t],
                                                 mod[:, g, :], ALU.mult, ALU.mult))
                v(nc.vector.tensor_tensor(xh[:, t, :], xh[:, t, :], yb[:, t, :], ALU.add))


        def ada_pe(pe):
            pe.wait_ge(sem("silu_c_spread"), 1)

            def body(g, j):
                if j % 2 == 0:
                    ada_pe.bank = V.take(pe)
                w = next_chunk(pe)[:, :].rearrange("p (k n) -> p k n", k=4)
                for k in range(4):
                    kt = (j % 2) * 4 + k
                    ins = pe.matmul(ada_pe.bank[:, :], yT[:, kt, 0:P], w[:, k, :], start=(kt == 0), stop=(kt == KT - 1))
                    if k == 0:
                        ins.then_inc(begun, 1)
                if j % 2:
                    ins.then_inc(V.done, 1)

            loop(pe, 36, 8, body, [(chunks, 8), (V.filled, 4)])

        def ada_act(act):
            act.wait_ge(sem("cols_in"), 16)
            nc.scalar.activation(col("c"), col("c"), ACT.Silu).then_inc(sem("silu_c"), 1)

        def ada_dve(dve):
            dve.wait_ge(sem("const_in"), 16)
            dve.wait_ge(sem("silu_c"), 1)
            for k in range(KT):
                ins = nc.vector.tensor_scalar(yT[:, k, 0:P], cst("ones"), col("c")[:, k:k + 1], None, ALU.mult)
            ins.then_inc(sem("silu_c_spread"), 1)
            dve.wait_ge(sem("ada_b_in"), 16)

            def body(g, j):
                bank = V.get(dve)
                at = arena1[:, bass.ds(g * 512, 512)]
                nc.vector.tensor_tensor(at, at, bank[:, :], ALU.add).then_inc(V.free, 1)

            loop(dve, 18, 4, body, [(V.emptied, 4)])
            V.through(dve)
            dve.wait_ge(sem("gains_in"), 16)
            for i, sc in enumerate((SC1, SC2, SC3)):
                ins = nc.vector.scalar_tensor_tensor(mod[:, sc, :], mod[:, sc, :], 1.0, gains[:, 2 * i, :], ALU.add, ALU.mult)
            for i, (g, w) in enumerate(((G1, 0.5), (G2, 1.0), (G3, 0.5))):
                ins = nc.vector.scalar_tensor_tensor(mod[:, g, :], mod[:, g, :], w, gains[:, 2 * i + 1, :], ALU.mult, ALU.mult)
            v(ins)


        def ffn_pe(pe, tag):
            V_seen[tag] = V.filled.n
            turn_pe(pe, yb, tag)
            A.evacuated(pe)

            def body(g, j):
                staying_pe(pe, V)

            loop(pe, FT, 4, body, [(chunks, 4), (V.filled, 4)])
            V.evacuated(pe)
            four = [V.take(pe) for _ in range(4)]
            for g in range(FT // 2):
                w = next_chunk(pe)[:, :].rearrange("p (k n) -> p k n", k=2)
                for k in range(2):
                    f = 2 * g + k
                    for t in range(TT):
                        for n in range(2):
                            ins = pe.matmul(four[2 * t + n][:, :], hT[:, f, t * P:(t + 1) * P], w[:, k, n * 512:(n + 1) * 512],
                                            start=(f == 0), stop=(f == FT - 1))
                            if k == t == n == 0:
                                ins.then_inc(begun, 1)
                            if f == FT - 1:
                                ins.then_inc(V.done, 1)

        def ffn_act(act, tag):
            root_act(TT)
            turn_act(act)
            filled = Count()
            filled.n = V_seen[tag]

            def body(g, j):
                filled.n += 1
                act.wait_ge(V.done, filled.at(filled.n))
                nc.scalar.activation(sgate[:, (filled.n - 1) % 4, :], V.banks[(filled.n - 1) % 4][:, 0:S],
                                     ACT.Silu).then_inc(sem("gate_ready"), 1)

            loop(act, FT, 4, body, [(filled, 4)])
            root_act(TT)

        V_seen = {}
        gates = Count()

        def ffn_dve(dve, tag, sc, sh, g):
            modulated_norm_dve(sc, sh, tag)

            def body(i, j):
                bank = V.get(dve)
                gates.n += 1
                dve.wait_ge(sem("gate_ready"), gates.at(gates.n))
                nc.vector.tensor_tensor(hT[:, i, :], sgate[:, (V.emptied.n - 1) % 4, :], bank[:, S:2 * S],
                                        ALU.mult).then_inc(V.free, 1)

            loop(dve, FT, 4, body, [(V.emptied, 4), (gates, 4)])
            for i in range(4):
                bank = V.get(dve)
                nc.vector.tensor_copy(yb[:, i // 2, (i % 2) * 512:(i % 2 + 1) * 512], bank[:, :]).then_inc(V.free, 1)
            V.through(dve)
            add_residual_dve(g)

        marks = {}

        def mark(name, semaphore, value):
            marks[name] = (semaphore, value)

        def await_mark(dve, name):
            dve.wait_ge(*marks[name])

        tiny = sb("tiny", [P, 512])
        arena5 = sb("arena5", [P, 7168])
        PAD = 3
        conv_in = arena2[:, 0:8 * (S + PAD)].rearrange("p (c s) -> p c s", c=8)
        qk_ch = arena2[:, 2072:2072 + 8 * S].rearrange("p (c s) -> p c s", c=8)
        hq_ch = arena2[:, 4120:5144].rearrange("p (h s) -> p h s", h=HEADS)
        sT = arena2[:, 5144:5912].rearrange("p (b s) -> p b s", b=2)
        v_m = arena3[:, 0:1024].rearrange("p (t w) -> p t w", t=TT)
        v_h = arena3[:, 1024:2048].rearrange("p (t w) -> p t w", t=TT)
        f_tok = arena3[:, 2048:3072].rearrange("p (t w) -> p t w", t=TT)
        hk_tok = arena3[:, 3072:4096].rearrange("p (t w) -> p t w", t=TT)
        lb = arena3[:, 4096:4608]
        one_lb = arena3[:, 4608:5120]
        norms = arena4[:, 1024:3072]
        mixg = arena4[:, 3072:5120].rearrange("p (t w) -> p t w", t=TT)
        hk_ch = arena4[:, 5120:6144].rearrange("p (h s) -> p h s", h=HEADS)
        NL = len(LEVELS)
        decayed = [arena5[:, i * 2304:(i + 1) * 2304].rearrange("p (k l s) -> p k l s", k=2, s=P) for i in range(2)]
        masked = arena5[:, 4608:5632].rearrange("p (l s) -> p l s", s=P)
        dm = arena5[:, 5632:7168].rearrange("p (h s) -> p h s", h=HEADS)
        att = arena3[:, 5120:5632].rearrange("p (k b s) -> p k b s", k=2, b=2)
        gate8 = tiny[:, 0:16].rearrange("p (t g) -> p t g", t=TT)
        t_ax, t_e, t_l, t_lf, t_b, t_x, t_nm, t_m, t_den, t_em, t_rec = [
            tiny[:, 16 + 8 * i:24 + 8 * i].rearrange("p (t h) -> p t h", t=TT) for i in range(11)]

        M_SEQ = [("S", 0), ("S", 1), ("T", 0), ("S", 2), ("N", 0), ("T", 1), ("S", 3), ("N", 1), ("T", 2), ("N", 2),
                 ("T", 3), ("N", 3)]

        def narrow_pe(pe, w, n):
            bank = V.take(pe)
            for t in range(TT):
                for k in range(KT):
                    ins = pe.matmul(bank[:, t * n:(t + 1) * n], yT[:, k, t * P:(t + 1) * P], w[:, k * n:(k + 1) * n],
                                    start=(k == 0), stop=(k == KT - 1))
            ins.then_inc(V.done, 1)

        def cumulate_pe(pe, ready, lf, n):
            pe.wait_ge(sem(ready), 1)
            bank = V.take(pe)
            pe.matmul(bank[:, 0:n], cst("tri"), lf[:, 0, :], start=True, stop=True)
            pe.matmul(bank[:, n:2 * n], cst("ones"), lf[:, 0, :], start=True, stop=False)
            pe.matmul(bank[:, n:2 * n], cst("tri"), lf[:, 1, :], start=False, stop=True).then_inc(V.done, 1)

        def rows_pe(pe, ready, x, heads):
            pe.wait_ge(sem(ready), 1)
            for h in range(0, heads, 2):
                bank = V.take(pe)
                for j in range(2):
                    for t in range(TT):
                        ins = pe.matmul(bank[:, j * S + t * P:j * S + (t + 1) * P],
                                        x[:, t, h + j:h + j + 1].broadcast_to([P, P]), ident, start=True, stop=True)
                ins.then_inc(V.done, 1)

        def mix_pe(pe):
            turn_pe(pe, yb, "mix")
            A.evacuated(pe)
            narrow_pe(pe, col("w_mif"), 8)
            for _ in range(4):
                staying_pe(pe, A)
            for _ in range(2):
                staying_pe(pe, A)
            moving_pe(pe, A)
            cumulate_pe(pe, "m_logf", t_lf, HEADS)
            moving_pe(pe, V)
            rows_pe(pe, "m_x", t_x, HEADS)
            moving_pe(pe, A)
            moving_pe(pe, V)
            pe.wait_ge(sem("hk_ready"), 1)
            for t in range(TT):
                bank = A.take(pe)
                for h in range(HEADS):
                    ins = pe.transpose(bank[:, h * P:(h + 1) * P], hk_tok[:, t, h * P:(h + 1) * P], ident)
                ins.then_inc(A.done, 1)
            moving_pe(pe, A)
            pe.wait_ge(sem("qk_ready"), 1)
            for what, h in M_SEQ:
                if what == "S":
                    bank = V.take(pe)
                    q, k = qk_ch[:, h, :], qk_ch[:, 4 + h, :]
                    pe.matmul(bank[:, 0:P], q[:, 0:P], k[:, 0:P], start=True, stop=True)
                    pe.matmul(bank[:, P:3 * P], q[:, P:S], k, start=True, stop=True).then_inc(V.done, 1)
                if what == "T":
                    pe.wait_ge(sem("m_scores"), h + 1)
                    bank = A.take(pe)
                    for j in range(3):
                        ins = pe.transpose(bank[:, j * P:(j + 1) * P], dm[:, h, j * P:(j + 1) * P], ident)
                    ins.then_inc(A.done, 1)
                if what == "N":
                    A.evacuated(pe)
                    bank = V.take(pe)
                    val = v_m[:, :, h * P:(h + 1) * P]
                    w = sT[:, h % 2, :]
                    pe.matmul(bank[:, 0:P], w[:, 0:P], val[:, 0, :], start=True, stop=True)
                    pe.matmul(bank[:, P:2 * P], w[:, P:2 * P], val[:, 0, :], start=True, stop=False)
                    pe.matmul(bank[:, P:2 * P], w[:, 2 * P:3 * P], val[:, 1, :], start=False, stop=True).then_inc(V.done, 1)

            def decays(i):
                h, t = divmod(i, TT)
                lf = f_tok[:, :, h * P:(h + 1) * P]
                for a0, b0 in ((0, 512), (512, NL * P)):
                    bank = A.take(pe)
                    pe.matmul(bank[:, 0:b0 - a0], lf[:, t, :], cst("decay")[:, a0:b0], start=True,
                              stop=True).then_inc(A.done, 1)
                if t:
                    bank = A.take(pe)
                    pe.matmul(bank[:, 0:P], lf[:, 1, :], cst("tri"), start=True, stop=True)
                    pe.matmul(bank[:, P:2 * P], lf[:, 0, :], cst("after"), start=True, stop=True).then_inc(A.done, 1)

            def attend(i):
                h, t = divmod(i, TT)
                pe.wait_ge(sem("h_decayed"), i + 1)
                q, k = decayed[i % 2][:, 1], decayed[i % 2][:, 0]
                for l0 in (0, 4):
                    bank = V.take(pe)
                    for l in range(l0, l0 + 4):
                        lhs, rhs = (k[:, l, :], q[:, l, :]) if l < NL else (
                            hk_ch[:, h, t * P:(t + 1) * P], hq_ch[:, h, t * P:(t + 1) * P])
                        ins = pe.matmul(bank[:, (l - l0) * P:(l - l0 + 1) * P], lhs, rhs, start=True, stop=True)
                    ins.then_inc(V.done, 1)
                if t:
                    bank = V.take(pe)
                    pe.matmul(bank[:, 0:P], k[:, NL + 1, :], q[:, NL, :], start=True, stop=True).then_inc(V.done, 1)

            def read_out(i):
                h, t = divmod(i, TT)
                pe.wait_ge(sem("h_att"), i + 1)
                bank = V.take(pe)
                val = v_h[:, :, h * P:(h + 1) * P]
                ins = pe.matmul(bank[:, 0:P], att[:, 0, i % 2, :], val[:, t, :], start=True, stop=not t)
                if t:
                    ins = pe.matmul(bank[:, 0:P], att[:, 1, i % 2, :], val[:, 0, :], start=False, stop=True)
                ins.then_inc(V.done, 1)

            pe.wait_ge(sem("h_logf"), 1)
            decays(0)
            for i in range(HEADS * TT):
                if i < HEADS * TT - 1:
                    decays(i + 1)
                attend(i)
                if i:
                    read_out(i - 1)
            read_out(HEADS * TT - 1)
            turn_pe(pe, yb, "mixed")
            A.evacuated(pe)
            moving_pe(pe, V)
            moving_pe(pe, V)

        def mix_act(act):
            root_act(TT)
            turn_act(act)
            act.wait_ge(sem("m_gates"), 1)
            a(nc.scalar.activation(t_e, t_ax, ACT.Exp, scale=-1.0))
            nc.scalar.activation(t_l, t_e, ACT.Ln, bias=1.0).then_inc(sem("m_log"), 1)
            act.wait_ge(sem("conv_pad"), 1)
            for c in range(4):
                bank = A.get(act)
                nc.scalar.copy(conv_in[:, 2 * c:2 * c + 2, PAD:], bank[:, :].rearrange("p (j s) -> p j s", j=2)
                               ).then_inc(A.free, 1)
                mark(f"conv_in{c}", A.free, 4 + A.emptied.n)
            for c in range(2):
                bank = A.get(act)
                nc.scalar.activation(hq_ch[:, 2 * c:2 * c + 2, :], bank[:, :].rearrange("p (j s) -> p j s", j=2),
                                     ACT.Silu).then_inc(A.free, 1)
            for t in range(TT):
                bank = A.get(act)
                nc.scalar.activation(f_tok[:, t, :], bank[:, :], ACT.Sigmoid).then_inc(A.free, 1)
            mark("forget", A.free, 4 + A.emptied.n)
            act.wait_ge(sem("lb_diff"), 1)
            nc.scalar.activation(lb, lb, ACT.Sigmoid).then_inc(sem("lb_ready"), 1)
            for t in range(TT):
                bank = A.get(act)
                nc.scalar.activation(mixg[:, t, 0:W1], bank[:, :], ACT.Sigmoid).then_inc(A.free, 1)
            for c in range(8):
                act.wait_ge(sem("conv_done"), c + 1)
                ins = nc.scalar.activation(qk_ch[:, c, :], qk_ch[:, c, :], ACT.Silu, bias=col("conv_b")[:, c:c + 1])
            ins.then_inc(sem("qk_ready"), 1)
            act.wait_ge(sem("hk_ready"), 1)
            nc.scalar.activation(f_tok[:, :, :], f_tok[:, :, :], ACT.Ln).then_inc(sem("h_logf"), 1)
            for t in range(TT):
                bank = A.get(act)
                nc.scalar.copy(hk_ch[:, :, t * P:(t + 1) * P], bank[:, :].rearrange("p (h s) -> p h s", h=HEADS)
                               ).then_inc(A.free, 1)
            for t in range(TT):
                bank = A.get(act)
                nc.scalar.activation(mixg[:, t, W1:], bank[:, :], ACT.Silu).then_inc(A.free, 1)
            act.wait_ge(sem("m_max"), 1)
            for h in range(HEADS):
                nc.scalar.activation(dm[:, h, 0:P], dm[:, h, 0:P], ACT.Exp, bias=t_nm[:, 0, h:h + 1])
                nc.scalar.activation(dm[:, h, P:3 * P], dm[:, h, P:3 * P], ACT.Exp, bias=t_nm[:, 1, h:h + 1]
                                     ).then_inc(sem("m_weights"), 1)
            nc.scalar.activation(t_em, t_nm, ACT.Exp).then_inc(sem("m_weights"), 1)
            for h in range(HEADS):
                bank = A.get(act)
                nc.scalar.copy(sT[:, h % 2, :], bank[:, 0:3 * P]).then_inc(A.free, 1)
            for i in range(HEADS * TT):
                e = decayed[i % 2][:, 0].rearrange("p l s -> p (l s)")
                for a0, b0 in ((0, 512), (512, NL * P)) + (((NL * P, NL * P + 2 * P),) if i % TT else ()):
                    bank = A.get(act)
                    nc.scalar.activation(e[:, a0:b0], bank[:, 0:b0 - a0], ACT.Exp).then_inc(A.free, 1)
                mark(f"decay{i}", A.free, 4 + A.emptied.n)
            root_act(2 * TT * HEADS)
            turn_act(act)
            root_act(TT)

        def mix_dve(dve):
            vec = nc.vector
            modulated_norm_dve(SC2, SH2, "mix")
            vec.memset(conv_in[:, :, 0:PAD], 0.0).then_inc(sem("conv_pad"), 1)
            dve.wait_ge(sem("norms_in"), 16)
            vec.tensor_tensor(lb, norms[:, D:D + W1], norms[:, D + W1:D + 2 * W1], ALU.subtract
                              ).then_inc(sem("lb_diff"), 1)
            bank = V.get(dve)
            vec.tensor_tensor(gate8, bank[:, 0:16].rearrange("p (t g) -> p t g", t=TT),
                              col("gate_b").unsqueeze(1).broadcast_to([P, TT, 8]), ALU.add).then_inc(V.free, 1)
            V.through(dve)
            vec.scalar_tensor_tensor(t_ax, gate8[:, :, HEADS:], -1.0, gate8[:, :, HEADS:], ALU.mult, ALU.max).then_inc(sem("m_gates"), 1)
            dve.wait_ge(sem("m_log"), 1)
            vec.scalar_tensor_tensor(t_lf, gate8[:, :, HEADS:], 0.0, t_l, ALU.min, ALU.subtract
                                     ).then_inc(sem("m_logf"), 1)
            for c in range(8):
                if c % 2 == 0:
                    await_mark(dve, f"conv_in{c // 2}")
                w = lambda j: col("conv_w")[:, j * 8 + c:j * 8 + c + 1]
                v(vec.tensor_scalar(qk_ch[:, c, :], conv_in[:, c, 0:S], w(0), None, ALU.mult))
                for j in (1, 2):
                    v(vec.scalar_tensor_tensor(qk_ch[:, c, :], conv_in[:, c, j:j + S], w(j), qk_ch[:, c, :],
                                               ALU.mult, ALU.add))
                vec.scalar_tensor_tensor(qk_ch[:, c, :], conv_in[:, c, 3:3 + S], w(3), qk_ch[:, c, :],
                                         ALU.mult, ALU.add).then_inc(sem("conv_done"), 1)
            bank = V.get(dve)
            vec.tensor_copy(t_b, bank[:, 0:8].rearrange("p (t h) -> p t h", t=TT)).then_inc(V.free, 1)
            V.through(dve)
            vec.tensor_tensor(t_x, gate8[:, :, 0:HEADS], t_b, ALU.subtract).then_inc(sem("m_x"), 1)
            dve.wait_ge(sem("lb_ready"), 1)
            v(vec.tensor_scalar(one_lb, lb, -1.0, 1.0, ALU.mult, ALU.add))
            await_mark(dve, "forget")
            wide = lambda r: r.unsqueeze(1).broadcast_to([P, TT, W1])
            v(vec.tensor_tensor(f_tok, f_tok, wide(one_lb), ALU.mult))
            v(vec.tensor_tensor(f_tok, f_tok, wide(lb), ALU.add))
            vec.tensor_scalar(hk_tok, f_tok, -1.0, 1.0, ALU.mult, ALU.add).then_inc(sem("hk_ready"), 1)
            for t in range(TT):
                bank = V.get(dve)
                vec.tensor_copy(v_m[:, t, :], bank[:, :]).then_inc(V.free, 1)
            for h in range(0, HEADS, 2):
                bank = V.get(dve)
                for j in range(2):
                    x, b, d = bank[:, j * S:(j + 1) * S], t_b[:, :, h + j], dm[:, h + j, :]
                    vec.scalar_tensor_tensor(d[:, 0:P], x[:, 0:P], b[:, 0:1], cst("causal"), ALU.add, ALU.add)
                    vec.tensor_scalar(d[:, P:2 * P], x[:, 0:P], b[:, 1:2], None, ALU.add)
                    ins = vec.scalar_tensor_tensor(d[:, 2 * P:3 * P], x[:, P:S], b[:, 1:2], cst("causal"),
                                                   ALU.add, ALU.add)
                ins.then_inc(V.free, 1)
            V.through(dve)
            vec.tensor_reduce(t_m[:, 0, :], dm[:, :, 0:P], AX_X, ALU.max)
            v(vec.tensor_reduce(t_m[:, 1, :], dm[:, :, P:3 * P], AX_X, ALU.max))
            vec.tensor_scalar(t_nm, t_m, -1.0, None, ALU.mult).then_inc(sem("m_max"), 1)
            for t in range(TT):
                bank = V.get(dve)
                vec.tensor_copy(v_h[:, t, :], bank[:, :]).then_inc(V.free, 1)
            for what, h in M_SEQ:
                if what == "S":
                    bank = V.get(dve)
                    dve.wait_ge(sem("m_weights"), h + 1)
                    for t, a0, b0 in ((0, 0, P), (1, P, 3 * P)):
                        ins = vec.tensor_tensor_reduce(dm[:, h, a0:b0], bank[:, a0:b0], dm[:, h, a0:b0],
                                                       float(P) ** -0.5, 0.0, ALU.mult, ALU.add, t_den[:, t, h:h + 1])
                        if t == 0:
                            v(ins)
                    ins.then_inc(sem("m_scores"), 1)
                    dve.wait_ge(sem("m_scores"), h + 1)
                    vec.memset(tiny[:, 500:501], 0.0).then_inc(V.free, 1)
                if what == "N":
                    if h == 0:
                        pass
                    v(vec.scalar_tensor_tensor(t_rec[:, :, h], t_den[:, :, h], -1.0, t_den[:, :, h], ALU.mult, ALU.max))
                    if h == 0:
                        dve.wait_ge(sem("m_weights"), HEADS + 1)
                    v(vec.tensor_tensor(t_rec[:, :, h], t_rec[:, :, h], t_em[:, :, h], ALU.max))
                    v(vec.reciprocal(t_rec[:, :, h], t_rec[:, :, h]))
                    bank = V.get(dve)
                    for t in range(TT):
                        ins = vec.tensor_scalar(yb[:, t, h * P:(h + 1) * P], bank[:, t * P:(t + 1) * P],
                                                t_rec[:, t, h:h + 1], None, ALU.mult)
                    ins.then_inc(V.free, 1)

            def decay(i):
                h, t = divmod(i, TT)
                await_mark(dve, f"decay{i}")
                e, q = decayed[i % 2][:, 0], decayed[i % 2][:, 1]
                at = slice(t * P, (t + 1) * P)
                v(vec.tensor_tensor(q[:, 0:NL + t, :], e[:, 0:NL + t, :],
                                    hq_ch[:, h, at].unsqueeze(1).broadcast_to([P, NL + t, P]), ALU.mult))
                ins = vec.tensor_tensor(e[:, 0:NL, :], e[:, 0:NL, :],
                                        hk_ch[:, h, at].unsqueeze(1).broadcast_to([P, NL, P]), ALU.mult)
                if t:
                    ins = vec.tensor_tensor(e[:, NL + 1, :], e[:, NL + 1, :], hk_ch[:, h, 0:P], ALU.mult)
                ins.then_inc(sem("h_decayed"), 1)

            def mask(i):
                for l0 in (0, 4):
                    bank = V.get(dve)
                    vec.tensor_tensor(masked[:, l0:l0 + 4, :], bank[:, :].rearrange("p (l s) -> p l s", s=P),
                                      cst("keep").rearrange("p (l s) -> p l s", s=P)[:, l0:l0 + 4, :],
                                      ALU.mult).then_inc(V.free, 1)
                if i % TT:
                    bank = V.get(dve)
                    vec.tensor_copy(att[:, 1, i % 2, :], bank[:, 0:P]).then_inc(V.free, 1)
                V.through(dve)
                vec.tensor_reduce(att[:, 0, i % 2, :], masked.rearrange("p l s -> p s l"), AX_X, ALU.add
                                  ).then_inc(sem("h_att"), 1)
                dve.wait_ge(sem("h_att"), i + 1)

            def take_out(i):
                h, t = divmod(i, TT)
                bank = V.get(dve)
                vec.tensor_copy(yb[:, t, W1 + h * P:W1 + (h + 1) * P], bank[:, 0:P]).then_inc(V.free, 1)

            decay(0)
            for i in range(HEADS * TT):
                if i < HEADS * TT - 1:
                    decay(i + 1)
                mask(i)
                if i:
                    take_out(i - 1)
            take_out(HEADS * TT - 1)
            V.through(dve)
            n = TT * 2 * HEADS
            squares = arena2[:, 0:2048].rearrange("p (t h w) -> p t h w", t=TT, h=2 * HEADS)
            by_head = yb[:, :, :].rearrange("p t (h w) -> p t h w", w=P)
            v(vec.tensor_tensor(squares, by_head, by_head, ALU.mult))
            v(vec.tensor_reduce(small[:, 128:128 + n].rearrange("p (t h) -> p t h", t=TT), squares, AX_X, ALU.add))
            rstd_dve(small[:, 160:160 + n], small[:, 128:128 + n], n, 1.0 / P, EPS)
            for t in range(TT):
                v(vec.tensor_tensor(by_head[:, t], by_head[:, t],
                                    small[:, 160 + t * 8:168 + t * 8].unsqueeze(2).broadcast_to([P, 8, P]), ALU.mult))
                v(vec.tensor_tensor(yb[:, t, :], yb[:, t, :], norms[:, 0:D], ALU.mult))
                vec.tensor_tensor(yb[:, t, :], yb[:, t, :], mixg[:, t, :], ALU.mult).then_inc(sem("y_mixed"), 1)
            for n in range(2):
                for t in range(TT):
                    bank = V.get(dve)
                    vec.tensor_copy(yb[:, t, n * 512:(n + 1) * 512], bank[:, :]).then_inc(V.free, 1)
            V.through(dve)
            add_residual_dve(G2)

        U = lambda arena, i, n=1: arena[:, i * D:(i + n) * D]
        C4 = lambda x: x.rearrange("p (q s) -> p q s", q=PAIRS)
        gates2 = U(arena1, 0, 4).rearrange("p (t w) -> p t w", t=TT)
        fqk = U(arena1, 4, 2).rearrange("p (c s) -> p c s", s=S)
        fv = U(arena1, 6).rearrange("p (t w) -> p t w", t=TT)
        yf, yr = C4(U(arena1, 7)), C4(U(arena1, 8))
        fdm = arena2[:, 0:FOX_H * 384].rearrange("p (h s) -> p h s", h=FOX_H)
        fsT = arena2[:, 3072:3072 + 4 * 384].rearrange("p (b s) -> p b s", b=4)
        raw = arena3[:, 0:14 * (S + 1)].rearrange("p (c s) -> p c s", c=14)
        shifted = arena4[:, 0:14 * S].rearrange("p (c s) -> p c s", s=S)
        r_c, k_c, v_c = shifted[:, 0:4], shifted[:, 4:8], shifted[:, 8:12]
        wa, gl = shifted[:, 12], shifted[:, 13]
        lora = U(arena4, 4)
        lw, cs, cb, kk, ai, bonus, g_c = [C4(U(arena5, i)) for i in range(7)]
        kap, bet, kh, rh = lw, cb, kk, r_c
        ec, tmp = C4(U(arena3, 0)), C4(U(arena3, 1))
        f8 = tiny[:, 128:144].rearrange("p (t g) -> p t g", t=TT)
        f_ax, f_e, f_l, f_lf, f_b, f_x, f_nm, f_den, f_rec = [
            tiny[:, 144 + 16 * i:160 + 16 * i].rearrange("p (t h) -> p t h", t=TT) for i in range(9)]
        f_m = tiny[:, 304:320].rearrange("p (t h) -> p t h", t=TT)
        GRP = 4

        def m4(arena, i, n, at=0):
            return arena[:, i * D + at:i * D + at + GRP * n].rearrange("p (c n) -> p c n", c=GRP)

        LC, BD = m4(arena2, 0, 128), m4(arena2, 0, 128, 512)
        powers = [m4(arena2, 1, 128), m4(arena2, 1, 128, 512), m4(arena2, 2, 128), m4(arena2, 2, 128, 512)]
        v_st, bet_st, kh_st = [m4(arena2, 3, 64, 256 * i) for i in range(3)]
        X = [m4(arena2, 4, 128), m4(arena2, 4, 128, 512)]

        def blocks4(arena, i):
            return U(arena, i).rearrange("p (c q n) -> p c q n", c=GRP, q=PAIRS)

        v_bd, bet_bd, u_bd, GT = blocks4(arena2, 5), blocks4(arena1, 4), blocks4(arena1, 5), blocks4(arena1, 6)
        Qp = m4(arena3, 2, 64)
        state = [arena3[:, 2304 + 256 * i:2560 + 256 * i].rearrange("p (q n) -> p q n", q=PAIRS) for i in range(2)]
        PAR = [slice(0, DH), slice(DH, P)]
        F_STEPS = FOX_H + 2

        def fox_pe(pe):
            for s in range(F_STEPS):
                if s < FOX_H:
                    par, h = PAR[s % 2], s // 2
                    q, k = fqk[par, h, :], fqk[par, 4 + h, :]
                    bank = V.take(pe)
                    pe.matmul(bank[:, 0:P], q[:, 0:P], k[:, 0:P], start=True, stop=True)
                    pe.matmul(bank[:, P:3 * P], q[:, P:S], k, start=True, stop=True).then_inc(V.done, 1)
                if 1 <= s <= FOX_H:
                    pe.wait_ge(sem("fox_probs"), s)
                    bank = A.take(pe)
                    for j in range(3):
                        ins = pe.transpose(bank[:, j * P:(j + 1) * P], fdm[:, s - 1, j * P:(j + 1) * P], ident)
                    ins.then_inc(A.done, 1)
                if s >= 3 and s % 2:
                    A.evacuated(pe)
                    bank = V.take(pe)
                    for h in (s - 3, s - 2):
                        par, w, val = PAR[h % 2], fsT[:, h % 4, :], fv[:, :, h * DH:(h + 1) * DH]
                        pe.matmul(bank[par, 0:P], val[:, 0, :], w[:, 0:P], start=True, stop=True)
                        pe.matmul(bank[par, P:S], val[:, 0, :], w[:, P:2 * P], start=True, stop=False)
                        ins = pe.matmul(bank[par, P:S], val[:, 1, :], w[:, 2 * P:3 * P], start=False, stop=True)
                    ins.then_inc(V.done, 1)

        def fox_act(act):
            for s in range(F_STEPS):
                if s < FOX_H:
                    act.wait_ge(sem("fox_max"), s + 1)
                    for t, a0, b0 in ((0, 0, P), (1, P, 3 * P)):
                        ins = nc.scalar.activation(fdm[:, s, a0:b0], fdm[:, s, a0:b0], ACT.Exp,
                                                   bias=f_nm[:, t, s:s + 1], accum_out=f_den[:, t, s:s + 1])
                    ins.then_inc(sem("fox_exp"), 1)
                if 1 <= s <= FOX_H:
                    bank = A.get(act)
                    nc.scalar.copy(fsT[:, (s - 1) % 4, :], bank[:, 0:3 * P]).then_inc(A.free, 1)

        def fox_dve(dve):
            vec = nc.vector
            for s in range(F_STEPS):
                if s < FOX_H:
                    bank = V.get(dve)
                    vec.scalar_tensor_tensor(fdm[:, s, :], bank[:, 0:3 * P], DH ** -0.5, fdm[:, s, :],
                                             ALU.mult, ALU.add).then_inc(V.free, 1)
                    V.through(dve)
                    vec.tensor_reduce(f_m[:, 0, s:s + 1], fdm[:, s, 0:P], AX_X, ALU.max)
                    v(vec.tensor_reduce(f_m[:, 1, s:s + 1], fdm[:, s, P:3 * P], AX_X, ALU.max))
                    vec.tensor_scalar(f_nm[:, :, s], f_m[:, :, s], -1.0, None, ALU.mult).then_inc(sem("fox_max"), 1)
                if 1 <= s <= FOX_H:
                    dve.wait_ge(sem("fox_exp"), s)
                    v(vec.reciprocal(f_rec[:, :, s - 1], f_den[:, :, s - 1]))
                    for t, a0, b0 in ((0, 0, P), (1, P, 3 * P)):
                        ins = vec.tensor_scalar(fdm[:, s - 1, a0:b0], fdm[:, s - 1, a0:b0],
                                                f_rec[:, t, s - 1:s], None, ALU.mult)
                    ins.then_inc(sem("fox_probs"), 1)
                if s >= 3 and s % 2:
                    bank = V.get(dve)
                    vec.tensor_copy(yf[:, (s - 3) // 2, :], bank[:, 0:S]).then_inc(V.free, 1)

        def par_sums_pe(pe, queue, src):
            for i in range(2):
                bank = queue.take(pe)
                pe.matmul(bank[:, :], cst("par_ones"), src[:, 2 * i:2 * i + 2, :], start=True,
                          stop=True).then_inc(queue.done, 1)

        def half(x, i):
            return x[:, 2 * i:2 * i + 2, :]

        def two(bank):
            return bank[:, :].rearrange("p (j s) -> p j s", j=2)

        by_chunk = lambda x: x.rearrange("p q s -> p (q s)").rearrange("p (c n) -> p c n", c=NCH)
        kap_n, bet_n, kh_n, v_n = by_chunk(kap), by_chunk(bet), by_chunk(kh), by_chunk(C4(arena3[:, 3072:4096]))

        def chunk_out(x):
            return x.rearrange("p c (q s) -> p q c s", q=PAIRS)

        def chunk_in(x):
            return x.rearrange("p q (c s) -> p q c s", s=CH)

        def chunk_ap(x, c, par):
            return x[par, :, c * CH:(c + 1) * CH] if x is rh else x[par, c, :]

        def four_chunks_pe(pe, g):
            cc = range(GRP)
            both = [(c, par) for c in cc for par in PAR]
            for pair in ((kap_n, bet_n), (kh_n, v_n)):
                bank = A.take(pe)
                for i, x in enumerate(pair):
                    for c, par in both:
                        ins = pe.matmul(bank[par, i * 256 + c * DH:i * 256 + (c + 1) * DH],
                                        chunk_ap(x, g * GRP + c, par), cst("id64")[par, :], start=True, stop=True)
                ins.then_inc(A.done, 1)
            for key in (bet_n, kh_n):
                bank = V.take(pe)
                for c, par in both:
                    for i, x in enumerate((kap_n, rh)):
                        ins = pe.matmul(bank[par, c * P + i * DH:c * P + (i + 1) * DH],
                                        chunk_ap(key, g * GRP + c, par), chunk_ap(x, g * GRP + c, par),
                                        start=True, stop=True)
                ins.then_inc(V.done, 1)
            bank = V.take(pe)
            for c, par in both:
                ins = pe.matmul(bank[par, c * DH:(c + 1) * DH], chunk_ap(kap_n, g * GRP + c, par),
                                chunk_ap(bet_n, g * GRP + c, par), start=True, stop=True)
            ins.then_inc(V.done, 1)
            A.evacuated(pe)
            V.evacuated(pe)
            bank = V.take(pe)
            for c, par in both:
                ins = pe.matmul(bank[par, c * DH:(c + 1) * DH], BD[par, c, 0:DH], v_st[par, c, :], start=True, stop=True)
            ins.then_inc(V.done, 1)
            for step in range(4):
                left = LC[:, :, 0:DH] if step == 0 else powers[step][:, :, DH:P]
                right = powers[step][:, :, 0:DH]
                if step < 3:
                    bank = A.take(pe)
                    for c, par in both:
                        ins = pe.matmul(bank[par, c * P:c * P + DH], left[par, c, :], right[par, c, :],
                                        start=True, stop=True)
                        ins = pe.matmul(bank[par, c * P + DH:(c + 1) * P], right[par, c, :], left[par, c, :],
                                        start=True, stop=True)
                    ins.then_inc(A.done, 1)
                V.evacuated(pe)
                bank = V.take(pe)
                for c, par in both:
                    ins = pe.matmul(bank[par, c * P:(c + 1) * P], left[par, c, :], X[step % 2][par, c, :],
                                    start=True, stop=True)
                ins.then_inc(V.done, 1)
                A.evacuated(pe)
            V.evacuated(pe)
            w, u = X[0][:, :, 0:DH], X[0][:, :, DH:P]
            for c0 in (0, 2):
                bank = V.take(pe)
                for c, par in both:
                    if c0 <= c < c0 + 2:
                        ins = pe.matmul(bank[par, (c - c0) * 256:(c - c0 + 1) * 256], w[par, c, :], bet_bd[par, c],
                                        start=True, stop=True)
                ins.then_inc(V.done, 1)
            bank = V.take(pe)
            for c, par in both:
                ins = pe.matmul(bank[par, c * DH:(c + 1) * DH], w[par, c, :], LC[par, c, DH:P], start=True, stop=True)
            ins.then_inc(V.done, 1)
            y_bank = A.take(pe)
            pe.wait_ge(sem("u_blocks"), g + 1)
            for c in cc:
                n = g * GRP + c
                old = state[n % 2]
                if n < NCH - 1:
                    bank = V.take(pe)
                    for par in PAR:
                        pe.matmul(bank[par, 0:256], kh_st[par, c, :], v_bd[par, c], start=True, stop=False)
                        ins = pe.matmul(bank[par, 0:256], bet_st[par, c, :], u_bd[par, c], start=False, stop=(n == 0))
                    if n:
                        V.evacuated_but(pe, 1)
                        for q in range(PAIRS):
                            for par in PAR:
                                ins = pe.matmul(bank[par, q * DH:(q + 1) * DH], GT[par, c, q, :], old[par, q, :],
                                                start=False, stop=(q == PAIRS - 1))
                    ins.then_inc(V.done, 1)
                else:
                    V.evacuated(pe)
                if n == 0:
                    V.evacuated_but(pe, 1)
                for par in PAR:
                    out_c = y_bank[par, c * DH:(c + 1) * DH]
                    pe.matmul(out_c, v_st[par, c, :], BD[par, c, DH:P], start=True, stop=False)
                    ins = pe.matmul(out_c, u[par, c, :], LC[par, c, DH:P], start=False, stop=(n == 0))
                    if n:
                        for q in range(PAIRS):
                            ins = pe.matmul(y_bank[par, c * DH + q * CH:c * DH + (q + 1) * CH], old[par, q, :],
                                            Qp[par, c, q * CH:(q + 1) * CH], start=False, stop=(q == PAIRS - 1))
            ins.then_inc(A.done, 1)

        def four_chunks_act(act, g):
            copy = nc.scalar.copy
            quad = lambda x: x.rearrange("p (c n) -> p c n", c=GRP)
            for dst in ((X[0][:, :, 0:DH], bet_st), (kh_st, v_st)):
                bank = A.get(act)
                copy(dst[0], quad(bank[:, 0:256]))
                copy(dst[1], quad(bank[:, 256:512])).then_inc(A.free, 1)
            mark(f"by_token{g}", A.free, 4 + A.emptied.n)
            for step in range(3):
                bank = A.get(act)
                copy(powers[step + 1], quad(bank[:, :])).then_inc(A.free, 1)
            bank = A.get(act)
            to = yr[:, :, g * GRP * CH:(g + 1) * GRP * CH].rearrange("p q (c s) -> p c q s", c=GRP)
            copy(to, bank[:, 0:256].rearrange("p (c q s) -> p c q s", c=GRP, q=PAIRS)).then_inc(A.free, 1)
            mark(f"y_chunks{g}", A.free, 4 + A.emptied.n)

        def four_chunks_dve(dve, g):
            vec = nc.vector
            quad = lambda x: x.rearrange("p (c n) -> p c n", c=GRP)
            mask = cst("s_t").unsqueeze(1).broadcast_to([P, GRP, P])
            for dst in (LC, BD):
                bank = V.get(dve)
                vec.tensor_tensor(dst, quad(bank[:, :]), mask, ALU.mult).then_inc(V.free, 1)
            bank = V.get(dve)
            vec.tensor_tensor(powers[0][:, :, 0:DH], quad(bank[:, 0:256]),
                              cst("t_s").unsqueeze(1).broadcast_to([P, GRP, DH]), ALU.mult).then_inc(V.free, 1)
            pairs = cst("pairs").unsqueeze(1).unsqueeze(3).broadcast_to([P, GRP, PAIRS, DH])

            def expand(dst, src):
                return vec.tensor_tensor(dst, src.unsqueeze(2).broadcast_to([P, GRP, PAIRS, DH]), pairs, ALU.mult)

            await_mark(dve, f"by_token{g}")
            bank = V.get(dve)
            vec.tensor_copy(X[0][:, :, DH:P], quad(bank[:, 0:256])).then_inc(V.free, 1)
            expand(v_bd, v_st)
            expand(bet_bd, bet_st)
            V.through(dve)
            for step in range(4):
                bank = V.get(dve)
                vec.tensor_tensor(X[(step + 1) % 2], X[step % 2], quad(bank[:, :]), ALU.add).then_inc(V.free, 1)
                V.through(dve)
            expand(u_bd, X[0][:, :, DH:P]).then_inc(sem("u_blocks"), 1)
            for c0 in (0, 2):
                bank = V.get(dve)
                vec.tensor_tensor(GT[:, c0:c0 + 2].rearrange("p c q n -> p (c q) n"),
                                  bank[:, :].rearrange("p (m n) -> p m n", n=DH),
                                  cst("id64").unsqueeze(1).broadcast_to([P, 8, DH]), ALU.add).then_inc(V.free, 1)
            bank = V.get(dve)
            r = rh[:, :, g * GRP * CH:(g + 1) * GRP * CH].rearrange("p q (c s) -> p c q s", c=GRP)
            vec.tensor_tensor(Qp.rearrange("p c (q s) -> p c q s", q=PAIRS),
                              bank[:, 0:256].rearrange("p (c q s) -> p c q s", c=GRP, q=PAIRS), r,
                              ALU.add).then_inc(V.free, 1)
            for c in range(GRP):
                n = g * GRP + c
                if n < NCH - 1:
                    bank = V.get(dve)
                    last = ec[:, :, n * CH + CH - 1:n * CH + CH].broadcast_to([P, PAIRS, DH])
                    vec.tensor_tensor(state[(n + 1) % 2], bank[:, 0:256].rearrange("p (q n) -> p q n", q=PAIRS),
                                      last, ALU.mult).then_inc(V.free, 1)

        def mix2_pe(pe):
            turn_pe(pe, yb, "mix2")
            A.evacuated(pe)
            narrow_pe(pe, col("w_fox"), FOX_H)
            for _ in range(11):
                staying_pe(pe, A)
            moving_pe(pe, V)
            cumulate_pe(pe, "f_logf", f_lf, FOX_H)
            moving_pe(pe, A)
            moving_pe(pe, A)
            rows_pe(pe, "f_x", f_x, FOX_H)
            pe.wait_ge(sem("lora_in"), 16)
            pe.wait_ge(sem("low_rank"), 1)
            for rows, rhs, at in ((PAR[0], wa, 0), (PAR[1], wa, 0), (slice(0, P), gl, 512)):
                for i in range(2):
                    bank = A.take(pe)
                    for j in range(2):
                        a0 = at + (2 * i + j) * P
                        ins = pe.matmul(bank[:, j * S:(j + 1) * S], lora[rows, a0:a0 + P], rhs[rows, :],
                                        start=True, stop=True)
                    ins.then_inc(A.done, 1)
            moving_pe(pe, A)
            moving_pe(pe, A)
            pe.wait_ge(sem("rw_squares"), 1)
            par_sums_pe(pe, A, tmp)
            pe.wait_ge(sem("rw_bonus"), 1)
            par_sums_pe(pe, V, bonus)
            fox_pe(pe)
            V.evacuated(pe)
            for _ in range(2):
                moving_pe(pe, V, k_tiles=4, src=yf)
            pe.wait_ge(sem("rw_ready"), 1)
            for g in range(NCH // GRP):
                four_chunks_pe(pe, g)
            A.evacuated(pe)
            par_sums_pe(pe, V, yr)
            pe.wait_ge(sem("rw_var"), 1)
            par_sums_pe(pe, A, tmp)
            pe.wait_ge(sem("rw_out"), 1)
            for _ in range(2):
                moving_pe(pe, V, k_tiles=4, src=yr)
            turn_pe(pe, yb, "merged")
            A.evacuated(pe)
            moving_pe(pe, V)
            moving_pe(pe, V)

        def mix2_act(act):
            turn_act(act)
            act.dma_start(lora, dram["lora"]).then_inc(sem("lora_in"), 16)
            act.wait_ge(sem("f_gates"), 1)
            a(nc.scalar.activation(f_e, f_ax, ACT.Exp, scale=-1.0))
            nc.scalar.activation(f_l, f_e, ACT.Ln, bias=1.0).then_inc(sem("f_log"), 1)
            for c in range(4):
                bank = A.get(act)
                nc.scalar.copy(half(fqk, c), two(bank)).then_inc(A.free, 1)
            for c in range(7):
                bank = A.get(act)
                nc.scalar.copy(raw[:, 2 * c:2 * c + 2, 1:], two(bank)).then_inc(A.free, 1)
            mark("raw", A.free, 4 + A.emptied.n)
            for n in range(2):
                for t in range(TT):
                    bank = A.get(act)
                    nc.scalar.activation(gates2[:, t, n * 512:(n + 1) * 512], bank[:, :], ACT.Sigmoid).then_inc(A.free, 1)
            act.wait_ge(sem("shifted"), 1)
            nc.scalar.activation(wa[0:DH, :], wa[0:DH, :], ACT.Tanh)
            nc.scalar.activation(gl, gl, ACT.Sigmoid).then_inc(sem("low_rank"), 1)
            for dst, bias in ((lw, "w0"), (ai, "a0")):
                for i in range(2):
                    bank = A.get(act)
                    for j in range(2):
                        ins = nc.scalar.activation(dst[:, 2 * i + j, :], bank[:, j * S:(j + 1) * S], ACT.Sigmoid,
                                                   bias=col(bias)[:, 2 * i + j:2 * i + j + 1])
                    ins.then_inc(A.free, 1)
            mark("decay_and_a", A.free, 4 + A.emptied.n)
            for i in range(2):
                bank = A.get(act)
                nc.scalar.copy(half(g_c, i), two(bank)).then_inc(A.free, 1)
            for n in range(2, 4):
                for t in range(TT):
                    bank = A.get(act)
                    nc.scalar.activation(gates2[:, t, n * 512:(n + 1) * 512], bank[:, :], ACT.Sigmoid).then_inc(A.free, 1)
            for i in range(2):
                bank = A.get(act)
                nc.scalar.activation(half(tmp, i), two(bank), ACT.Sqrt).then_inc(A.free, 1)
            mark("norms", A.free, 4 + A.emptied.n)
            act.wait_ge(sem("rw_sums"), 1)
            a(nc.scalar.activation(ec, cs, ACT.Exp))
            nc.scalar.activation(cb, cb, ACT.Exp)
            nc.scalar.activation(cs, cs, ACT.Exp, scale=-1.0).then_inc(sem("rw_exps"), 1)
            fox_act(act)
            for g in range(NCH // GRP):
                four_chunks_act(act, g)
            act.wait_ge(sem("gn_eps"), 1)
            for i in range(2):
                bank = A.get(act)
                nc.scalar.activation(half(tmp, i), two(bank), ACT.Sqrt, bias=small[:, 503:504], scale=1.0 / DH
                                     ).then_inc(A.free, 1)
            mark("deviations", A.free, 4 + A.emptied.n)
            turn_act(act)
            act.wait_ge(sem("rw_out"), 1)
            act.dma_start(arena2[:, 0:4 * D], dram["lns"].partition_broadcast(P)).then_inc(sem("lns_in"), 16)
            root_act(TT)

        lns = arena2[:, 0:4 * D].rearrange("p (m d) -> p m d", m=4)

        def layer_norm_dve(i, tag):
            vec = nc.vector
            v(vec.scalar_tensor_tensor(xh[:, :, :], xh[:, :, :], ALPHA, yb[:, :, :], ALU.mult, ALU.add))
            v(vec.tensor_reduce(small[:, 140:142], xh[:, :, :], AX_X, ALU.add))
            v(vec.tensor_scalar(small[:, 142:144], small[:, 140:142], -1.0 / D, None, ALU.mult))
            for t in range(TT):
                ins = vec.tensor_scalar(xh[:, t, :], xh[:, t, :], small[:, 142 + t:143 + t], None, ALU.add)
            v(ins)
            for t in range(TT):
                ins = vec.tensor_tensor_reduce(yb[:, t, :], xh[:, t, :], xh[:, t, :], 1.0, 0.0,
                                               ALU.mult, ALU.add, small[:, 128 + t:129 + t])
            v(ins)
            rstd_dve(small[:, 130:132], small[:, 128:130], TT, 1.0 / D, LN_EPS)
            for t in range(TT):
                v(vec.scalar_tensor_tensor(xh[:, t, :], xh[:, t, :], small[:, 130 + t:131 + t], lns[:, i, :],
                                           ALU.mult, ALU.mult))
                vec.tensor_tensor(xh[:, t, :], xh[:, t, :], lns[:, i + 1, :], ALU.add).then_inc(sem(f"y_{tag}"), 1)
            nc.vector.wait_ge(sem(f"y_{tag}"), TT)

        def mix2_dve(dve):
            vec = nc.vector
            for t in range(TT):
                vec.tensor_copy(yb[:, t, :], xh[:, t, :]).then_inc(sem("y_mix2"), 1)
            vec.memset(raw[:, :, 0:1], 0.0)
            vec.memset(small[:, 503:504], GN_EPS).then_inc(sem("gn_eps"), 1)
            bank = V.get(dve)
            vec.tensor_tensor(f8, bank[:, 0:16].rearrange("p (t g) -> p t g", t=TT),
                              col("fox_b").unsqueeze(1).broadcast_to([P, TT, 8]), ALU.add).then_inc(V.free, 1)
            V.through(dve)
            vec.scalar_tensor_tensor(f_ax, f8, -1.0, f8, ALU.mult, ALU.max).then_inc(sem("f_gates"), 1)
            dve.wait_ge(sem("f_log"), 1)
            vec.scalar_tensor_tensor(f_lf, f8, 0.0, f_l, ALU.min, ALU.subtract).then_inc(sem("f_logf"), 1)
            await_mark(dve, "raw")
            v(vec.tensor_tensor(shifted, raw[:, :, 0:S], raw[:, :, 1:], ALU.subtract))
            for c in range(13, -1, -1):
                ins = vec.scalar_tensor_tensor(shifted[:, c, :], shifted[:, c, :], col("mu")[:, c:c + 1],
                                               raw[:, c, 1:], ALU.mult, ALU.add)
                if c == 12:
                    ins.then_inc(sem("shifted"), 1)
            v(ins)
            for t in range(TT):
                bank = V.get(dve)
                vec.tensor_copy(fv[:, t, :], bank[:, :]).then_inc(V.free, 1)
            bank = V.get(dve)
            vec.tensor_copy(f_b, bank[:, 0:16].rearrange("p (t h) -> p t h", t=TT)).then_inc(V.free, 1)
            V.through(dve)
            vec.tensor_scalar(f_x, f_b, -1.0, None, ALU.mult).then_inc(sem("f_x"), 1)
            for q in range(PAIRS):
                ins = vec.tensor_scalar(kk[:, q, :], k_c[:, q, :], col("k_k")[:, q:q + 1], None, ALU.mult)
            v(ins)
            vec.tensor_tensor(tmp, kk, kk, ALU.mult).then_inc(sem("rw_squares"), 1)
            for h in range(0, FOX_H, 2):
                bank = V.get(dve)
                for j in range(2):
                    x, b, d = bank[:, j * S:(j + 1) * S], f_b[:, :, h + j], fdm[:, h + j, :]
                    vec.scalar_tensor_tensor(d[:, 0:P], x[:, 0:P], b[:, 0:1], cst("causal"), ALU.add, ALU.add)
                    vec.tensor_scalar(d[:, P:2 * P], x[:, 0:P], b[:, 1:2], None, ALU.add)
                    ins = vec.scalar_tensor_tensor(d[:, 2 * P:3 * P], x[:, P:S], b[:, 1:2], cst("causal"),
                                                   ALU.add, ALU.add)
                ins.then_inc(V.free, 1)
            V.through(dve)
            await_mark(dve, "decay_and_a")
            v(vec.tensor_scalar(lw, lw, -float(np.exp(-0.5)), None, ALU.mult))
            for q in range(PAIRS):
                ins = vec.tensor_tensor_scan(cs[:, q, :], cst("starts"), lw[:, q, :], 0.0, ALU.mult, ALU.add)
            v(ins)
            vec.tensor_tensor(cb, cs, lw, ALU.subtract).then_inc(sem("rw_sums"), 1)
            await_mark(dve, "norms")
            v(vec.tensor_scalar(tmp, tmp, 1e-12, None, ALU.max))
            v(vec.reciprocal(tmp, tmp))
            v(vec.tensor_tensor(kk, kk, tmp, ALU.mult))
            for q in range(PAIRS):
                ins = vec.tensor_scalar(tmp[:, q, :], ai[:, q, :], -1.0, col("k_a")[:, q:q + 1], ALU.add, ALU.mult)
            v(ins)
            v(vec.scalar_tensor_tensor(k_c, tmp, 1.0, k_c, ALU.add, ALU.mult))
            v(vec.tensor_tensor(bonus, r_c, k_c, ALU.mult))
            for q in range(PAIRS):
                ins = vec.tensor_scalar(bonus[:, q, :], bonus[:, q, :], col("r_k")[:, q:q + 1], None, ALU.mult)
            ins.then_inc(sem("rw_bonus"), 1)
            v(vec.scalar_tensor_tensor(ai, ai, -1.0, kk, ALU.mult, ALU.mult))
            dve.wait_ge(sem("rw_exps"), 1)
            v(vec.tensor_tensor(chunk_out(kap_n), chunk_in(kk), chunk_in(cb), ALU.mult))
            vec.tensor_tensor(chunk_out(bet_n), chunk_in(ai), chunk_in(cs), ALU.mult)
            vec.tensor_tensor(chunk_out(kh_n), chunk_in(k_c), chunk_in(cs), ALU.mult)
            vec.tensor_copy(chunk_out(v_n), chunk_in(v_c))
            vec.tensor_tensor(rh, r_c, ec, ALU.mult).then_inc(sem("rw_ready"), 1)
            for i in range(2):
                bank = V.get(dve)
                vec.tensor_tensor(half(bonus, i), half(v_c, i), two(bank), ALU.mult).then_inc(V.free, 1)
            fox_dve(dve)
            for n in range(2):
                for t in range(TT):
                    bank = V.get(dve)
                    at = slice(n * 512, (n + 1) * 512)
                    vec.tensor_tensor(yb[:, t, at], gates2[:, t, at], bank[:, :], ALU.mult).then_inc(V.free, 1)
            for g in range(NCH // GRP):
                four_chunks_dve(dve, g)
            await_mark(dve, f"y_chunks{NCH // GRP - 1}")
            for i in range(2):
                bank = V.get(dve)
                vec.scalar_tensor_tensor(half(yr, i), two(bank), -1.0 / DH, half(yr, i), ALU.mult, ALU.add
                                         ).then_inc(V.free, 1)
            V.through(dve)
            vec.tensor_tensor(tmp, yr, yr, ALU.mult).then_inc(sem("rw_var"), 1)
            await_mark(dve, "deviations")
            v(vec.reciprocal(tmp, tmp))
            v(vec.tensor_tensor(yr, yr, tmp, ALU.mult))
            for q in range(PAIRS):
                ins = vec.tensor_scalar(yr[:, q, :], yr[:, q, :], col("ln_g")[:, q:q + 1], col("ln_b")[:, q:q + 1],
                                        ALU.mult, ALU.add)
            v(ins)
            v(vec.tensor_tensor(yr, yr, bonus, ALU.add))
            vec.tensor_tensor(yr, yr, g_c, ALU.mult).then_inc(sem("rw_out"), 1)
            part = U(arena5, 0).rearrange("p (j n) -> p j n", j=2)
            for n in range(2):
                for t in range(TT):
                    bank = V.get(dve)
                    at = slice(n * 512, (n + 1) * 512)
                    vec.tensor_tensor(part[:, t, :], gates2[:, t, n * 512 + D:(n + 1) * 512 + D], bank[:, :],
                                      ALU.mult).then_inc(V.free, 1)
                    V.through(dve)
                    ins = vec.tensor_tensor(yb[:, t, at], yb[:, t, at], part[:, t, :], ALU.add)
                    if n == 1:
                        ins.then_inc(sem("y_merged"), 1)
                    else:
                        v(ins)
            for n in range(2):
                for t in range(TT):
                    bank = V.get(dve)
                    vec.tensor_copy(yb[:, t, n * 512:(n + 1) * 512], bank[:, :]).then_inc(V.free, 1)
            V.through(dve)
            dve.wait_ge(sem("lns_in"), 16)
            layer_norm_dve(0, "peer")

        NH2 = 2 * PH
        NPICK = PH * TOPK
        qT = U(arena1, 0, 4).rearrange("p (h s) -> p h s", h=NH2)
        scores = U(arena1, 4, 4).rearrange("p (t h k) -> p t h k", t=TT, h=NH2)
        top_s = arena3[:, 0:256].rearrange("p (h k) -> p h k", h=NH2)
        top_i = arena3[:, 256:512].bitcast(U32).rearrange("p (h k) -> p h k", h=NH2)
        top_f = arena3[:, 512:768].rearrange("p (h c k) -> p h c k", h=PH, c=2)
        sums = arena3[:, 1024:3072].rearrange("p (h i j) -> p h i j", h=PH, i=TOPK)
        spare_key = arena3[:, 3072:3072 + NH2 * NKEY].rearrange("p (h k) -> p h k", h=NH2)
        spare_sum = U(arena4, 0, 2).rearrange("p (h m) -> p h m", h=PH)
        one_hot = U(arena4, 2, 2).rearrange("p (h k i) -> p h k i", h=PH, k=TOPK)
        best = arena4[:, 4096:4352].rearrange("p (t h k) -> p t h k", t=TT, h=PH)
        pos = arena4[:, 4352:4480].bitcast(U32).rearrange("p (h k) -> p h k", h=PH)
        digit_u = arena4[:, 4480:4608].bitcast(U32).rearrange("p (h k) -> p h k", h=PH)
        digit_f = arena4[:, 4608:4736].rearrange("p (h k) -> p h k", h=PH)
        key_no = arena4[:, 4736:4992].rearrange("p (c h k) -> p c h k", c=2, h=PH)
        expert_f = arena4[:, 4992:5120].rearrange("p (h k) -> p h k", h=PH)
        expert = arena5[:, 0:256].bitcast(U32).rearrange("p (t n) -> p t n", t=TT)
        hidden = arena5[:, 256:512].rearrange("p (t n) -> p t n", t=TT)
        denom = arena5[:, 512:528].rearrange("p (t h) -> p t h", t=TT)
        dots = arena5[:, 544:576].rearrange("p (b n) -> p b n", b=2)
        picked = arena5[:, 576:608].bitcast(U32).rearrange("p (b n) -> p b n", b=2)
        ROWS = 8
        rows_in = ring[:, :, :].rearrange("p g n -> p (g n)").rearrange("p (b d) -> p b d", b=ROWS)
        acc = yb
        row_landed = [sem(f"row_landed{j}") for j in range(ROWS)]
        row_used, picked_copied = sem("row_used"), sem("picked_copied")
        PASSES = NPICK // ROWS

        def peer_pe(pe):
            turn_pe(pe, xh, "peer")
            A.evacuated(pe)
            for _ in range(8):
                staying_pe(pe, A)
            A.evacuated(pe)
            keys = next_chunk(pe)[:, :].rearrange("p (h k) -> p h k", h=NH2)
            for t in range(TT):
                for h0 in range(0, NH2, 4):
                    bank = A.take(pe)
                    for h in range(h0, h0 + 4):
                        ins = pe.matmul(bank[:, (h - h0) * P:(h - h0 + 1) * P], qT[:, h, t * P:(t + 1) * P], keys[:, h, :],
                                        start=True, stop=True)
                        if t == h == 0:
                            ins.then_inc(begun, 1)
                    ins.then_inc(A.done, 1)

        def peer_act(act):
            turn_act(act)
            for c in range(8):
                bank = A.get(act)
                nc.scalar.copy(qT[:, 2 * c:2 * c + 2, :], two(bank)).then_inc(A.free, 1)
            for t in range(TT):
                for h0 in range(0, NH2, 4):
                    bank = A.get(act)
                    nc.scalar.copy(scores[:, t, h0:h0 + 4, :], bank[:, :].rearrange("p (h k) -> p h k", h=4)
                                   ).then_inc(A.free, 1)
                mark(f"scores{t}", A.free, 4 + A.emptied.n)
            for t in range(TT):
                act.wait_ge(sem("best_ready"), t + 1)
                nc.scalar.activation(best[:, t], best[:, t], ACT.Exp).then_inc(sem("best_exp"), 1)
            for t in range(TT):
                act.wait_ge(sem("dots_ready"), t + 1)
                nc.scalar.activation(hidden[:, t, :], hidden[:, t, :], ACT.Gelu).then_inc(sem("gelu_ready"), 1)
            root_act(TT)

        def top16_dve(values, indices, src, spare):
            vec = nc.vector
            v(vec.max(values[:, 0:8], src))
            vec.max_index(indices[:, 0:8], values[:, 0:8], src)
            v(vec.match_replace(spare, values[:, 0:8], src, NEG))
            v(vec.max(values[:, 8:16], spare))
            return vec.max_index(indices[:, 8:16], values[:, 8:16], spare)

        def pick_dve(dve, t):
            vec = nc.vector
            await_mark(dve, f"scores{t}")
            for h in range(NH2):
                ins = top16_dve(top_s[:, h, :], top_i[:, h, :], scores[:, t, h, :], spare_key[:, h, :])
            v(ins)
            halves = top_s.rearrange("p (h c) k -> p h c k", c=2)
            v(vec.tensor_copy(top_f.rearrange("p h c k -> p (h c) k"), top_i))
            v(vec.tensor_tensor(sums, halves[:, :, 0, :].unsqueeze(3).broadcast_to([P, PH, TOPK, TOPK]),
                                halves[:, :, 1, :].unsqueeze(2).broadcast_to([P, PH, TOPK, TOPK]), ALU.add))
            flat = sums.rearrange("p h i j -> p h (i j)")
            for h in range(PH):
                ins = top16_dve(best[:, t, h, :], pos[:, h, :], flat[:, h, :], spare_sum[:, h, :])
            v(ins)
            for c, (op, by) in enumerate(((ALU.logical_shift_right, 4), (ALU.bitwise_and, 15))):
                v(vec.tensor_scalar(digit_u, pos, by, None, op))
                v(vec.tensor_copy(digit_f, digit_u))
                v(vec.tensor_tensor(one_hot, digit_f.unsqueeze(3).broadcast_to([P, PH, TOPK, TOPK]),
                                    cst("digits").unsqueeze(1).unsqueeze(1).broadcast_to([P, PH, TOPK, TOPK]),
                                    ALU.is_equal))
                v(vec.tensor_tensor(one_hot, one_hot, top_f[:, :, c, :].unsqueeze(2).broadcast_to([P, PH, TOPK, TOPK]),
                                    ALU.mult))
                v(vec.tensor_reduce(key_no[:, c], one_hot, AX_X, ALU.add))
            v(vec.scalar_tensor_tensor(expert_f, key_no[:, 0], float(NKEY), key_no[:, 1], ALU.mult, ALU.add))
            vec.tensor_copy(expert[:, t, :].rearrange("p (h k) -> p h k", h=PH), expert_f).then_inc(sem("expert_ready"), 1)
            v(vec.tensor_copy(denom[:, t, :], best[:, t, :, 0]))
            vec.tensor_tensor(best[:, t], best[:, t], denom[:, t, :].unsqueeze(2).broadcast_to([P, PH, TOPK]),
                              ALU.subtract).then_inc(sem("best_ready"), 1)
            dve.wait_ge(sem("best_exp"), t + 1)
            v(vec.tensor_reduce(denom[:, t, :], best[:, t], AX_X, ALU.add))
            v(vec.reciprocal(denom[:, t, :], denom[:, t, :]))
            v(vec.tensor_tensor(best[:, t], best[:, t], denom[:, t, :].unsqueeze(2).broadcast_to([P, PH, TOPK]),
                                ALU.mult))

        rows_count = {"dve": 0}

        def dots_dve(dve, t):
            base = rows_count["dve"]
            with dve.Fori(0, PASSES) as i:
                for j in range(ROWS):
                    dve.wait_ge(row_landed[j], (i + base + 1) * 16)
                    nc.vector.tensor_tensor_reduce(rows_in[:, j, :], rows_in[:, j, :], xh[:, t, :], 1.0, 0.0, ALU.mult,
                                                   ALU.add, dots[:, 0, j:j + 1]).then_inc(row_used, 1)
                dve.wait_ge(row_used, (i + base + 1) * ROWS)
                nc.vector.tensor_copy(hidden[:, t, bass.ds(i * ROWS, ROWS)], dots[:, 0, 0:ROWS]).then_inc(sem("dots_kept"), 1)
                dve.wait_ge(sem("dots_kept"), i + t * PASSES + 1)
            rows_count["dve"] += PASSES
            nc.vector.memset(small[:, 504:505], 0.0).then_inc(sem("dots_ready"), 1)

        def coef_dve(dve, t):
            dve.wait_ge(sem("gelu_ready"), t + 1)
            v(nc.vector.tensor_tensor(hidden[:, t, :], hidden[:, t, :], best[:, t].rearrange("p h k -> p (h k)"), ALU.mult))

        def mix_rows_dve(dve, t):
            base = rows_count["dve"]
            v(nc.vector.memset(acc[:, t, :], 0.0))
            with dve.Fori(0, PASSES) as i:
                for j in range(ROWS):
                    dve.wait_ge(row_landed[j], (i + base + 1) * 16)
                    dve.wait_ge(row_used, (i + base) * ROWS + j)
                    nc.vector.scalar_tensor_tensor(acc[:, t, :], rows_in[:, j, :], hidden[:, t, bass.ds(i * ROWS + j, 1)],
                                                   acc[:, t, :], ALU.mult, ALU.add).then_inc(row_used, 1)
            rows_count["dve"] += PASSES
            dve.wait_ge(row_used, rows_count["dve"] * ROWS)

        def peer_dve(dve):
            for t in range(TT):
                pick_dve(dve, t)
            dots_dve(dve, 0)
            coef_dve(dve, 0)
            dots_dve(dve, 1)
            coef_dve(dve, 1)
            for t in range(TT):
                mix_rows_dve(dve, t)
            layer_norm_dve(2, "result")

        def peer_pool(pool):
            turn = 0
            pool.wait_ge(*marks["scores1"])
            for table, t in (("experts_u", 0), ("experts_u", 1), ("experts_v", 0), ("experts_v", 1)):
                base = turn * PASSES
                pool.wait_ge(sem("expert_ready"), t + 1)

                def one_pass(i, b):
                    for j in range(ROWS):
                        if turn or not isinstance(i, int) or i:
                            pool.wait_ge(row_used, (i + base - 1) * ROWS + j + 1)
                        if j == 0:
                            nc.gpsimd.tensor_copy(picked[:, b, 0:ROWS], expert[:, t, bass.ds(i * ROWS, ROWS)]
                                                  ).then_inc(picked_copied, 1)
                            pool.wait_ge(picked_copied, i + base + 1)
                        pool.sem_inc(sem("gather_asked"), 1)
                        nc.gpsimd.indirect_dma_start(
                            out=rows_in[:, j, :], out_offset=None, in_=dram[table],
                            in_offset=bass.IndirectOffsetOnAxis(ap=picked[:, b, j:j + 1], axis=0)
                            ).then_inc(row_landed[j], 16)

                if turn == 0:
                    one_pass(0, 0)
                    one_pass(1, 1)
                with pool.Fori(int(turn == 0), PASSES // 2) as i:
                    one_pass(i * 2, 0)
                    one_pass(i * 2 + 1, 1)
                turn += 1

        block = ctx.enter_context(nc.Block())
        stream = dram["stream"]

        @block.sync
        def _(sp):
            sp.dma_start(cols[:, :], dram["cols"]).then_inc(sem("cols_in"), 16)
            sp.dma_start(const[:, :], dram["const"]).then_inc(sem("const_in"), 16)
            for g in range(SLOTS):
                sp.dma_start(ring[:, g, :], stream[g]).then_inc(landed[g], 16)
            with sp.Fori(0, stream.shape[0] // SLOTS - 1) as i:
                for j in range(SLOTS):
                    sp.wait_ge(begun, i * SLOTS + j + 2)
                    sp.dma_start(ring[:, j, :], stream[(i + 1) * SLOTS + j]).then_inc(landed[j], 16)
            sp.wait_ge(sem("y_result"), TT)
            sp.dma_start(out.rearrange("b (t p) d -> p (b t) d", p=P), xh[:, :, :]).then_inc(sem("out_written"), 16)
            sp.wait_ge(sem("out_written"), 16)

        @block.tensor
        def _(pe):
            pe.wait_ge(sem("const_in"), 16)
            ada_pe(pe)
            ffn_pe(pe, "ffn1")
            mix_pe(pe)
            ffn_pe(pe, "ffn2")
            mix2_pe(pe)
            peer_pe(pe)

        @block.scalar
        def _(act):
            act.dma_start(arena1[:, :], dram["ada_b"].partition_broadcast(P)).then_inc(sem("ada_b_in"), 16)
            act.dma_start(xh[:, :, :], dram["x"].rearrange("b (t p) d -> p (b t) d", p=P)).then_inc(sem("x_in"), 16)
            act.dma_start(arena2[:, :], dram["gains"].partition_broadcast(P)).then_inc(sem("gains_in"), 16)
            act.dma_start(norms, dram["norms"].partition_broadcast(P)).then_inc(sem("norms_in"), 16)
            nc.scalar.memzero(small[:, 500:501]).then_inc(A.free, 4)
            ada_act(act)
            ffn_act(act, "ffn1")
            mix_act(act)
            ffn_act(act, "ffn2")
            mix2_act(act)
            peer_act(act)

        @block.gpsimd
        def _(pool):
            peer_pool(pool)

        @block.vector
        def _(dve):
            nc.vector.memset(small[:, 501:502], 0.0).then_inc(V.free, 4)
            dve.wait_ge(sem("x_in"), 16)
            ada_dve(dve)
            ffn_dve(dve, "ffn1", SC1, SH1, G1)
            mix_dve(dve)
            ffn_dve(dve, "ffn2", SC3, SH3, G3)
            mix2_dve(dve)
            peer_dve(dve)



def layout(inputs):
    x = {k: np.asarray(v) for k, v in inputs.items()}
    f = x["w_in"][0]
    m = np.split(f, np.cumsum([512, 512, 512, 512, 8, 512, 512, 512])[:8], axis=1)
    mq, mk, mv, mo, mif, hq, hf, hi, hg = m
    s = x["w_in_2"][0]
    fq, fk, fv, ff, rr, rk, rv, rwa, rg, gates = np.split(
        s, np.cumsum([512, 512, 512, 8, 512, 512, 512, 128, 128])[:9], axis=1)
    ffn = [np.concatenate([gate_up(x[n + "_w_gate"][0], x[n + "_w_up"][0]), down(x[n + "_w_down"][0])])
           for n in ("ffn1", "ffn2")]
    keys = np.ascontiguousarray(x["peer_sub_keys_2"][0].transpose(3, 0, 1, 2)).reshape(1, P, CHUNK)
    stream = np.concatenate([
        a_form(x["ada_w"][0]), ffn[0],
        w_form(np.concatenate([mq, mk, hq], 1)), a_form(np.concatenate([hf, mv, mo, hi, hg], 1)),
        a_form(x["w_out"][0]), ffn[1],
        w_form(np.concatenate([fq, fk, rr, rk, rv, rwa, rg], 1)), a_form(np.concatenate([fv, gates], 1)),
        a_form(x["p_fox_2"][0]), a_form(x["p_rwkv_2"][0]), a_form(x["w_o_2"][0]),
        w_form(x["peer_w_q_2"][0]), keys])
    const, const_at = pack(constants())
    mu = x["rwkv_mu_2"][0]
    cols, cols_at = pack({
        "c": columns(x["c"][0]), "conv_w": columns(x["mlstm_conv_w"][0]), "conv_b": columns(x["mlstm_conv_b"][0]),
        "w_mif": narrow(mif), "w_fox": narrow(ff), "gate_b": spread(x["mlstm_gate_b"][0]),
        "fox_b": spread(x["fox_f_bias_2"][0]), "mu": columns(mu), "w0": columns(x["rwkv_w0_2"][0]),
        "a0": columns(x["rwkv_a0_2"][0]), "k_k": columns(x["rwkv_k_k_2"][0]), "k_a": columns(x["rwkv_k_a_2"][0]),
        "r_k": columns(x["rwkv_r_k_2"][0]), "ln_g": columns(x["rwkv_ln_g_2"][0]), "ln_b": columns(x["rwkv_ln_b_2"][0])})
    lora = np.concatenate([np.concatenate([x["rwkv_w2_2"][0], x["rwkv_a2_2"][0]], 0), x["rwkv_g2_2"][0]], 1)
    mats, where = {"stream": stream, "const": const, "cols": cols, "lora": np.ascontiguousarray(lora)}, {}
    mats["gains"] = np.concatenate([x[n][0] for n in ("ffn1_pre_g", "ffn1_post_g", "mix_pre_g", "mix_post_g",
                                                      "ffn2_pre_g", "ffn2_post_g")])
    mats["norms"] = np.concatenate([x["mlstm_norm_g"][0], x["hgrn_norm_g"][0], x["hgrn_lb_logits"].reshape(-1)])
    mats["lns"] = np.concatenate([x[n][0] for n in ("ln1_g_2", "ln1_b_2", "ln2_g_2", "ln2_b_2")])
    mats["ada_b"], mats["x"] = x["ada_b"][0], x["x"]
    mats["experts_u"], mats["experts_v"] = x["peer_u_2"][0], x["peer_v_2"][0]
    return {k: np.ascontiguousarray(v) for k, v in mats.items()}, {"const": const_at, "cols": cols_at}


def kernel(**inputs):
    import concourse.bacc as _bacc
    from concourse import mybir as _mybir
    from concourse.bass_utils import run_bass_kernel_spmd as _run

    nc = _bacc.Bacc("TRN2", target_bir_lowering=False, num_devices=1)
    arrays, where = layout(inputs)
    dram = {k: nc.dram_tensor(f"in_{k}", a.shape, _mybir.dt.from_np(a.dtype), kind="ExternalInput").ap()
            for k, a in arrays.items()}
    out = nc.dram_tensor("out_0", (1, S, D), F32, kind="ExternalOutput").ap()
    program(nc, dram, out, where)
    r = _run(nc, [{f"in_{k}": a for k, a in arrays.items()}], core_ids=[0])
    return r.results[0]["out_0"]
```

```python
from contextlib import ExitStack

import concourse.bass as bass
import numpy as np
from concourse import mybir

ALU = mybir.AluOpType
ACT = mybir.ActivationFunctionType
F32 = mybir.dt.float32
F32R = mybir.dt.float32r
BF16 = mybir.dt.bfloat16
U32 = mybir.dt.uint32
AX_X = mybir.AxisListType.X

P = 128
S, D, F = 256, 1024, 2816
TT, KT, FT = S // P, D // P, F // P
N_MOD = 9
HEADS, W1 = 4, 512
FOX_H, RW_H, DH = 8, 8, 64
PAIRS = RW_H // 2
CH = 16
NCH = S // CH
PH, NKEY, TOPK = 8, 128, 16
NEXP = NKEY * NKEY
EARLY = 44
GROUP = 4
EPS, LN_EPS, GN_EPS = 1e-6, 1e-5, 64e-5
ALPHA = 2.0 ** 0.25
SLOTS, CHUNK = 4, 2048
LEVELS = [64, 32, 16, 8, 4, 2, 1]
NEG = -3.0e38



def w_form(w):
    k, n = w.shape
    v = w.reshape(k // P, P, n // 256, 256).transpose(2, 1, 0, 3)
    return np.ascontiguousarray(v).reshape(-1, P, CHUNK)


def a_form(w):
    k, n = w.shape
    v = w.reshape(k // 512, 4, P, n // 512, 512).transpose(3, 0, 2, 1, 4)
    return np.ascontiguousarray(v).reshape(-1, P, CHUNK)


def gate_up(wg, wu):
    v = np.stack([wg.reshape(KT, P, FT, P), wu.reshape(KT, P, FT, P)], axis=3)
    return np.ascontiguousarray(v.transpose(2, 1, 0, 3, 4)).reshape(-1, P, CHUNK)


def down(w):
    v = w.reshape(FT // 2, 2, P, D).transpose(0, 2, 1, 3)
    return np.ascontiguousarray(v).reshape(-1, P, CHUNK)


def narrow(w):
    return np.ascontiguousarray(w.reshape(KT, P, -1).transpose(1, 0, 2)).reshape(P, -1)


def columns(v):
    v = np.atleast_2d(v)
    return np.ascontiguousarray(v.reshape(v.shape[0], -1, P).transpose(2, 0, 1)).reshape(P, -1)


def spread(v):
    return np.ascontiguousarray(np.broadcast_to(v.reshape(1, -1), (P, v.size)))


def constants():
    u, t = np.arange(P)[:, None], np.arange(P)[None, :]
    out = {"ident": u == t, "ones": np.ones((P, P)), "tri": u <= t, "after": u > t}
    out["par_ones"] = u // DH == t // DH
    decay, keep = [], []
    for m in LEVELS:
        half = (t // m) % 2 == 1
        start = t // (2 * m) * (2 * m)
        decay.append(np.where(half, (u >= start + m) & (u <= t), (u > t) & (u < start + m)))
        keep.append((u // (2 * m) == t // (2 * m)) & ((u // m) % 2 == 0) & half)
    out["decay"] = np.concatenate(decay, 1)
    out["keep"] = np.concatenate(keep + [u == t], 1)
    out["causal"] = np.where(t <= u, 0.0, NEG)
    out["id64"] = u % DH == np.arange(DH)[None, :]
    q, r = np.arange(P)[:, None] % DH, np.arange(DH)[None, :]
    same = q // CH == r // CH
    out["s_t"] = np.concatenate([same & (q < r), same & (q <= r)], 1)
    out["t_s"] = same & (r < q)
    out["pairs"] = q // CH == np.arange(PAIRS)[None, :]
    out["starts"] = np.broadcast_to(np.arange(S)[None, :] % CH != 0, (P, S))
    return {k: np.ascontiguousarray(v, dtype=np.float32) for k, v in out.items()}


def pack(parts):
    at, where = 0, {}
    for name, a in parts.items():
        where[name] = (at, at + a.shape[1])
        at += a.shape[1]
    return np.ascontiguousarray(np.concatenate(list(parts.values()), axis=1)), where



class Count:

    def __init__(self):
        self.n, self.term = 0, None

    def at(self, n):
        return n if self.term is None else self.term + n


class Banks:

    def __init__(self, banks, done, free):
        self.banks, self.done, self.free = banks, done, free
        self.filled, self.emptied = Count(), Count()

    def take(self, pe):
        c = self.filled
        pe.wait_ge(self.free, c.at(c.n + 1))
        c.n += 1
        return self.banks[(c.n - 1) % 4]

    def evacuated(self, pe):
        c = self.filled
        pe.wait_ge(self.free, c.at(c.n + 4))

    def evacuated_but(self, pe, n):
        c = self.filled
        pe.wait_ge(self.free, c.at(c.n + 4 - n))

    def get(self, eng):
        c = self.emptied
        eng.wait_ge(self.done, c.at(c.n + 1))
        c.n += 1
        return self.banks[(c.n - 1) % 4]

    def through(self, eng):
        c = self.emptied
        eng.wait_ge(self.free, c.at(c.n + 4))


def loop(eng, total, unroll, body, counts):
    passes = total // unroll
    if passes > 1:
        starts = [c.n for c, _ in counts]
        with eng.Fori(0, passes) as i:
            for c, per in counts:
                c.term = i * per
            for j in range(unroll):
                body(i * unroll + j, j)
        for (c, per), start in zip(counts, starts):
            assert c.n - start == per
            c.n, c.term = start + per * passes, None
    else:
        passes = 0
    for g in range(passes * unroll, total):
        body(g, g)



def program(nc, dram, out, where):
    ctx = ExitStack()
    with ctx:
        sems = {}

        def sem(name):
            if name not in sems:
                sems[name] = ctx.enter_context(nc.semaphore(name))
            return sems[name]

        def sb(name, shape, dt=F32):
            return ctx.enter_context(nc.sbuf_tensor(name, shape, dt))

        sizes = {"arena3": FT * S, "arena4": 6 * D, "arena5": 7 * D, "arena1": N_MOD * D, "arena2": 6 * D}
        shared = {"ring": SLOTS * CHUNK, "yT": KT * S, "yb": TT * D, "field": sum(sizes.values())}
        with ExitStack() as names:
            rounded = {name: names.enter_context(nc.sbuf_tensor(f"{name}_rounded", [P, n], F32R))
                       for name, n in [*list(shared.items())[:3], *sizes.items()]}
        ring_flat_r, yT_r, yb_r, arena2_r, arena3_r, arena4_r, arena5_r = [
            rounded[name] for name in ("ring", "yT", "yb", "arena2", "arena3", "arena4", "arena5")]
        ring_flat, yT_flat, yb, field = [sb(name, [P, n]) for name, n in shared.items()]

        def arena(name):
            start = sum(list(sizes.values())[:list(sizes).index(name)])
            return field[:, start:start + sizes[name]]

        arena1, arena2, arena3, arena4, arena5 = [arena(f"arena{i}") for i in range(1, 6)]
        yb = yb[:, :].rearrange("p (t d) -> p t d", t=TT)
        ring = ring_flat[:, :].rearrange("p (g n) -> p g n", g=SLOTS)
        ring_r = ring_flat_r[:, :].rearrange("p (g n) -> p g n", g=SLOTS)
        yT = yT_flat[:, :].rearrange("p (k s) -> p k s", s=S)
        yT_r = yT_r[:, :].rearrange("p (k s) -> p k s", s=S)
        n_const = max(b for _, b in where["const"].values())
        const = sb("const", [P, n_const])

        def cst(name):
            a, b = where["const"][name]
            return const[:, a:b]

        n_cols = max(b for _, b in where["cols"].values())
        cols = sb("cols", [P, n_cols])

        def col(name):
            a, b = where["cols"][name]
            return cols[:, a:b]

        xh = sb("xh", [P, TT, D])
        small = sb("small", [P, 512])

        banks = [ctx.enter_context(nc.psum_tensor(f"bank{i}", [P, 512], F32)) for i in range(8)]
        A = Banks(banks[:4], sem("act_bank_filled"), sem("act_bank_free"))
        V = Banks(banks[4:], sem("dve_bank_filled"), sem("dve_bank_free"))

        mod = arena1[:, :].rearrange("p (m d) -> p m d", m=N_MOD)
        gains = arena2[:, :].rearrange("p (m d) -> p m d", m=6)
        hT = arena3[:, :].rearrange("p (f s) -> p f s", s=S)
        hT_r = arena3_r[:, :].rearrange("p (f s) -> p f s", s=S)
        sgate = arena4[:, 0:4 * S].rearrange("p (j s) -> p j s", j=4)
        weight_top = arena4_r[:, 2048:2048 + 2 * CHUNK].rearrange("p (b n) -> p b n", b=2)
        y_top = [arena4_r[:, 1024:2048].rearrange("p (k s) -> p k s", k=4),
                 arena5_r[:, FT * S:FT * S + 1024].rearrange("p (k s) -> p k s", k=4)]
        hT_top = arena5_r[:, 0:FT * S].rearrange("p (f s) -> p f s", s=S)
        hT_junk = arena3[:, 0:2 * D].rearrange("p (t d) -> p t d", t=TT)
        junk = arena2[:, 0:2 * D].rearrange("p (t d) -> p t d", t=TT)
        SH1, SC1, G1, SH2, SC2, G2, SH3, SC3, G3 = range(N_MOD)

        tiny = sb("tiny", [P, 512])
        ident = cst("ident")
        ones_32 = tiny[:, KT * 32:KT * 32 + 32]

        landed = [sem(f"chunk_landed{j}") for j in range(SLOTS)]
        begun = sem("chunk_begun")
        chunks = Count()
        v_steps, a_steps, g_steps = Count(), Count(), Count()
        root_asked, root_done = sem("root_asked"), sem("root_done")
        roots = {"dve": 0, "act": 0}

        def v(ins):
            v_steps.n += 1
            ins.then_inc(sem("dve_step"), 1)
            nc.vector.wait_ge(sem("dve_step"), v_steps.at(v_steps.n))

        def a(ins):
            a_steps.n += 1
            ins.then_inc(sem("act_step"), 1)
            nc.scalar.wait_ge(sem("act_step"), a_steps.at(a_steps.n))

        def next_chunk(pe):
            g = chunks.n
            n = 16 * (g // SLOTS + 1)
            pe.wait_ge(landed[g % SLOTS], n if chunks.term is None else chunks.term * (16 // SLOTS) + n)
            chunks.n += 1
            return ring[:, g % SLOTS, :]

        top_chunks, rest_chunks = Count(), Count()
        weights_split = sem("weights_split")
        weight_splits = {"dve": Count(), "pe": Count(), "act": Count()}

        def split_dve(top, rest, x):
            v(nc.vector.tensor_copy(top, x))
            return nc.vector.tensor_tensor(rest, x, top.bitcast(F32), ALU.subtract)

        def top_chunk_act(act, gap=0):
            g = top_chunks.n
            n = 16 * (g // SLOTS + 1)
            act.wait_ge(landed[g % SLOTS], n if top_chunks.term is None else top_chunks.term * (16 // SLOTS) + n)
            act.wait_ge(begun, top_chunks.at(g - gap))
            top_chunks.n += 1
            weight_splits["act"].n += 1
            for half in (slice(0, CHUNK // 2), slice(CHUNK // 2, CHUNK)):
                nc.scalar.copy(weight_top[:, (weight_splits["act"].n - 1) % 2, half], ring[:, g % SLOTS, half]
                               ).then_inc(sem("weight_top_ready"), 1)

        def rest_chunk_dve(dve):
            g, c = rest_chunks.n, weight_splits["dve"]
            rest_chunks.n += 1
            c.n += 1
            for i, half in enumerate((slice(0, CHUNK // 2), slice(CHUNK // 2, CHUNK))):
                done = 2 * c.n - 1 + i
                dve.wait_ge(sem("weight_top_ready"), done if c.term is None else c.term * 2 + done)
                ins = nc.vector.tensor_tensor(ring_r[:, g % SLOTS, half], ring[:, g % SLOTS, half],
                                              weight_top[:, (c.n - 1) % 2, half].bitcast(F32), ALU.subtract)
            ins.then_inc(weights_split, 1)

        def next_split_chunk(pe):
            g, c = chunks.n, weight_splits["pe"]
            c.n += 1
            pe.wait_ge(weights_split, c.at(c.n))
            chunks.n += 1
            return weight_top[:, (c.n - 1) % 2, :], ring_r[:, g % SLOTS, :]

        def three_passes(pe, bank, stays, moves, start, stop):
            (s_top, s_rest), (m_top, m_rest) = stays, moves
            first = pe.matmul(bank, s_top, m_top, start=start, stop=False)
            pe.matmul(bank, s_top, m_rest, start=False, stop=False)
            return first, pe.matmul(bank, s_rest, m_top, start=False, stop=stop)


        def root_act(n):
            roots["act"] += 1
            nc.scalar.wait_ge(root_asked, roots["act"])
            nc.scalar.activation(small[:, 64:64 + n], small[:, 0:n], ACT.Sqrt).then_inc(root_done, 1)

        def rstd_dve(dst, ss, n, scale, eps):
            roots["dve"] += 1
            nc.vector.tensor_scalar(small[:, 0:n], ss, scale, eps, ALU.mult, ALU.add).then_inc(root_asked, 1)
            nc.vector.wait_ge(root_done, roots["dve"])
            v(nc.vector.reciprocal(dst, small[:, 64:64 + n]))

        def square_sums(src, n, junk=junk):
            for i in range(n):
                ins = nc.vector.tensor_tensor_reduce(junk[:, i, 0:src.shape[2]], src[:, i, :], src[:, i, :], 1.0, 0.0,
                                                     ALU.mult, ALU.add, small[:, 128 + i:129 + i])
            v(ins)

        def modulated_norm_dve(sc, sh, tag):
            square_sums(xh, TT, hT_junk if tag == "ffn1" else junk)
            rstd_dve(small[:, 130:132], small[:, 128:130], TT, 1.0 / D, EPS)
            for t in range(TT):
                v(nc.vector.scalar_tensor_tensor(yb[:, t, :], xh[:, t, :], small[:, 130 + t:131 + t],
                                                 mod[:, sc, :], ALU.mult, ALU.mult))
                nc.vector.tensor_tensor(yb[:, t, :], yb[:, t, :], mod[:, sh, :],
                                        ALU.add).then_inc(sem(f"y_{tag}"), 1)

        def turn_pe(pe, src, tag, by_tile=True):
            for t in range(TT):
                pe.wait_ge(sem(f"y_{tag}"), t + 1)
                for k in range(0, KT, 4):
                    bank = A.take(pe)
                    for j in range(4):
                        ins = pe.transpose(bank[:, j * P:(j + 1) * P], src[:, t, (k + j) * P:(k + j + 1) * P],
                                           ident)
                    ins.then_inc(A.done, 1)

        def turn_act(act):
            for t in range(TT):
                for k in range(0, KT, 4):
                    bank = A.get(act)
                    nc.scalar.copy(yT[:, k:k + 4, t * P:(t + 1) * P],
                                   bank[:, :].rearrange("p (j s) -> p j s", j=4)).then_inc(A.free, 1)

        def moving_pe(pe, queue, k_tiles=KT, src=None):
            src = yT if src is None else src
            two = [queue.take(pe), queue.take(pe)]
            for c in range(0, k_tiles, 4):
                w = next_chunk(pe)[:, :].rearrange("p (k n) -> p k n", k=4)
                for t in range(TT):
                    for k in range(4):
                        ins = pe.matmul(two[t][:, :], src[:, c + k, t * P:(t + 1) * P], w[:, k, :],
                                        start=(c + k == 0), stop=(c + k == k_tiles - 1))
                        if t == 0 and k == 0:
                            ins.then_inc(begun, 1)
                    if c + k == k_tiles - 1:
                        ins.then_inc(queue.done, 1)

        def staying_pe(pe, queue, src=None):
            src = yT if src is None else src
            bank = queue.take(pe)
            w = next_chunk(pe)[:, :].rearrange("p (k n) -> p k n", k=KT)
            for j in range(2):
                for k in range(KT):
                    ins = pe.matmul(bank[:, j * S:(j + 1) * S], w[:, k, j * P:(j + 1) * P], src[:, k, :],
                                    start=(k == 0), stop=(k == KT - 1))
                    if j == 0 and k == 0:
                        ins.then_inc(begun, 1)
            ins.then_inc(queue.done, 1)

        def add_residual_dve(g):
            square_sums(yb, TT)
            rstd_dve(small[:, 130:132], small[:, 128:130], TT, 1.0 / D, EPS)
            for t in range(TT):
                v(nc.vector.scalar_tensor_tensor(yb[:, t, :], yb[:, t, :], small[:, 130 + t:131 + t],
                                                 mod[:, g, :], ALU.mult, ALU.mult))
                v(nc.vector.tensor_tensor(xh[:, t, :], xh[:, t, :], yb[:, t, :], ALU.add))


        silu_c = tiny[:, 0:KT * 32].rearrange("p (k n) -> p k n", k=KT)
        ADA, ADA_FIRST = N_MOD * D // 512, 4
        partial_late = arena5[:, 7 * D - 512:7 * D]

        def partial(tile):
            if isinstance(tile, int) and tile < ADA_FIRST:
                return arena3[:, tile * 512:(tile + 1) * 512]
            return partial_late

        def ada_groups_pe(pe, tile, halves=(0, 1)):
            if 0 in halves:
                ada_groups_pe.bank = A.take(pe)
            bank = ada_groups_pe.bank
            for c in halves:
                w = next_chunk(pe)[:, :].rearrange("p (k n) -> p k n", k=4)
                for k in range(4):
                    ins = pe.matmul(bank[32 * k:32 * k + 32, :], silu_c[:, 4 * c + k, :], w[:, k, :],
                                    start=(c == 0), stop=(c == 1 and k > 0))
                    if k == 0:
                        ins.then_inc(begun, 1)
            if 1 not in halves:
                return
            if isinstance(tile, int) and tile in (0, ADA_FIRST):
                pe.wait_ge(sem(f"ada_b_in{int(tile > 0)}"), 16)
            pe.matmul(bank[0:32, :], ones_32, arena1[:, bass.ds(tile * 512, 512)], start=False, stop=True
                      ).then_inc(A.done, 1)

        def ada_sum_pe(pe, tile, but=0):
            A.evacuated_but(pe, but)
            bank = A.take(pe)
            pe.matmul(bank[:, :], cst("ones"), partial(tile), start=True, stop=True).then_inc(A.done, 1)

        def ada_groups_act(act, tile):
            bank = A.get(act)
            nc.scalar.copy(partial(tile), bank[:, :]).then_inc(A.free, 1)

        def ada_sum_act(act, tile):
            bank = A.get(act)
            nc.scalar.activation(arena1[:, bass.ds(tile * 512, 512)], bank[:, :], ACT.Copy, scale=1.0 / 32
                                 ).then_inc(A.free, 1)

        def ada_pe(pe):
            pe.wait_ge(sem("silu_c_spread"), 1)
            for tile in range(ADA_FIRST):
                ada_groups_pe(pe, tile)
                if tile == 0:
                    pe.wait_ge(sem("const_in"), 16)
                else:
                    ada_sum_pe(pe, tile - 1, but=1)
            ada_sum_pe(pe, ADA_FIRST - 1)

        def ada_act(act):
            act.wait_ge(sem("cols_in"), 16)
            nc.scalar.activation(col("c"), col("c"), ACT.Silu).then_inc(sem("silu_c"), 1)
            for tile in range(ADA_FIRST):
                ada_groups_act(act, tile)
                if tile:
                    ada_sum_act(act, tile - 1)
            ada_sum_act(act, ADA_FIRST - 1)
            marks["first_rows"] = (A.free, 4 + A.emptied.n)

        marks = {}

        def ada_dve(dve):
            v(nc.vector.memset(tiny[:, :], 1.0))
            dve.wait_ge(sem("silu_c"), 1)
            for k in range(KT):
                ins = nc.vector.tensor_scalar(silu_c[:, k, :], silu_c[:, k, :], col("c")[:, k:k + 1], None, ALU.mult)
            ins.then_inc(sem("silu_c_spread"), 1)
            dve.wait_ge(*marks["first_rows"])
            dve.wait_ge(sem("first_gain_in"), 16)
            v(nc.vector.scalar_tensor_tensor(mod[:, SC1, :], mod[:, SC1, :], 1.0, gains[:, 0, :], ALU.add, ALU.mult))

        def ada_rest_dve(dve):
            dve.wait_ge(*marks["all_rows"])
            dve.wait_ge(sem("gains_in"), 16)
            for i, sc in ((1, SC2), (2, SC3)):
                nc.vector.scalar_tensor_tensor(mod[:, sc, :], mod[:, sc, :], 1.0, gains[:, 2 * i, :], ALU.add, ALU.mult)
            for i, (g, w) in enumerate(((G1, 0.5), (G2, 1.0), (G3, 0.5))):
                ins = nc.vector.scalar_tensor_tensor(mod[:, g, :], mod[:, g, :], w, gains[:, 2 * i + 1, :], ALU.mult, ALU.mult)
            v(ins)


        ADA_LAST_PAIRS = ADA - ADA_FIRST - FT // 2

        def ffn_pe(pe, tag):
            V_seen[tag] = V.filled.n
            chunk_at[tag] = chunks.n
            turn_pe(pe, yb, tag)
            pe.wait_ge(sem(f"y_split_{tag}"), 1)

            def gate_up_tile(g, j):
                bank = V.take(pe)
                top, rest = [w.rearrange("p (k n) -> p k n", k=KT) for w in next_split_chunk(pe)]
                for c in range(2):
                    for k in range(KT):
                        cols_c = slice(c * P, (c + 1) * P)
                        first, last = three_passes(pe, bank[:, c * S:(c + 1) * S],
                                                   (top[:, k, cols_c], rest[:, k, cols_c]),
                                                   (y_top[k // 4][:, k % 4, :], yT_r[:, k, :]), k == 0, k == KT - 1)
                        if c == k == 0:
                            first.then_inc(begun, 1)
                last.then_inc(V.done, 1)

            def pair(g, j):
                gate_up_tile(2 * g, 0)
                if not isinstance(g, int) or g > 0:
                    ada_sum_pe(pe, None)
                ada_groups_pe(pe, g + ADA_FIRST, (0,))
                gate_up_tile(2 * g + 1, 1)
                ada_groups_pe(pe, g + ADA_FIRST, (1,))

            if tag == "ffn1":
                pair(0, 0)
                loop(pe, FT // 2 - 1, 2, lambda g, j: pair(g + 1, j),
                     [(chunks, 8), (V.filled, 4), (A.filled, 4), (weight_splits["pe"], 4)])
            else:
                loop(pe, FT, 4, gate_up_tile, [(chunks, 4), (V.filled, 4), (weight_splits["pe"], 4)])
            four = [V.take(pe) for _ in range(4)]
            pe.wait_ge(sem(f"hidden_split_{tag}"), 1)
            for g in range(FT // 2):
                top, rest = [w.rearrange("p (k n) -> p k n", k=2) for w in next_split_chunk(pe)]
                for k in range(2):
                    f = 2 * g + k
                    for t in range(TT):
                        tokens = slice(t * P, (t + 1) * P)
                        for n in range(2):
                            outs = slice(n * 512, (n + 1) * 512)
                            first, last = three_passes(pe, four[2 * t + n][:, :], (hT_top[:, f, tokens], hT_r[:, f, tokens]),
                                                       (top[:, k, outs], rest[:, k, outs]), f == 0, f == FT - 1)
                            if k == t == n == 0:
                                first.then_inc(begun, 1)
                            if f == FT - 1:
                                last.then_inc(V.done, 1)
                if tag == "ffn1" and g % 2 == 0 and g // 2 <= ADA_LAST_PAIRS:
                    ada_sum_pe(pe, None)
                if tag == "ffn1" and g // 2 < ADA_LAST_PAIRS:
                    ada_groups_pe(pe, ADA - ADA_LAST_PAIRS + g // 2, (g % 2,))
            V_end[tag] = V.filled.n

        def ffn_act(act, tag):
            top_chunks.n = chunk_at[tag]
            top_chunk_act(act)
            root_act(TT)
            turn_act(act)
            turned[tag] = A.emptied.n
            filled = Count()
            filled.n = V_seen[tag]

            def gate(g, gap=0):
                top_chunks.n += gap // 2
                top_chunk_act(act, gap)
                filled.n += 1
                act.wait_ge(V.done, filled.at(filled.n))
                nc.scalar.activation(sgate[:, (filled.n - 1) % 4, :], V.banks[(filled.n - 1) % 4][:, 0:S],
                                     ACT.Silu).then_inc(sem("gate_ready"), 1)

            def pair(g, j):
                gate(2 * g, 2)
                if not isinstance(g, int) or g > 0:
                    ada_sum_act(act, g + ADA_FIRST - 1)
                gate(2 * g + 1, 2)
                ada_groups_act(act, None)

            if tag == "ffn1":
                pair(0, 0)
                loop(act, FT // 2 - 1, 2, lambda g, j: pair(g + 1, j), [(filled, 4), (top_chunks, 8), (A.emptied, 4)])
                for g in range(FT // 2):
                    if g + 1 < FT // 2:
                        top_chunks.n += g // 2 < ADA_LAST_PAIRS
                        top_chunk_act(act, sum(i // 2 < ADA_LAST_PAIRS for i in (g - 1, g)))
                    if g % 2 == 0 and g // 2 <= ADA_LAST_PAIRS:
                        ada_sum_act(act, ADA - ADA_LAST_PAIRS + g // 2 - 1)
                    if g % 2 and g // 2 < ADA_LAST_PAIRS:
                        ada_groups_act(act, None)
                marks["all_rows"] = (A.free, 4 + A.emptied.n)
            else:
                loop(act, FT, 4, lambda g, j: gate(g), [(filled, 4), (top_chunks, 4)])
                for _ in range(FT // 2 - 1):
                    top_chunk_act(act)
            if tag == "ffn1":
                act.wait_ge(V.done, V_end[tag])
                act.dma_start(norms, dram["norms"].partition_broadcast(P)).then_inc(sem("norms_in"), 16)
            root_act(TT)

        V_seen, V_end, chunk_at, turned = {}, {}, {}, {}
        gates = Count()

        def ffn_dve(dve, tag, sc, sh, g):
            rest_chunks.n = chunk_at[tag]
            rest_chunk_dve(dve)
            modulated_norm_dve(sc, sh, tag)
            for i in range(4):
                dve.wait_ge(A.free, 4 + turned[tag] - 3 + i)
                k, tokens = i % 2 * 4, slice(i // 2 * P, (i // 2 + 1) * P)
                ins = split_dve(y_top[i % 2][:, :, tokens], yT_r[:, k:k + 4, tokens], yT[:, k:k + 4, tokens])
            ins.then_inc(sem(f"y_split_{tag}"), 1)

            def hidden_tile(i):
                rest_chunks.n += tag == "ffn1"
                rest_chunk_dve(dve)
                bank = V.get(dve)
                gates.n += 1
                dve.wait_ge(sem("gate_ready"), gates.at(gates.n))
                v(nc.vector.tensor_tensor(hT[:, i, :], sgate[:, (V.emptied.n - 1) % 4, :], bank[:, S:2 * S],
                                          ALU.mult))
                split_dve(hT_top[:, i, :], hT_r[:, i, :], hT[:, i, :]).then_inc(V.free, 1)

            def pair(i, j):
                hidden_tile(2 * i)
                hidden_tile(2 * i + 1)

            if tag == "ffn1":
                loop(dve, FT // 2, 2, pair, [(V.emptied, 4), (gates, 4), (rest_chunks, 8), (weight_splits["dve"], 4), (v_steps, 8)])
            else:
                loop(dve, FT, 4, lambda i, j: hidden_tile(i),
                     [(V.emptied, 4), (gates, 4), (rest_chunks, 4), (weight_splits["dve"], 4), (v_steps, 8)])
            V.through(dve)
            nc.vector.memset(small[:, 505:506], 0.0).then_inc(sem(f"hidden_split_{tag}"), 1)
            for i in range(FT // 2 - 1):
                rest_chunks.n += tag == "ffn1" and i // 2 < ADA_LAST_PAIRS
                rest_chunk_dve(dve)
            if tag == "ffn1":
                ada_rest_dve(dve)
            for i in range(4):
                bank = V.get(dve)
                nc.vector.tensor_copy(yb[:, i // 2, (i % 2) * 512:(i % 2 + 1) * 512], bank[:, :]).then_inc(V.free, 1)
            V.through(dve)
            add_residual_dve(g)

        def mark(name, semaphore, value):
            marks[name] = (semaphore, value)

        def await_mark(dve, name):
            dve.wait_ge(*marks[name])

        PAD = 3
        conv_in = arena2[:, 0:8 * (S + PAD)].rearrange("p (c s) -> p c s", c=8)
        qk_ch = arena2[:, 2072:2072 + 8 * S].rearrange("p (c s) -> p c s", c=8)
        hq_ch = arena2[:, 4120:5144].rearrange("p (h s) -> p h s", h=HEADS)
        sT = arena2[:, 5144:5912].rearrange("p (b s) -> p b s", b=2)
        v_m = arena3[:, 0:1024].rearrange("p (t w) -> p t w", t=TT)
        v_h = arena3[:, 1024:2048].rearrange("p (t w) -> p t w", t=TT)
        f_tok = arena3[:, 2048:3072].rearrange("p (t w) -> p t w", t=TT)
        hk_tok = arena3[:, 3072:4096].rearrange("p (t w) -> p t w", t=TT)
        lb = arena3[:, 4096:4608]
        one_lb = arena3[:, 4608:5120]
        norms = arena4[:, 1024:3072]
        mixg = arena4[:, 3072:5120].rearrange("p (t w) -> p t w", t=TT)
        hk_ch = arena4[:, 5120:6144].rearrange("p (h s) -> p h s", h=HEADS)
        NL = len(LEVELS)
        decayed = [arena5[:, i * 2304:(i + 1) * 2304].rearrange("p (k l s) -> p k l s", k=2, s=P) for i in range(2)]
        masked = arena5[:, 4608:5632].rearrange("p (l s) -> p l s", s=P)
        dm = arena5[:, 5632:7168].rearrange("p (h s) -> p h s", h=HEADS)
        att = arena3[:, 5120:5632].rearrange("p (k b s) -> p k b s", k=2, b=2)
        gate8 = tiny[:, 0:16].rearrange("p (t g) -> p t g", t=TT)
        t_ax, t_e, t_l, t_lf, t_b, t_x, t_nm, t_m, t_den, t_em, t_rec = [
            tiny[:, 16 + 8 * i:24 + 8 * i].rearrange("p (t h) -> p t h", t=TT) for i in range(11)]

        M_SEQ = [("S", 0), ("S", 1), ("T", 0), ("S", 2), ("N", 0), ("T", 1), ("S", 3), ("N", 1), ("T", 2), ("N", 2),
                 ("T", 3), ("N", 3)]

        def narrow_pe(pe, w, n):
            bank = V.take(pe)
            for t in range(TT):
                for k in range(KT):
                    ins = pe.matmul(bank[:, t * n:(t + 1) * n], yT[:, k, t * P:(t + 1) * P], w[:, k * n:(k + 1) * n],
                                    start=(k == 0), stop=(k == KT - 1))
            ins.then_inc(V.done, 1)

        def cumulate_pe(pe, ready, lf, n):
            pe.wait_ge(sem(ready), 1)
            bank = V.take(pe)
            pe.matmul(bank[:, 0:n], cst("tri"), lf[:, 0, :], start=True, stop=True)
            pe.matmul(bank[:, n:2 * n], cst("ones"), lf[:, 0, :], start=True, stop=False)
            pe.matmul(bank[:, n:2 * n], cst("tri"), lf[:, 1, :], start=False, stop=True).then_inc(V.done, 1)

        def rows_pe(pe, ready, x, heads):
            pe.wait_ge(sem(ready), 1)
            for h in range(0, heads, 2):
                bank = V.take(pe)
                for j in range(2):
                    for t in range(TT):
                        ins = pe.matmul(bank[:, j * S + t * P:j * S + (t + 1) * P],
                                        x[:, t, h + j:h + j + 1].broadcast_to([P, P]), ident, start=True, stop=True)
                ins.then_inc(V.done, 1)

        def mix_pe(pe):
            turn_pe(pe, yb, "mix")
            A.evacuated(pe)
            narrow_pe(pe, col("w_mif"), 8)
            for _ in range(4):
                staying_pe(pe, A)
            for _ in range(2):
                staying_pe(pe, A)
            moving_pe(pe, A)
            cumulate_pe(pe, "m_logf", t_lf, HEADS)
            moving_pe(pe, V)
            rows_pe(pe, "m_x", t_x, HEADS)
            moving_pe(pe, A)
            moving_pe(pe, V)
            pe.wait_ge(sem("hk_ready"), 1)
            for t in range(TT):
                bank = A.take(pe)
                for h in range(HEADS):
                    ins = pe.transpose(bank[:, h * P:(h + 1) * P], hk_tok[:, t, h * P:(h + 1) * P], ident)
                ins.then_inc(A.done, 1)
            moving_pe(pe, A)
            pe.wait_ge(sem("qk_ready"), 1)
            for what, h in M_SEQ:
                if what == "S":
                    bank = V.take(pe)
                    q, k = qk_ch[:, h, :], qk_ch[:, 4 + h, :]
                    pe.matmul(bank[:, 0:P], q[:, 0:P], k[:, 0:P], start=True, stop=True)
                    pe.matmul(bank[:, P:3 * P], q[:, P:S], k, start=True, stop=True).then_inc(V.done, 1)
                if what == "T":
                    pe.wait_ge(sem("m_scores"), h + 1)
                    bank = A.take(pe)
                    for j in range(3):
                        ins = pe.transpose(bank[:, j * P:(j + 1) * P], dm[:, h, j * P:(j + 1) * P], ident)
                    ins.then_inc(A.done, 1)
                if what == "N":
                    A.evacuated(pe)
                    bank = V.take(pe)
                    val = v_m[:, :, h * P:(h + 1) * P]
                    w = sT[:, h % 2, :]
                    pe.matmul(bank[:, 0:P], w[:, 0:P], val[:, 0, :], start=True, stop=True)
                    pe.matmul(bank[:, P:2 * P], w[:, P:2 * P], val[:, 0, :], start=True, stop=False)
                    pe.matmul(bank[:, P:2 * P], w[:, 2 * P:3 * P], val[:, 1, :], start=False, stop=True).then_inc(V.done, 1)

            def decays(i):
                h, t = divmod(i, TT)
                lf = f_tok[:, :, h * P:(h + 1) * P]
                for a0, b0 in ((0, 512), (512, NL * P)):
                    bank = A.take(pe)
                    pe.matmul(bank[:, 0:b0 - a0], lf[:, t, :], cst("decay")[:, a0:b0], start=True,
                              stop=True).then_inc(A.done, 1)
                if t:
                    bank = A.take(pe)
                    pe.matmul(bank[:, 0:P], lf[:, 1, :], cst("tri"), start=True, stop=True)
                    pe.matmul(bank[:, P:2 * P], lf[:, 0, :], cst("after"), start=True, stop=True).then_inc(A.done, 1)

            def attend(i):
                h, t = divmod(i, TT)
                pe.wait_ge(sem("h_decayed"), i + 1)
                q, k = decayed[i % 2][:, 1], decayed[i % 2][:, 0]
                for l0 in (0, 4):
                    bank = V.take(pe)
                    for l in range(l0, l0 + 4):
                        lhs, rhs = (k[:, l, :], q[:, l, :]) if l < NL else (
                            hk_ch[:, h, t * P:(t + 1) * P], hq_ch[:, h, t * P:(t + 1) * P])
                        ins = pe.matmul(bank[:, (l - l0) * P:(l - l0 + 1) * P], lhs, rhs, start=True, stop=True)
                    ins.then_inc(V.done, 1)
                if t:
                    bank = V.take(pe)
                    pe.matmul(bank[:, 0:P], k[:, NL + 1, :], q[:, NL, :], start=True, stop=True).then_inc(V.done, 1)

            def read_out(i):
                h, t = divmod(i, TT)
                pe.wait_ge(sem("h_att"), i + 1)
                bank = V.take(pe)
                val = v_h[:, :, h * P:(h + 1) * P]
                ins = pe.matmul(bank[:, 0:P], att[:, 0, i % 2, :], val[:, t, :], start=True, stop=not t)
                if t:
                    ins = pe.matmul(bank[:, 0:P], att[:, 1, i % 2, :], val[:, 0, :], start=False, stop=True)
                ins.then_inc(V.done, 1)

            pe.wait_ge(sem("h_logf"), 1)
            decays(0)
            for i in range(HEADS * TT):
                if i < HEADS * TT - 1:
                    decays(i + 1)
                attend(i)
                if i:
                    read_out(i - 1)
            read_out(HEADS * TT - 1)
            turn_pe(pe, yb, "mixed")
            A.evacuated(pe)
            moving_pe(pe, V)
            moving_pe(pe, V)

        def mix_act(act):
            root_act(TT)
            turn_act(act)
            act.wait_ge(sem("m_gates"), 1)
            a(nc.scalar.activation(t_e, t_ax, ACT.Exp, scale=-1.0))
            nc.scalar.activation(t_l, t_e, ACT.Ln, bias=1.0).then_inc(sem("m_log"), 1)
            act.wait_ge(sem("conv_pad"), 1)
            for c in range(4):
                bank = A.get(act)
                nc.scalar.copy(conv_in[:, 2 * c:2 * c + 2, PAD:], bank[:, :].rearrange("p (j s) -> p j s", j=2)
                               ).then_inc(A.free, 1)
                mark(f"conv_in{c}", A.free, 4 + A.emptied.n)
            for c in range(2):
                bank = A.get(act)
                nc.scalar.activation(hq_ch[:, 2 * c:2 * c + 2, :], bank[:, :].rearrange("p (j s) -> p j s", j=2),
                                     ACT.Silu).then_inc(A.free, 1)
            for t in range(TT):
                bank = A.get(act)
                nc.scalar.activation(f_tok[:, t, :], bank[:, :], ACT.Sigmoid).then_inc(A.free, 1)
            mark("forget", A.free, 4 + A.emptied.n)
            act.wait_ge(sem("lb_diff"), 1)
            nc.scalar.activation(lb, lb, ACT.Sigmoid).then_inc(sem("lb_ready"), 1)
            for t in range(TT):
                bank = A.get(act)
                nc.scalar.activation(mixg[:, t, 0:W1], bank[:, :], ACT.Sigmoid).then_inc(A.free, 1)
            for c in range(8):
                act.wait_ge(sem("conv_done"), c + 1)
                ins = nc.scalar.activation(qk_ch[:, c, :], qk_ch[:, c, :], ACT.Silu, bias=col("conv_b")[:, c:c + 1])
            ins.then_inc(sem("qk_ready"), 1)
            act.wait_ge(sem("hk_ready"), 1)
            nc.scalar.activation(f_tok[:, :, :], f_tok[:, :, :], ACT.Ln).then_inc(sem("h_logf"), 1)
            for t in range(TT):
                bank = A.get(act)
                nc.scalar.copy(hk_ch[:, :, t * P:(t + 1) * P], bank[:, :].rearrange("p (h s) -> p h s", h=HEADS)
                               ).then_inc(A.free, 1)
            for t in range(TT):
                bank = A.get(act)
                nc.scalar.activation(mixg[:, t, W1:], bank[:, :], ACT.Silu).then_inc(A.free, 1)
            act.wait_ge(sem("m_max"), 1)
            for h in range(HEADS):
                nc.scalar.activation(dm[:, h, 0:P], dm[:, h, 0:P], ACT.Exp, bias=t_nm[:, 0, h:h + 1])
                nc.scalar.activation(dm[:, h, P:3 * P], dm[:, h, P:3 * P], ACT.Exp, bias=t_nm[:, 1, h:h + 1]
                                     ).then_inc(sem("m_weights"), 1)
            nc.scalar.activation(t_em, t_nm, ACT.Exp).then_inc(sem("m_weights"), 1)
            for h in range(HEADS):
                bank = A.get(act)
                nc.scalar.copy(sT[:, h % 2, :], bank[:, 0:3 * P]).then_inc(A.free, 1)
            for i in range(HEADS * TT):
                e = decayed[i % 2][:, 0].rearrange("p l s -> p (l s)")
                for a0, b0 in ((0, 512), (512, NL * P)) + (((NL * P, NL * P + 2 * P),) if i % TT else ()):
                    bank = A.get(act)
                    nc.scalar.activation(e[:, a0:b0], bank[:, 0:b0 - a0], ACT.Exp).then_inc(A.free, 1)
                mark(f"decay{i}", A.free, 4 + A.emptied.n)
            root_act(2 * TT * HEADS)
            turn_act(act)
            root_act(TT)

        def mix_dve(dve):
            vec = nc.vector
            modulated_norm_dve(SC2, SH2, "mix")
            vec.memset(conv_in[:, :, 0:PAD], 0.0).then_inc(sem("conv_pad"), 1)
            dve.wait_ge(sem("norms_in"), 16)
            vec.tensor_tensor(lb, norms[:, D:D + W1], norms[:, D + W1:D + 2 * W1], ALU.subtract
                              ).then_inc(sem("lb_diff"), 1)
            bank = V.get(dve)
            vec.tensor_tensor(gate8, bank[:, 0:16].rearrange("p (t g) -> p t g", t=TT),
                              col("gate_b").unsqueeze(1).broadcast_to([P, TT, 8]), ALU.add).then_inc(V.free, 1)
            V.through(dve)
            vec.scalar_tensor_tensor(t_ax, gate8[:, :, HEADS:], -1.0, gate8[:, :, HEADS:], ALU.mult, ALU.max).then_inc(sem("m_gates"), 1)
            dve.wait_ge(sem("m_log"), 1)
            vec.scalar_tensor_tensor(t_lf, gate8[:, :, HEADS:], 0.0, t_l, ALU.min, ALU.subtract
                                     ).then_inc(sem("m_logf"), 1)
            for c in range(8):
                if c % 2 == 0:
                    await_mark(dve, f"conv_in{c // 2}")
                w = lambda j: col("conv_w")[:, j * 8 + c:j * 8 + c + 1]
                v(vec.tensor_scalar(qk_ch[:, c, :], conv_in[:, c, 0:S], w(0), None, ALU.mult))
                for j in (1, 2):
                    v(vec.scalar_tensor_tensor(qk_ch[:, c, :], conv_in[:, c, j:j + S], w(j), qk_ch[:, c, :],
                                               ALU.mult, ALU.add))
                vec.scalar_tensor_tensor(qk_ch[:, c, :], conv_in[:, c, 3:3 + S], w(3), qk_ch[:, c, :],
                                         ALU.mult, ALU.add).then_inc(sem("conv_done"), 1)
            bank = V.get(dve)
            vec.tensor_copy(t_b, bank[:, 0:8].rearrange("p (t h) -> p t h", t=TT)).then_inc(V.free, 1)
            V.through(dve)
            vec.tensor_tensor(t_x, gate8[:, :, 0:HEADS], t_b, ALU.subtract).then_inc(sem("m_x"), 1)
            dve.wait_ge(sem("lb_ready"), 1)
            v(vec.tensor_scalar(one_lb, lb, -1.0, 1.0, ALU.mult, ALU.add))
            await_mark(dve, "forget")
            wide = lambda r: r.unsqueeze(1).broadcast_to([P, TT, W1])
            v(vec.tensor_tensor(f_tok, f_tok, wide(one_lb), ALU.mult))
            v(vec.tensor_tensor(f_tok, f_tok, wide(lb), ALU.add))
            vec.tensor_scalar(hk_tok, f_tok, -1.0, 1.0, ALU.mult, ALU.add).then_inc(sem("hk_ready"), 1)
            for t in range(TT):
                bank = V.get(dve)
                vec.tensor_copy(v_m[:, t, :], bank[:, :]).then_inc(V.free, 1)
            for h in range(0, HEADS, 2):
                bank = V.get(dve)
                for j in range(2):
                    x, b, d = bank[:, j * S:(j + 1) * S], t_b[:, :, h + j], dm[:, h + j, :]
                    vec.scalar_tensor_tensor(d[:, 0:P], x[:, 0:P], b[:, 0:1], cst("causal"), ALU.add, ALU.add)
                    vec.tensor_scalar(d[:, P:2 * P], x[:, 0:P], b[:, 1:2], None, ALU.add)
                    ins = vec.scalar_tensor_tensor(d[:, 2 * P:3 * P], x[:, P:S], b[:, 1:2], cst("causal"),
                                                   ALU.add, ALU.add)
                ins.then_inc(V.free, 1)
            V.through(dve)
            vec.tensor_reduce(t_m[:, 0, :], dm[:, :, 0:P], AX_X, ALU.max)
            v(vec.tensor_reduce(t_m[:, 1, :], dm[:, :, P:3 * P], AX_X, ALU.max))
            vec.tensor_scalar(t_nm, t_m, -1.0, None, ALU.mult).then_inc(sem("m_max"), 1)
            for t in range(TT):
                bank = V.get(dve)
                vec.tensor_copy(v_h[:, t, :], bank[:, :]).then_inc(V.free, 1)
            for what, h in M_SEQ:
                if what == "S":
                    bank = V.get(dve)
                    dve.wait_ge(sem("m_weights"), h + 1)
                    for t, a0, b0 in ((0, 0, P), (1, P, 3 * P)):
                        ins = vec.tensor_tensor_reduce(dm[:, h, a0:b0], bank[:, a0:b0], dm[:, h, a0:b0],
                                                       float(P) ** -0.5, 0.0, ALU.mult, ALU.add, t_den[:, t, h:h + 1])
                        if t == 0:
                            v(ins)
                    ins.then_inc(sem("m_scores"), 1)
                    dve.wait_ge(sem("m_scores"), h + 1)
                    vec.memset(tiny[:, 500:501], 0.0).then_inc(V.free, 1)
                if what == "N":
                    if h == 0:
                        pass
                    v(vec.scalar_tensor_tensor(t_rec[:, :, h], t_den[:, :, h], -1.0, t_den[:, :, h], ALU.mult, ALU.max))
                    if h == 0:
                        dve.wait_ge(sem("m_weights"), HEADS + 1)
                    v(vec.tensor_tensor(t_rec[:, :, h], t_rec[:, :, h], t_em[:, :, h], ALU.max))
                    v(vec.reciprocal(t_rec[:, :, h], t_rec[:, :, h]))
                    bank = V.get(dve)
                    for t in range(TT):
                        ins = vec.tensor_scalar(yb[:, t, h * P:(h + 1) * P], bank[:, t * P:(t + 1) * P],
                                                t_rec[:, t, h:h + 1], None, ALU.mult)
                    ins.then_inc(V.free, 1)

            def decay(i):
                h, t = divmod(i, TT)
                await_mark(dve, f"decay{i}")
                e, q = decayed[i % 2][:, 0], decayed[i % 2][:, 1]
                at = slice(t * P, (t + 1) * P)
                v(vec.tensor_tensor(q[:, 0:NL + t, :], e[:, 0:NL + t, :],
                                    hq_ch[:, h, at].unsqueeze(1).broadcast_to([P, NL + t, P]), ALU.mult))
                ins = vec.tensor_tensor(e[:, 0:NL, :], e[:, 0:NL, :],
                                        hk_ch[:, h, at].unsqueeze(1).broadcast_to([P, NL, P]), ALU.mult)
                if t:
                    ins = vec.tensor_tensor(e[:, NL + 1, :], e[:, NL + 1, :], hk_ch[:, h, 0:P], ALU.mult)
                ins.then_inc(sem("h_decayed"), 1)

            def mask(i):
                for l0 in (0, 4):
                    bank = V.get(dve)
                    vec.tensor_tensor(masked[:, l0:l0 + 4, :], bank[:, :].rearrange("p (l s) -> p l s", s=P),
                                      cst("keep").rearrange("p (l s) -> p l s", s=P)[:, l0:l0 + 4, :],
                                      ALU.mult).then_inc(V.free, 1)
                if i % TT:
                    bank = V.get(dve)
                    vec.tensor_copy(att[:, 1, i % 2, :], bank[:, 0:P]).then_inc(V.free, 1)
                V.through(dve)
                vec.tensor_reduce(att[:, 0, i % 2, :], masked.rearrange("p l s -> p s l"), AX_X, ALU.add
                                  ).then_inc(sem("h_att"), 1)
                dve.wait_ge(sem("h_att"), i + 1)

            def take_out(i):
                h, t = divmod(i, TT)
                bank = V.get(dve)
                vec.tensor_copy(yb[:, t, W1 + h * P:W1 + (h + 1) * P], bank[:, 0:P]).then_inc(V.free, 1)

            decay(0)
            for i in range(HEADS * TT):
                if i < HEADS * TT - 1:
                    decay(i + 1)
                mask(i)
                if i:
                    take_out(i - 1)
            take_out(HEADS * TT - 1)
            V.through(dve)
            n = TT * 2 * HEADS
            squares = arena2[:, 0:2048].rearrange("p (t h w) -> p t h w", t=TT, h=2 * HEADS)
            by_head = yb[:, :, :].rearrange("p t (h w) -> p t h w", w=P)
            v(vec.tensor_tensor(squares, by_head, by_head, ALU.mult))
            v(vec.tensor_reduce(small[:, 128:128 + n].rearrange("p (t h) -> p t h", t=TT), squares, AX_X, ALU.add))
            rstd_dve(small[:, 160:160 + n], small[:, 128:128 + n], n, 1.0 / P, EPS)
            for t in range(TT):
                v(vec.tensor_tensor(by_head[:, t], by_head[:, t],
                                    small[:, 160 + t * 8:168 + t * 8].unsqueeze(2).broadcast_to([P, 8, P]), ALU.mult))
                v(vec.tensor_tensor(yb[:, t, :], yb[:, t, :], norms[:, 0:D], ALU.mult))
                vec.tensor_tensor(yb[:, t, :], yb[:, t, :], mixg[:, t, :], ALU.mult).then_inc(sem("y_mixed"), 1)
            for n in range(2):
                for t in range(TT):
                    bank = V.get(dve)
                    vec.tensor_copy(yb[:, t, n * 512:(n + 1) * 512], bank[:, :]).then_inc(V.free, 1)
            V.through(dve)
            add_residual_dve(G2)

        U = lambda arena, i, n=1: arena[:, i * D:(i + n) * D]
        C4 = lambda x: x.rearrange("p (q s) -> p q s", q=PAIRS)
        gates2 = U(arena1, 0, 4).rearrange("p (t w) -> p t w", t=TT)
        fqk = U(arena1, 4, 2).rearrange("p (c s) -> p c s", s=S)
        fv = U(arena1, 6).rearrange("p (t w) -> p t w", t=TT)
        yf, yr = C4(U(arena1, 7)), C4(U(arena1, 8))
        fdm = arena2[:, 0:FOX_H * 384].rearrange("p (h s) -> p h s", h=FOX_H)
        fsT = arena2[:, 3072:3072 + 4 * 384].rearrange("p (b s) -> p b s", b=4)
        raw = arena3[:, 0:14 * (S + 1)].rearrange("p (c s) -> p c s", c=14)
        shifted = arena4[:, 0:14 * S].rearrange("p (c s) -> p c s", s=S)
        r_c, k_c, v_c = shifted[:, 0:4], shifted[:, 4:8], shifted[:, 8:12]
        wa, gl = shifted[:, 12], shifted[:, 13]
        lora = U(arena4, 4)
        lw, cs, cb, kk, ai, bonus, g_c = [C4(U(arena5, i)) for i in range(7)]
        kap, bet, kh, rh = lw, cb, kk, r_c
        ec, tmp = C4(U(arena3, 0)), C4(U(arena3, 1))
        f8 = tiny[:, 128:144].rearrange("p (t g) -> p t g", t=TT)
        f_ax, f_e, f_l, f_lf, f_b, f_x, f_nm, f_den, f_rec = [
            tiny[:, 144 + 16 * i:160 + 16 * i].rearrange("p (t h) -> p t h", t=TT) for i in range(9)]
        f_m = tiny[:, 304:320].rearrange("p (t h) -> p t h", t=TT)
        GRP = 4

        def m4(arena, i, n, at=0):
            return arena[:, i * D + at:i * D + at + GRP * n].rearrange("p (c n) -> p c n", c=GRP)

        LC, BD = m4(arena2, 0, 128), m4(arena2, 0, 128, 512)
        powers = [m4(arena2, 1, 128), m4(arena2, 1, 128, 512), m4(arena2, 2, 128), m4(arena2, 2, 128, 512)]
        v_st, bet_st, kh_st = [m4(arena2, 3, 64, 256 * i) for i in range(3)]
        X = [m4(arena2, 4, 128), m4(arena2, 4, 128, 512)]

        def blocks4(arena, i):
            return U(arena, i).rearrange("p (c q n) -> p c q n", c=GRP, q=PAIRS)

        v_bd, bet_bd, u_bd, GT = blocks4(arena2, 5), blocks4(arena1, 4), blocks4(arena1, 5), blocks4(arena1, 6)
        Qp = m4(arena3, 2, 64)
        state = [arena3[:, 2304 + 256 * i:2560 + 256 * i].rearrange("p (q n) -> p q n", q=PAIRS) for i in range(2)]
        PAR = [slice(0, DH), slice(DH, P)]
        F_STEPS = FOX_H + 2

        def fox_pe(pe):
            for s in range(F_STEPS):
                if s < FOX_H:
                    par, h = PAR[s % 2], s // 2
                    q, k = fqk[par, h, :], fqk[par, 4 + h, :]
                    bank = V.take(pe)
                    pe.matmul(bank[:, 0:P], q[:, 0:P], k[:, 0:P], start=True, stop=True)
                    pe.matmul(bank[:, P:3 * P], q[:, P:S], k, start=True, stop=True).then_inc(V.done, 1)
                if 1 <= s <= FOX_H:
                    pe.wait_ge(sem("fox_probs"), s)
                    bank = A.take(pe)
                    for j in range(3):
                        ins = pe.transpose(bank[:, j * P:(j + 1) * P], fdm[:, s - 1, j * P:(j + 1) * P], ident)
                    ins.then_inc(A.done, 1)
                if s >= 3 and s % 2:
                    A.evacuated(pe)
                    bank = V.take(pe)
                    for h in (s - 3, s - 2):
                        par, w, val = PAR[h % 2], fsT[:, h % 4, :], fv[:, :, h * DH:(h + 1) * DH]
                        pe.matmul(bank[par, 0:P], val[:, 0, :], w[:, 0:P], start=True, stop=True)
                        pe.matmul(bank[par, P:S], val[:, 0, :], w[:, P:2 * P], start=True, stop=False)
                        ins = pe.matmul(bank[par, P:S], val[:, 1, :], w[:, 2 * P:3 * P], start=False, stop=True)
                    ins.then_inc(V.done, 1)

        def fox_act(act):
            for s in range(F_STEPS):
                if s < FOX_H:
                    act.wait_ge(sem("fox_max"), s + 1)
                    for t, a0, b0 in ((0, 0, P), (1, P, 3 * P)):
                        ins = nc.scalar.activation(fdm[:, s, a0:b0], fdm[:, s, a0:b0], ACT.Exp,
                                                   bias=f_nm[:, t, s:s + 1], accum_out=f_den[:, t, s:s + 1])
                    ins.then_inc(sem("fox_exp"), 1)
                if 1 <= s <= FOX_H:
                    bank = A.get(act)
                    nc.scalar.copy(fsT[:, (s - 1) % 4, :], bank[:, 0:3 * P]).then_inc(A.free, 1)

        def fox_dve(dve):
            vec = nc.vector
            for s in range(F_STEPS):
                if s < FOX_H:
                    bank = V.get(dve)
                    vec.scalar_tensor_tensor(fdm[:, s, :], bank[:, 0:3 * P], DH ** -0.5, fdm[:, s, :],
                                             ALU.mult, ALU.add).then_inc(V.free, 1)
                    V.through(dve)
                    vec.tensor_reduce(f_m[:, 0, s:s + 1], fdm[:, s, 0:P], AX_X, ALU.max)
                    v(vec.tensor_reduce(f_m[:, 1, s:s + 1], fdm[:, s, P:3 * P], AX_X, ALU.max))
                    vec.tensor_scalar(f_nm[:, :, s], f_m[:, :, s], -1.0, None, ALU.mult).then_inc(sem("fox_max"), 1)
                if 1 <= s <= FOX_H:
                    dve.wait_ge(sem("fox_exp"), s)
                    v(vec.reciprocal(f_rec[:, :, s - 1], f_den[:, :, s - 1]))
                    for t, a0, b0 in ((0, 0, P), (1, P, 3 * P)):
                        ins = vec.tensor_scalar(fdm[:, s - 1, a0:b0], fdm[:, s - 1, a0:b0],
                                                f_rec[:, t, s - 1:s], None, ALU.mult)
                    ins.then_inc(sem("fox_probs"), 1)
                if s >= 3 and s % 2:
                    bank = V.get(dve)
                    vec.tensor_copy(yf[:, (s - 3) // 2, :], bank[:, 0:S]).then_inc(V.free, 1)

        def par_sums_pe(pe, queue, src):
            for i in range(2):
                bank = queue.take(pe)
                pe.matmul(bank[:, :], cst("par_ones"), src[:, 2 * i:2 * i + 2, :], start=True,
                          stop=True).then_inc(queue.done, 1)

        def half(x, i):
            return x[:, 2 * i:2 * i + 2, :]

        def two(bank):
            return bank[:, :].rearrange("p (j s) -> p j s", j=2)

        by_chunk = lambda x: x.rearrange("p q s -> p (q s)").rearrange("p (c n) -> p c n", c=NCH)
        kap_n, bet_n, kh_n, v_n = by_chunk(kap), by_chunk(bet), by_chunk(kh), by_chunk(C4(arena3[:, 3072:4096]))

        def chunk_out(x):
            return x.rearrange("p c (q s) -> p q c s", q=PAIRS)

        def chunk_in(x):
            return x.rearrange("p q (c s) -> p q c s", s=CH)

        def chunk_ap(x, c, par):
            return x[par, :, c * CH:(c + 1) * CH] if x is rh else x[par, c, :]

        def four_chunks_pe(pe, g):
            cc = range(GRP)
            both = [(c, par) for c in cc for par in PAR]
            for pair in ((kap_n, bet_n), (kh_n, v_n)):
                bank = A.take(pe)
                for i, x in enumerate(pair):
                    for c, par in both:
                        ins = pe.matmul(bank[par, i * 256 + c * DH:i * 256 + (c + 1) * DH],
                                        chunk_ap(x, g * GRP + c, par), cst("id64")[par, :], start=True, stop=True)
                ins.then_inc(A.done, 1)
            for key in (bet_n, kh_n):
                bank = V.take(pe)
                for c, par in both:
                    for i, x in enumerate((kap_n, rh)):
                        ins = pe.matmul(bank[par, c * P + i * DH:c * P + (i + 1) * DH],
                                        chunk_ap(key, g * GRP + c, par), chunk_ap(x, g * GRP + c, par),
                                        start=True, stop=True)
                ins.then_inc(V.done, 1)
            bank = V.take(pe)
            for c, par in both:
                ins = pe.matmul(bank[par, c * DH:(c + 1) * DH], chunk_ap(kap_n, g * GRP + c, par),
                                chunk_ap(bet_n, g * GRP + c, par), start=True, stop=True)
            ins.then_inc(V.done, 1)
            A.evacuated(pe)
            V.evacuated(pe)
            bank = V.take(pe)
            for c, par in both:
                ins = pe.matmul(bank[par, c * DH:(c + 1) * DH], BD[par, c, 0:DH], v_st[par, c, :], start=True, stop=True)
            ins.then_inc(V.done, 1)
            for step in range(4):
                left = LC[:, :, 0:DH] if step == 0 else powers[step][:, :, DH:P]
                right = powers[step][:, :, 0:DH]
                if step < 3:
                    bank = A.take(pe)
                    for c, par in both:
                        ins = pe.matmul(bank[par, c * P:c * P + DH], left[par, c, :], right[par, c, :],
                                        start=True, stop=True)
                        ins = pe.matmul(bank[par, c * P + DH:(c + 1) * P], right[par, c, :], left[par, c, :],
                                        start=True, stop=True)
                    ins.then_inc(A.done, 1)
                V.evacuated(pe)
                bank = V.take(pe)
                for c, par in both:
                    ins = pe.matmul(bank[par, c * P:(c + 1) * P], left[par, c, :], X[step % 2][par, c, :],
                                    start=True, stop=True)
                ins.then_inc(V.done, 1)
                A.evacuated(pe)
            V.evacuated(pe)
            w, u = X[0][:, :, 0:DH], X[0][:, :, DH:P]
            for c0 in (0, 2):
                bank = V.take(pe)
                for c, par in both:
                    if c0 <= c < c0 + 2:
                        ins = pe.matmul(bank[par, (c - c0) * 256:(c - c0 + 1) * 256], w[par, c, :], bet_bd[par, c],
                                        start=True, stop=True)
                ins.then_inc(V.done, 1)
            bank = V.take(pe)
            for c, par in both:
                ins = pe.matmul(bank[par, c * DH:(c + 1) * DH], w[par, c, :], LC[par, c, DH:P], start=True, stop=True)
            ins.then_inc(V.done, 1)
            y_bank = A.take(pe)
            pe.wait_ge(sem("u_blocks"), g + 1)
            for c in cc:
                n = g * GRP + c
                old = state[n % 2]
                if n < NCH - 1:
                    bank = V.take(pe)
                    for par in PAR:
                        pe.matmul(bank[par, 0:256], kh_st[par, c, :], v_bd[par, c], start=True, stop=False)
                        ins = pe.matmul(bank[par, 0:256], bet_st[par, c, :], u_bd[par, c], start=False, stop=(n == 0))
                    if n:
                        V.evacuated_but(pe, 1)
                        for q in range(PAIRS):
                            for par in PAR:
                                ins = pe.matmul(bank[par, q * DH:(q + 1) * DH], GT[par, c, q, :], old[par, q, :],
                                                start=False, stop=(q == PAIRS - 1))
                    ins.then_inc(V.done, 1)
                else:
                    V.evacuated(pe)
                if n == 0:
                    V.evacuated_but(pe, 1)
                for par in PAR:
                    out_c = y_bank[par, c * DH:(c + 1) * DH]
                    pe.matmul(out_c, v_st[par, c, :], BD[par, c, DH:P], start=True, stop=False)
                    ins = pe.matmul(out_c, u[par, c, :], LC[par, c, DH:P], start=False, stop=(n == 0))
                    if n:
                        for q in range(PAIRS):
                            ins = pe.matmul(y_bank[par, c * DH + q * CH:c * DH + (q + 1) * CH], old[par, q, :],
                                            Qp[par, c, q * CH:(q + 1) * CH], start=False, stop=(q == PAIRS - 1))
            ins.then_inc(A.done, 1)

        def four_chunks_act(act, g):
            copy = nc.scalar.copy
            quad = lambda x: x.rearrange("p (c n) -> p c n", c=GRP)
            for dst in ((X[0][:, :, 0:DH], bet_st), (kh_st, v_st)):
                bank = A.get(act)
                copy(dst[0], quad(bank[:, 0:256]))
                copy(dst[1], quad(bank[:, 256:512])).then_inc(A.free, 1)
            mark(f"by_token{g}", A.free, 4 + A.emptied.n)
            for step in range(3):
                bank = A.get(act)
                copy(powers[step + 1], quad(bank[:, :])).then_inc(A.free, 1)
            bank = A.get(act)
            to = yr[:, :, g * GRP * CH:(g + 1) * GRP * CH].rearrange("p q (c s) -> p c q s", c=GRP)
            copy(to, bank[:, 0:256].rearrange("p (c q s) -> p c q s", c=GRP, q=PAIRS)).then_inc(A.free, 1)
            mark(f"y_chunks{g}", A.free, 4 + A.emptied.n)

        def four_chunks_dve(dve, g):
            vec = nc.vector
            quad = lambda x: x.rearrange("p (c n) -> p c n", c=GRP)
            mask = cst("s_t").unsqueeze(1).broadcast_to([P, GRP, P])
            for dst in (LC, BD):
                bank = V.get(dve)
                vec.tensor_tensor(dst, quad(bank[:, :]), mask, ALU.mult).then_inc(V.free, 1)
            bank = V.get(dve)
            vec.tensor_tensor(powers[0][:, :, 0:DH], quad(bank[:, 0:256]),
                              cst("t_s").unsqueeze(1).broadcast_to([P, GRP, DH]), ALU.mult).then_inc(V.free, 1)
            pairs = cst("pairs").unsqueeze(1).unsqueeze(3).broadcast_to([P, GRP, PAIRS, DH])

            def expand(dst, src):
                return vec.tensor_tensor(dst, src.unsqueeze(2).broadcast_to([P, GRP, PAIRS, DH]), pairs, ALU.mult)

            await_mark(dve, f"by_token{g}")
            bank = V.get(dve)
            vec.tensor_copy(X[0][:, :, DH:P], quad(bank[:, 0:256])).then_inc(V.free, 1)
            expand(v_bd, v_st)
            expand(bet_bd, bet_st)
            V.through(dve)
            for step in range(4):
                bank = V.get(dve)
                vec.tensor_tensor(X[(step + 1) % 2], X[step % 2], quad(bank[:, :]), ALU.add).then_inc(V.free, 1)
                V.through(dve)
            expand(u_bd, X[0][:, :, DH:P]).then_inc(sem("u_blocks"), 1)
            for c0 in (0, 2):
                bank = V.get(dve)
                vec.tensor_tensor(GT[:, c0:c0 + 2].rearrange("p c q n -> p (c q) n"),
                                  bank[:, :].rearrange("p (m n) -> p m n", n=DH),
                                  cst("id64").unsqueeze(1).broadcast_to([P, 8, DH]), ALU.add).then_inc(V.free, 1)
            bank = V.get(dve)
            r = rh[:, :, g * GRP * CH:(g + 1) * GRP * CH].rearrange("p q (c s) -> p c q s", c=GRP)
            vec.tensor_tensor(Qp.rearrange("p c (q s) -> p c q s", q=PAIRS),
                              bank[:, 0:256].rearrange("p (c q s) -> p c q s", c=GRP, q=PAIRS), r,
                              ALU.add).then_inc(V.free, 1)
            for c in range(GRP):
                n = g * GRP + c
                if n < NCH - 1:
                    bank = V.get(dve)
                    last = ec[:, :, n * CH + CH - 1:n * CH + CH].broadcast_to([P, PAIRS, DH])
                    vec.tensor_tensor(state[(n + 1) % 2], bank[:, 0:256].rearrange("p (q n) -> p q n", q=PAIRS),
                                      last, ALU.mult).then_inc(V.free, 1)

        def mix2_pe(pe):
            turn_pe(pe, yb, "mix2")
            A.evacuated(pe)
            narrow_pe(pe, col("w_fox"), FOX_H)
            for _ in range(11):
                staying_pe(pe, A)
            moving_pe(pe, V)
            cumulate_pe(pe, "f_logf", f_lf, FOX_H)
            moving_pe(pe, A)
            moving_pe(pe, A)
            rows_pe(pe, "f_x", f_x, FOX_H)
            pe.wait_ge(sem("lora_in"), 16)
            pe.wait_ge(sem("low_rank"), 1)
            for rows, rhs, at in ((PAR[0], wa, 0), (PAR[1], wa, 0), (slice(0, P), gl, 512)):
                for i in range(2):
                    bank = A.take(pe)
                    for j in range(2):
                        a0 = at + (2 * i + j) * P
                        ins = pe.matmul(bank[:, j * S:(j + 1) * S], lora[rows, a0:a0 + P], rhs[rows, :],
                                        start=True, stop=True)
                    ins.then_inc(A.done, 1)
            moving_pe(pe, A)
            moving_pe(pe, A)
            pe.wait_ge(sem("rw_squares"), 1)
            par_sums_pe(pe, A, tmp)
            pe.wait_ge(sem("rw_bonus"), 1)
            par_sums_pe(pe, V, bonus)
            fox_pe(pe)
            V.evacuated(pe)
            for _ in range(2):
                moving_pe(pe, V, k_tiles=4, src=yf)
            pe.wait_ge(sem("rw_ready"), 1)
            for g in range(NCH // GRP):
                four_chunks_pe(pe, g)
            A.evacuated(pe)
            par_sums_pe(pe, V, yr)
            pe.wait_ge(sem("rw_var"), 1)
            par_sums_pe(pe, A, tmp)
            pe.wait_ge(sem("rw_out"), 1)
            for _ in range(2):
                moving_pe(pe, V, k_tiles=4, src=yr)
            turn_pe(pe, yb, "merged")
            A.evacuated(pe)
            moving_pe(pe, V)
            moving_pe(pe, V)

        def mix2_act(act):
            turn_act(act)
            act.dma_start(lora, dram["lora"]).then_inc(sem("lora_in"), 16)
            act.wait_ge(sem("f_gates"), 1)
            a(nc.scalar.activation(f_e, f_ax, ACT.Exp, scale=-1.0))
            nc.scalar.activation(f_l, f_e, ACT.Ln, bias=1.0).then_inc(sem("f_log"), 1)
            for c in range(4):
                bank = A.get(act)
                nc.scalar.copy(half(fqk, c), two(bank)).then_inc(A.free, 1)
            for c in range(7):
                bank = A.get(act)
                nc.scalar.copy(raw[:, 2 * c:2 * c + 2, 1:], two(bank)).then_inc(A.free, 1)
            mark("raw", A.free, 4 + A.emptied.n)
            for n in range(2):
                for t in range(TT):
                    bank = A.get(act)
                    nc.scalar.activation(gates2[:, t, n * 512:(n + 1) * 512], bank[:, :], ACT.Sigmoid).then_inc(A.free, 1)
            act.wait_ge(sem("shifted"), 1)
            nc.scalar.activation(wa[0:DH, :], wa[0:DH, :], ACT.Tanh)
            nc.scalar.activation(gl, gl, ACT.Sigmoid).then_inc(sem("low_rank"), 1)
            for dst, bias in ((lw, "w0"), (ai, "a0")):
                for i in range(2):
                    bank = A.get(act)
                    for j in range(2):
                        ins = nc.scalar.activation(dst[:, 2 * i + j, :], bank[:, j * S:(j + 1) * S], ACT.Sigmoid,
                                                   bias=col(bias)[:, 2 * i + j:2 * i + j + 1])
                    ins.then_inc(A.free, 1)
            mark("decay_and_a", A.free, 4 + A.emptied.n)
            for i in range(2):
                bank = A.get(act)
                nc.scalar.copy(half(g_c, i), two(bank)).then_inc(A.free, 1)
            for n in range(2, 4):
                for t in range(TT):
                    bank = A.get(act)
                    nc.scalar.activation(gates2[:, t, n * 512:(n + 1) * 512], bank[:, :], ACT.Sigmoid).then_inc(A.free, 1)
            for i in range(2):
                bank = A.get(act)
                nc.scalar.activation(half(tmp, i), two(bank), ACT.Sqrt).then_inc(A.free, 1)
            mark("norms", A.free, 4 + A.emptied.n)
            act.wait_ge(sem("rw_sums"), 1)
            a(nc.scalar.activation(ec, cs, ACT.Exp))
            nc.scalar.activation(cb, cb, ACT.Exp)
            nc.scalar.activation(cs, cs, ACT.Exp, scale=-1.0).then_inc(sem("rw_exps"), 1)
            fox_act(act)
            for g in range(NCH // GRP):
                four_chunks_act(act, g)
            act.wait_ge(sem("gn_eps"), 1)
            for i in range(2):
                bank = A.get(act)
                nc.scalar.activation(half(tmp, i), two(bank), ACT.Sqrt, bias=small[:, 503:504], scale=1.0 / DH
                                     ).then_inc(A.free, 1)
            mark("deviations", A.free, 4 + A.emptied.n)
            turn_act(act)
            act.wait_ge(sem("rw_out"), 1)
            act.dma_start(arena2[:, 0:2 * D], dram["lns"][0:2 * D].partition_broadcast(P)).then_inc(sem("lns_in"), 16)
            root_act(TT)

        lns = arena2[:, 0:2 * D].rearrange("p (m d) -> p m d", m=2)

        def layer_norm_dve(gain, shift, tag):
            vec = nc.vector
            v(vec.scalar_tensor_tensor(xh[:, :, :], xh[:, :, :], ALPHA, yb[:, :, :], ALU.mult, ALU.add))
            v(vec.tensor_reduce(small[:, 140:142], xh[:, :, :], AX_X, ALU.add))
            v(vec.tensor_scalar(small[:, 142:144], small[:, 140:142], -1.0 / D, None, ALU.mult))
            for t in range(TT):
                ins = vec.tensor_scalar(xh[:, t, :], xh[:, t, :], small[:, 142 + t:143 + t], None, ALU.add)
            v(ins)
            for t in range(TT):
                ins = vec.tensor_tensor_reduce(yb[:, t, :], xh[:, t, :], xh[:, t, :], 1.0, 0.0,
                                               ALU.mult, ALU.add, small[:, 128 + t:129 + t])
            v(ins)
            rstd_dve(small[:, 130:132], small[:, 128:130], TT, 1.0 / D, LN_EPS)
            for t in range(TT):
                v(vec.scalar_tensor_tensor(xh[:, t, :], xh[:, t, :], small[:, 130 + t:131 + t], gain,
                                           ALU.mult, ALU.mult))
                vec.tensor_tensor(xh[:, t, :], xh[:, t, :], shift, ALU.add).then_inc(sem(f"y_{tag}"), 1)
            nc.vector.wait_ge(sem(f"y_{tag}"), TT)

        def mix2_dve(dve):
            vec = nc.vector
            for t in range(TT):
                vec.tensor_copy(yb[:, t, :], xh[:, t, :]).then_inc(sem("y_mix2"), 1)
            vec.memset(raw[:, :, 0:1], 0.0)
            vec.memset(small[:, 503:504], GN_EPS).then_inc(sem("gn_eps"), 1)
            bank = V.get(dve)
            vec.tensor_tensor(f8, bank[:, 0:16].rearrange("p (t g) -> p t g", t=TT),
                              col("fox_b").unsqueeze(1).broadcast_to([P, TT, 8]), ALU.add).then_inc(V.free, 1)
            V.through(dve)
            vec.scalar_tensor_tensor(f_ax, f8, -1.0, f8, ALU.mult, ALU.max).then_inc(sem("f_gates"), 1)
            dve.wait_ge(sem("f_log"), 1)
            vec.scalar_tensor_tensor(f_lf, f8, 0.0, f_l, ALU.min, ALU.subtract).then_inc(sem("f_logf"), 1)
            await_mark(dve, "raw")
            v(vec.tensor_tensor(shifted, raw[:, :, 0:S], raw[:, :, 1:], ALU.subtract))
            for c in range(13, -1, -1):
                ins = vec.scalar_tensor_tensor(shifted[:, c, :], shifted[:, c, :], col("mu")[:, c:c + 1],
                                               raw[:, c, 1:], ALU.mult, ALU.add)
                if c == 12:
                    ins.then_inc(sem("shifted"), 1)
            v(ins)
            for t in range(TT):
                bank = V.get(dve)
                vec.tensor_copy(fv[:, t, :], bank[:, :]).then_inc(V.free, 1)
            bank = V.get(dve)
            vec.tensor_copy(f_b, bank[:, 0:16].rearrange("p (t h) -> p t h", t=TT)).then_inc(V.free, 1)
            V.through(dve)
            vec.tensor_scalar(f_x, f_b, -1.0, None, ALU.mult).then_inc(sem("f_x"), 1)
            for q in range(PAIRS):
                ins = vec.tensor_scalar(kk[:, q, :], k_c[:, q, :], col("k_k")[:, q:q + 1], None, ALU.mult)
            v(ins)
            vec.tensor_tensor(tmp, kk, kk, ALU.mult).then_inc(sem("rw_squares"), 1)
            for h in range(0, FOX_H, 2):
                bank = V.get(dve)
                for j in range(2):
                    x, b, d = bank[:, j * S:(j + 1) * S], f_b[:, :, h + j], fdm[:, h + j, :]
                    vec.scalar_tensor_tensor(d[:, 0:P], x[:, 0:P], b[:, 0:1], cst("causal"), ALU.add, ALU.add)
                    vec.tensor_scalar(d[:, P:2 * P], x[:, 0:P], b[:, 1:2], None, ALU.add)
                    ins = vec.scalar_tensor_tensor(d[:, 2 * P:3 * P], x[:, P:S], b[:, 1:2], cst("causal"),
                                                   ALU.add, ALU.add)
                ins.then_inc(V.free, 1)
            V.through(dve)
            await_mark(dve, "decay_and_a")
            v(vec.tensor_scalar(lw, lw, -float(np.exp(-0.5)), None, ALU.mult))
            for q in range(PAIRS):
                ins = vec.tensor_tensor_scan(cs[:, q, :], cst("starts"), lw[:, q, :], 0.0, ALU.mult, ALU.add)
            v(ins)
            vec.tensor_tensor(cb, cs, lw, ALU.subtract).then_inc(sem("rw_sums"), 1)
            await_mark(dve, "norms")
            v(vec.tensor_scalar(tmp, tmp, 1e-12, None, ALU.max))
            v(vec.reciprocal(tmp, tmp))
            v(vec.tensor_tensor(kk, kk, tmp, ALU.mult))
            for q in range(PAIRS):
                ins = vec.tensor_scalar(tmp[:, q, :], ai[:, q, :], -1.0, col("k_a")[:, q:q + 1], ALU.add, ALU.mult)
            v(ins)
            v(vec.scalar_tensor_tensor(k_c, tmp, 1.0, k_c, ALU.add, ALU.mult))
            v(vec.tensor_tensor(bonus, r_c, k_c, ALU.mult))
            for q in range(PAIRS):
                ins = vec.tensor_scalar(bonus[:, q, :], bonus[:, q, :], col("r_k")[:, q:q + 1], None, ALU.mult)
            ins.then_inc(sem("rw_bonus"), 1)
            v(vec.scalar_tensor_tensor(ai, ai, -1.0, kk, ALU.mult, ALU.mult))
            dve.wait_ge(sem("rw_exps"), 1)
            v(vec.tensor_tensor(chunk_out(kap_n), chunk_in(kk), chunk_in(cb), ALU.mult))
            vec.tensor_tensor(chunk_out(bet_n), chunk_in(ai), chunk_in(cs), ALU.mult)
            vec.tensor_tensor(chunk_out(kh_n), chunk_in(k_c), chunk_in(cs), ALU.mult)
            vec.tensor_copy(chunk_out(v_n), chunk_in(v_c))
            vec.tensor_tensor(rh, r_c, ec, ALU.mult).then_inc(sem("rw_ready"), 1)
            for i in range(2):
                bank = V.get(dve)
                vec.tensor_tensor(half(bonus, i), half(v_c, i), two(bank), ALU.mult).then_inc(V.free, 1)
            fox_dve(dve)
            for n in range(2):
                for t in range(TT):
                    bank = V.get(dve)
                    at = slice(n * 512, (n + 1) * 512)
                    vec.tensor_tensor(yb[:, t, at], gates2[:, t, at], bank[:, :], ALU.mult).then_inc(V.free, 1)
            for g in range(NCH // GRP):
                four_chunks_dve(dve, g)
            await_mark(dve, f"y_chunks{NCH // GRP - 1}")
            for i in range(2):
                bank = V.get(dve)
                vec.scalar_tensor_tensor(half(yr, i), two(bank), -1.0 / DH, half(yr, i), ALU.mult, ALU.add
                                         ).then_inc(V.free, 1)
            V.through(dve)
            vec.tensor_tensor(tmp, yr, yr, ALU.mult).then_inc(sem("rw_var"), 1)
            await_mark(dve, "deviations")
            v(vec.reciprocal(tmp, tmp))
            v(vec.tensor_tensor(yr, yr, tmp, ALU.mult))
            for q in range(PAIRS):
                ins = vec.tensor_scalar(yr[:, q, :], yr[:, q, :], col("ln_g")[:, q:q + 1], col("ln_b")[:, q:q + 1],
                                        ALU.mult, ALU.add)
            v(ins)
            v(vec.tensor_tensor(yr, yr, bonus, ALU.add))
            vec.tensor_tensor(yr, yr, g_c, ALU.mult).then_inc(sem("rw_out"), 1)
            part = U(arena5, 0).rearrange("p (j n) -> p j n", j=2)
            for n in range(2):
                for t in range(TT):
                    bank = V.get(dve)
                    at = slice(n * 512, (n + 1) * 512)
                    vec.tensor_tensor(part[:, t, :], gates2[:, t, n * 512 + D:(n + 1) * 512 + D], bank[:, :],
                                      ALU.mult).then_inc(V.free, 1)
                    V.through(dve)
                    ins = vec.tensor_tensor(yb[:, t, at], yb[:, t, at], part[:, t, :], ALU.add)
                    if n == 1:
                        ins.then_inc(sem("y_merged"), 1)
                    else:
                        v(ins)
            for n in range(2):
                for t in range(TT):
                    bank = V.get(dve)
                    vec.tensor_copy(yb[:, t, n * 512:(n + 1) * 512], bank[:, :]).then_inc(V.free, 1)
            V.through(dve)
            dve.wait_ge(sem("lns_in"), 16)
            layer_norm_dve(lns[:, 0, :], lns[:, 1, :], "peer")

        NH2 = 2 * PH
        NPICK = PH * TOPK
        HID = NKEY * S
        hidden = field[:, 0:HID].rearrange("p (j s) -> p j s", s=S)
        scratch = {"at": 80 * S}

        def take(n):
            scratch["at"] += n
            assert EARLY * S <= scratch["at"] <= HID
            return field[:, scratch["at"] - n:scratch["at"]]

        q_flat = take(NH2 * S)
        qT = q_flat.rearrange("p (h s) -> p h s", h=NH2)
        sums = q_flat[:, 0:PH * 256].rearrange("p (h i j) -> p h i j", h=PH, i=TOPK)
        scores = take(TT * NH2 * NKEY).rearrange("p (t h k) -> p t h k", t=TT, h=NH2)
        spare = take(NPICK * TOPK)
        spare_key, spare_sum = [spare.rearrange("p (h m) -> p h m", h=n) for n in (NH2, PH)]
        one_hot = spare.rearrange("p (h k i) -> p h k i", h=PH, k=TOPK)
        top_s = take(NH2 * TOPK).rearrange("p (h k) -> p h k", h=NH2)
        top_i = take(NH2 * TOPK).bitcast(U32).rearrange("p (h k) -> p h k", h=NH2)
        top_f = take(NH2 * TOPK).rearrange("p (h c k) -> p h c k", h=PH, c=2)
        best = take(TT * NPICK).rearrange("p (t h k) -> p t h k", t=TT, h=PH)
        key_no = take(TT * 2 * NPICK).rearrange("p (t c h k) -> p t c h k", t=TT, c=2, h=PH)
        pos = take(NPICK).bitcast(U32).rearrange("p (h k) -> p h k", h=PH)
        digit_u = take(NPICK).bitcast(U32).rearrange("p (h k) -> p h k", h=PH)
        digit_f = take(NPICK).rearrange("p (h k) -> p h k", h=PH)
        denom = take(TT * PH).rearrange("p (t h) -> p t h", t=TT)

        picksT = field[:, HID:HID + 3 * S].rearrange("p (c s) -> p c s", c=3)
        behind = arena2_r[:, 6 * D - (sum(sizes.values()) - HID):6 * D]
        h_top, h_rest = [behind[:, i * 512:(i + 1) * 512].rearrange("p (b s) -> p b s", b=2) for i in range(2)]
        free_at = where["const"]["decay"][0]
        room = const[:, free_at:free_at + 2048]
        assert where["const"]["causal"][1] == free_at + 2048
        hot = room.rearrange("p (b c q k) -> p b c q k", b=2, c=2, q=GROUP)
        raw_hot = [x.bitcast(BF16).rearrange("p (c q k) -> p c q k", c=2, q=GROUP)
                   for x in (tiny[:, 0:512], field[:, HID + 3 * S:HID + 5 * S])]
        gelu_out = room[:, 0:1024].rearrange("p (b s) -> p b s", b=4)
        numbers = cst("s_t")
        digits = numbers[:, 0:TOPK]

        E_SLOTS = 4
        expert_w, expert_rest, expert_top = [
            x.rearrange("p (g n) -> p g n", g=E_SLOTS)
            for x in (ring_flat[:, 0:4096], ring_flat_r[:, 0:4096], ring_flat_r[:, 4096:8192])]
        y_top_e = yb_r[:, :].rearrange("p (k s) -> p k s", s=S)
        expert_landed = [sem(f"expert_landed{j}") for j in range(E_SLOTS)]
        expert_begun, expert_top_ready = sem("expert_begun"), sem("expert_top_ready")
        u_split, v_split, h_top_ready, h_split = sem("u_split"), sem("v_split"), sem("h_top_ready"), sem("h_split")
        GROUPS = S // GROUP
        LATE = NKEY - EARLY
        seen = {}

        def peer_pe(pe):
            turn_pe(pe, xh, "peer")
            A.evacuated(pe)
            for _ in range(8):
                staying_pe(pe, A)
            A.evacuated(pe)
            keys = next_chunk(pe)[:, :].rearrange("p (h k) -> p h k", h=NH2)
            for t in range(TT):
                for h0 in range(0, NH2, 4):
                    bank = A.take(pe)
                    for h in range(h0, h0 + 4):
                        ins = pe.matmul(bank[:, (h - h0) * P:(h - h0 + 1) * P], qT[:, h, t * P:(t + 1) * P], keys[:, h, :],
                                        start=True, stop=True)
                        if t == h == 0:
                            ins.then_inc(begun, 1)
                    ins.then_inc(A.done, 1)

            tiles, groups, mixed = Count(), Count(), Count()

            def u_tile(g, j):
                bank = A.take(pe)
                slot = tiles.n % E_SLOTS
                tiles.n += 1
                pe.wait_ge(u_split, tiles.at(tiles.n))
                top, rest = [x[:, slot, :].rearrange("p (k n) -> p k n", k=KT) for x in (expert_top, expert_rest)]
                for k in range(KT):
                    first, last = three_passes(pe, bank[:, 0:S], (top[:, k, :], rest[:, k, :]),
                                               (y_top_e[:, k, :], yT_r[:, k, :]), k == 0, k == KT - 1)
                    if k == 0:
                        first.then_inc(expert_begun, 1)
                last.then_inc(A.done, 1)

            def w_group(g, j):
                bank = V.take(pe)
                groups.n += 1
                pe.wait_ge(sem("first_hot_ready"), groups.at(groups.n))
                pe.wait_ge(sem("second_hot_ready"), groups.at(groups.n))
                for q in range(GROUP):
                    ins = pe.matmul(bank[:, q * P:(q + 1) * P], hot[:, j % 2, 0, q, :], hot[:, j % 2, 1, q, :],
                                    start=True, stop=True)
                ins.then_inc(V.done, 1)

            pe.wait_ge(sem("y_split_peer"), 1)
            loop(pe, EARLY, 4, u_tile, [(tiles, 4), (A.filled, 4)])
            pe.wait_ge(sem("picks_ready"), 1)
            for t in range(TT):
                bank = A.take(pe)
                for c, src in enumerate((key_no[:, t, 0], key_no[:, t, 1], best[:, t])):
                    ins = pe.transpose(bank[:, c * P:(c + 1) * P], src.rearrange("p h k -> p (h k)"), ident)
                ins.then_inc(A.done, 1)
            seen["groups"] = V.filled.n
            loop(pe, GROUPS, 4, w_group, [(V.filled, 4), (groups, 4)])
            loop(pe, LATE, 4, u_tile, [(tiles, 4), (A.filled, 4)])

            four = [V.take(pe) for _ in range(4)]

            def v_tile(g, j):
                static = isinstance(g, int)
                first_tile, last_tile = static and g == 0, static and g == NKEY - 1
                slot, b = mixed.n % E_SLOTS, mixed.n % 2
                mixed.n += 1
                pe.wait_ge(v_split, mixed.at(mixed.n))
                pe.wait_ge(h_split, mixed.at(mixed.n))
                for t in range(TT):
                    tokens = slice(t * P, (t + 1) * P)
                    for n in range(2):
                        outs = slice(n * 512, (n + 1) * 512)
                        first, last = three_passes(pe, four[2 * t + n][:, :], (h_top[:, b, tokens], h_rest[:, b, tokens]),
                                                   (expert_top[:, slot, outs], expert_rest[:, slot, outs]),
                                                   first_tile, last_tile)
                        if t == n == 0:
                            first.then_inc(expert_begun, 1)
                        if last_tile:
                            last.then_inc(V.done, 1)

            for g in range(4):
                v_tile(g, g)
            loop(pe, NKEY - 8, 4, lambda g, j: v_tile(None, j), [(mixed, 4)])
            for g in range(NKEY - 4, NKEY):
                v_tile(g, g)

        def peer_act(act):
            turn_act(act)
            for c in range(8):
                bank = A.get(act)
                nc.scalar.copy(qT[:, 2 * c:2 * c + 2, :], two(bank)).then_inc(A.free, 1)
            mark("queries", A.free, 4 + A.emptied.n)
            for t in range(TT):
                for h0 in range(0, NH2, 4):
                    bank = A.get(act)
                    nc.scalar.copy(scores[:, t, h0:h0 + 4, :], bank[:, :].rearrange("p (h k) -> p h k", h=4)
                                   ).then_inc(A.free, 1)
                mark(f"scores{t}", A.free, 4 + A.emptied.n)

            tops, w_banks, late = Count(), Count(), Count()

            def top_expert():
                n = tops.n
                full = 16 * (n // E_SLOTS + 1)
                act.wait_ge(expert_landed[n % E_SLOTS], full if tops.term is None else tops.term * (16 // E_SLOTS) + full)
                if n >= 3:
                    act.wait_ge(expert_begun, tops.at(n - 2))
                tops.n += 1
                nc.scalar.copy(expert_top[:, n % E_SLOTS, :], expert_w[:, n % E_SLOTS, :]).then_inc(expert_top_ready, 1)

            for _ in range(3):
                top_expert()

            def early(g, j):
                bank = A.get(act)
                nc.scalar.activation(hidden[:, bass.ds(g, 1), :].rearrange("p o s -> p (o s)"), bank[:, 0:S],
                                     ACT.Gelu).then_inc(A.free, 1)
                top_expert()

            loop(act, EARLY, 4, early, [(A.emptied, 4), (tops, 4)])
            act.wait_ge(sem("best_ready"), 1)
            nc.scalar.activation(best[:, :], best[:, :], ACT.Exp).then_inc(sem("best_exp"), 1)
            for t in range(TT):
                bank = A.get(act)
                nc.scalar.copy(picksT[:, :, t * P:(t + 1) * P], bank[:, 0:3 * P].rearrange("p (c s) -> p c s", c=3)
                               ).then_inc(A.free, 1)
            mark("picks_turned", A.free, 4 + A.emptied.n)

            w_banks.n = seen["groups"]
            seconds = Count()

            def second_hot():
                seconds.n += 1
                act.wait_ge(sem("raw_hot_ready"), seconds.at(seconds.n))
                if seconds.n > 2:
                    act.wait_ge(V.done, seconds.at(seen["groups"] + seconds.n - 2))
                b = (seconds.n - 1) % 2
                nc.scalar.copy(hot[:, b, 1], raw_hot[b][:, 1]).then_inc(sem("second_hot_ready"), 1)

            def store(g, j):
                if not isinstance(g, int) or g < GROUPS - 2:
                    second_hot()
                w_banks.n += 1
                act.wait_ge(V.done, w_banks.at(w_banks.n))
                bank = V.banks[(w_banks.n - 1) % 4]
                nc.scalar.copy(hidden[:, EARLY:NKEY, bass.ds(g * GROUP, GROUP)],
                               bank[:, :].rearrange("p (q k) -> p k q", q=GROUP)[:, EARLY:NKEY, :]
                               ).then_inc(sem("late_stored"), 1)

            second_hot()
            second_hot()
            loop(act, GROUPS - 2, 4, store, [(w_banks, 4), (seconds, 4)])
            store(GROUPS - 2, 0)
            store(GROUPS - 1, 0)
            seen["late"] = A.emptied.n

            def late_gelu(g, j, first=False):
                bank = A.get(act)
                late.n += 1
                if not first:
                    act.wait_ge(sem("late_scaled"), late.at(late.n - 4))
                nc.scalar.activation(gelu_out[:, (late.n - 1) % 4, :], bank[:, 0:S], ACT.Gelu).then_inc(A.free, 1)
                top_expert()

            for j in range(4):
                late_gelu(j, j, True)
            loop(act, LATE - 4, 4, late_gelu, [(A.emptied, 4), (tops, 4), (late, 4)])
            loop(act, NKEY - 3, 4, lambda g, j: top_expert(), [(tops, 4)])
            root_act(TT)

        def top16_dve(values, indices, src, spare):
            vec = nc.vector
            v(vec.max(values[:, 0:8], src))
            vec.max_index(indices[:, 0:8], values[:, 0:8], src)
            v(vec.match_replace(spare, values[:, 0:8], src, NEG))
            v(vec.max(values[:, 8:16], spare))
            return vec.max_index(indices[:, 8:16], values[:, 8:16], spare)

        def pick_dve(dve, t):
            vec = nc.vector
            await_mark(dve, f"scores{t}")
            for h in range(NH2):
                ins = top16_dve(top_s[:, h, :], top_i[:, h, :], scores[:, t, h, :], spare_key[:, h, :])
            v(ins)
            halves = top_s.rearrange("p (h c) k -> p h c k", c=2)
            v(vec.tensor_copy(top_f.rearrange("p h c k -> p (h c) k"), top_i))
            await_mark(dve, "scores1")
            v(vec.tensor_tensor(sums, halves[:, :, 0, :].unsqueeze(3).broadcast_to([P, PH, TOPK, TOPK]),
                                halves[:, :, 1, :].unsqueeze(2).broadcast_to([P, PH, TOPK, TOPK]), ALU.add))
            flat = sums.rearrange("p h i j -> p h (i j)")
            for h in range(PH):
                ins = top16_dve(best[:, t, h, :], pos[:, h, :], flat[:, h, :], spare_sum[:, h, :])
            v(ins)
            for c, (op, by) in enumerate(((ALU.logical_shift_right, 4), (ALU.bitwise_and, 15))):
                v(vec.tensor_scalar(digit_u, pos, by, None, op))
                v(vec.tensor_copy(digit_f, digit_u))
                v(vec.tensor_tensor(one_hot, digit_f.unsqueeze(3).broadcast_to([P, PH, TOPK, TOPK]),
                                    digits.unsqueeze(1).unsqueeze(1).broadcast_to([P, PH, TOPK, TOPK]),
                                    ALU.is_equal))
                v(vec.tensor_tensor(one_hot, one_hot, top_f[:, :, c, :].unsqueeze(2).broadcast_to([P, PH, TOPK, TOPK]),
                                    ALU.mult))
                v(vec.tensor_reduce(key_no[:, t, c], one_hot, AX_X, ALU.add))
            v(vec.tensor_copy(denom[:, t, :], best[:, t, :, 0]))
            ins = vec.tensor_tensor(best[:, t], best[:, t], denom[:, t, :].unsqueeze(2).broadcast_to([P, PH, TOPK]),
                                    ALU.subtract)
            v(ins)

        def peer_dve(dve):
            vec = nc.vector
            await_mark(dve, "queries")
            split_dve(y_top_e, yT_r, yT).then_inc(sem("y_split_peer"), 1)
            dve.wait_ge(sem("numbers_in"), 16)
            for t in range(TT):
                pick_dve(dve, t)
            vec.memset(small[:, 506:507], 0.0).then_inc(sem("best_ready"), 1)
            dve.wait_ge(sem("best_exp"), 1)
            for t in range(TT):
                v(vec.tensor_reduce(denom[:, t, :], best[:, t], AX_X, ALU.add))
            v(vec.reciprocal(denom, denom))
            for t in range(TT):
                ins = vec.tensor_tensor(best[:, t], best[:, t], denom[:, t, :].unsqueeze(2).broadcast_to([P, PH, TOPK]),
                                        ALU.mult)
            ins.then_inc(sem("picks_ready"), 1)
            await_mark(dve, "picks_turned")
            hots, scaled = Count(), Count()

            def hot_group():
                n = hots.n
                if n >= 2:
                    dve.wait_ge(sem("first_hot_ready"), hots.at(n - 1))
                    dve.wait_ge(sem("second_hot_ready"), hots.at(n - 1))
                at = bass.ds((n if hots.term is None else hots.term + n) * GROUP, GROUP)
                hots.n += 1
                vec.tensor_tensor(raw_hot[n % 2], numbers.unsqueeze(1).unsqueeze(1).broadcast_to([P, 2, GROUP, NKEY]),
                                  picksT[:, 0:2, at].unsqueeze(3).broadcast_to([P, 2, GROUP, NKEY]),
                                  ALU.is_equal).then_inc(sem("raw_hot_ready"), 1)

            def scale_early(g):
                bank = V.get(dve)
                scaled.n += 1
                dve.wait_ge(sem("late_stored"), scaled.at(scaled.n))
                at = hidden[:, 0:EARLY, bass.ds(g * GROUP, GROUP)]
                vec.tensor_tensor(at, at, bank[:, :].rearrange("p (q k) -> p k q", q=GROUP)[:, 0:EARLY, :],
                                  ALU.mult).then_inc(V.free, 1)

            def w_group(g, j):
                hot_group()
                scale_early(g)

            for _ in range(3):
                hot_group()
            loop(dve, GROUPS - 3, 4, w_group, [(V.emptied, 4), (hots, 4), (scaled, 4)])
            for g in range(GROUPS - 3, GROUPS):
                scale_early(g)

            late = Count()

            def scale_late(g, j):
                dve.wait_ge(A.free, late.at(4 + seen["late"] + late.n + 1))
                late.n += 1
                at = hidden[:, bass.ds(g + EARLY, 1), :].rearrange("p o s -> p (o s)")
                vec.tensor_tensor(at, at, gelu_out[:, (late.n - 1) % 4, :], ALU.mult).then_inc(sem("late_scaled"), 1)

            loop(dve, LATE, 4, scale_late, [(late, 4)])
            mixed = Count()

            def v_rests(g, j):
                slot = mixed.n % E_SLOTS
                mixed.n += 1
                dve.wait_ge(expert_top_ready, mixed.at(NKEY + mixed.n))
                vec.tensor_tensor(expert_rest[:, slot, :], expert_w[:, slot, :], expert_top[:, slot, :].bitcast(F32),
                                  ALU.subtract).then_inc(v_split, 1)

            loop(dve, NKEY, 4, v_rests, [(mixed, 4)])
            for i in range(4):
                bank = V.get(dve)
                vec.tensor_copy(yb[:, i // 2, (i % 2) * 512:(i % 2 + 1) * 512], bank[:, :]).then_inc(V.free, 1)
            V.through(dve)
            dve.wait_ge(sem("last_norm_in"), 16)
            layer_norm_dve(yT_flat[:, 0:D], yT_flat[:, D:2 * D], "result")

        def peer_pool(pool):
            rests, hots = Count(), Count()

            def u_rest(g, j):
                slot = rests.n % E_SLOTS
                rests.n += 1
                pool.wait_ge(expert_top_ready, rests.at(rests.n))
                nc.gpsimd.tensor_tensor(expert_rest[:, slot, :], expert_w[:, slot, :], expert_top[:, slot, :].bitcast(F32),
                                        ALU.subtract).then_inc(u_split, 1)

            def gate_group(g, j):
                pool.wait_ge(sem("raw_hot_ready"), hots.at(hots.n + 1))
                if hots.n >= 2 or hots.term is not None:
                    pool.wait_ge(V.done, hots.at(seen["groups"] + hots.n - 1))
                b = hots.n % 2
                hots.n += 1
                pool.sem_inc(sem("first_hot_asked"), 1)
                nc.gpsimd.tensor_tensor(hot[:, b, 0], raw_hot[b][:, 0],
                                        picksT[:, 2, bass.ds(g * GROUP, GROUP)].unsqueeze(2).broadcast_to([P, GROUP, NKEY]),
                                        ALU.mult).then_inc(sem("first_hot_ready"), 1)

            loop(pool, EARLY, 4, u_rest, [(rests, 4)])
            pool.wait_ge(*marks["picks_turned"])
            loop(pool, GROUPS, 4, gate_group, [(hots, 4)])
            loop(pool, LATE, 4, u_rest, [(rests, 4)])
            pool.wait_ge(sem("late_scaled"), LATE)
            tops = Count()

            def h_split_tile(g, j):
                pool.wait_ge(expert_begun, tops.at(NKEY + tops.n))
                b = tops.n % 2
                tops.n += 1
                src = hidden[:, bass.ds(g, 1), :].rearrange("p o s -> p (o s)")
                nc.gpsimd.tensor_copy(h_top[:, b, :], src).then_inc(h_top_ready, 1)
                pool.wait_ge(h_top_ready, tops.at(tops.n))
                pool.sem_inc(sem("h_rest_asked"), 1)
                nc.gpsimd.tensor_tensor(h_rest[:, b, :], src, h_top[:, b, :].bitcast(F32), ALU.subtract
                                        ).then_inc(h_split, 1)

            loop(pool, NKEY, 4, h_split_tile, [(tops, 4)])

        block = ctx.enter_context(nc.Block())
        stream = dram["stream"]

        @block.sync
        def _(sp):
            sp.dma_start(cols[:, :], dram["cols"]).then_inc(sem("cols_in"), 16)
            for g in range(SLOTS):
                sp.dma_start(ring[:, g, :], stream[g]).then_inc(landed[g], 16)
                if g == 1:
                    sp.dma_start(const[:, :], dram["const"]).then_inc(sem("const_in"), 16)
            with sp.Fori(0, stream.shape[0] // SLOTS - 1) as i:
                for j in range(SLOTS):
                    sp.wait_ge(begun, i * SLOTS + j + 2)
                    sp.dma_start(ring[:, j, :], stream[(i + 1) * SLOTS + j]).then_inc(landed[j], 16)
            sp.wait_ge(begun, stream.shape[0] - 3)
            sp.dma_start(numbers, dram["numbers"].partition_broadcast(P)).then_inc(sem("numbers_in"), 16)
            for g in range(E_SLOTS):
                sp.wait_ge(begun, stream.shape[0] - 2 + g // 2)
                sp.dma_start(expert_w[:, g, :], dram["experts"][g]).then_inc(expert_landed[g], 16)
            with sp.Fori(0, 2 * NKEY // E_SLOTS - 1) as i:
                for j in range(E_SLOTS):
                    sp.wait_ge(expert_begun, i * E_SLOTS + j + 2)
                    sp.dma_start(expert_w[:, j, :], dram["experts"][(i + 1) * E_SLOTS + j]).then_inc(expert_landed[j], 16)
            sp.dma_start(yT_flat[:, :], dram["lns"][2 * D:4 * D].partition_broadcast(P)).then_inc(sem("last_norm_in"), 16)
            sp.wait_ge(sem("y_result"), TT)
            sp.dma_start(out.rearrange("b (t p) d -> p (b t) d", p=P), xh[:, :, :]).then_inc(sem("out_written"), 16)
            sp.wait_ge(sem("out_written"), 16)

        @block.tensor
        def _(pe):
            ada_pe(pe)
            ffn_pe(pe, "ffn1")
            mix_pe(pe)
            ffn_pe(pe, "ffn2")
            mix2_pe(pe)
            peer_pe(pe)

        @block.scalar
        def _(act):
            act.dma_start(xh[:, :, :], dram["x"].rearrange("b (t p) d -> p (b t) d", p=P)).then_inc(sem("x_in"), 16)
            act.dma_start(arena2[:, 0:D], dram["gains"][0:D].partition_broadcast(P)).then_inc(sem("first_gain_in"), 16)
            nc.scalar.memzero(small[:, 500:501]).then_inc(A.free, 4)
            ada_act(act)
            act.dma_start(arena2[:, D:6 * D], dram["gains"][D:6 * D].partition_broadcast(P)).then_inc(sem("gains_in"), 16)
            ffn_act(act, "ffn1")
            mix_act(act)
            ffn_act(act, "ffn2")
            mix2_act(act)
            peer_act(act)

        @block.gpsimd
        def _(pool):
            for i, part in enumerate((slice(0, 512 * ADA_FIRST), slice(512 * ADA_FIRST, N_MOD * D))):
                nc.gpsimd.memset(arena1[:, part], 0.0).then_inc(sem("rows_zero"), 1)
                pool.wait_ge(sem("rows_zero"), i + 1)
                pool.dma_start(arena1[0:1, part], dram["ada_b"][part].partition_broadcast(1)).then_inc(sem(f"ada_b_in{i}"), 16)
            peer_pool(pool)

        @block.vector
        def _(dve):
            nc.vector.memset(small[:, 501:502], 0.0).then_inc(V.free, 4)
            dve.wait_ge(sem("x_in"), 16)
            ada_dve(dve)
            ffn_dve(dve, "ffn1", SC1, SH1, G1)
            mix_dve(dve)
            ffn_dve(dve, "ffn2", SC3, SH3, G3)
            mix2_dve(dve)
            peer_dve(dve)



def layout(inputs):
    x = {k: np.asarray(v) for k, v in inputs.items()}
    f = x["w_in"][0]
    m = np.split(f, np.cumsum([512, 512, 512, 512, 8, 512, 512, 512])[:8], axis=1)
    mq, mk, mv, mo, mif, hq, hf, hi, hg = m
    s = x["w_in_2"][0]
    fq, fk, fv, ff, rr, rk, rv, rwa, rg, gates = np.split(
        s, np.cumsum([512, 512, 512, 8, 512, 512, 512, 128, 128])[:9], axis=1)
    ffn = [np.concatenate([gate_up(x[n + "_w_gate"][0], x[n + "_w_up"][0]), down(x[n + "_w_down"][0])])
           for n in ("ffn1", "ffn2")]
    keys = np.ascontiguousarray(x["peer_sub_keys_2"][0].transpose(3, 0, 1, 2)).reshape(1, P, CHUNK)
    ada = a_form(x["ada_w"][0])
    turns = len(ada) - 8
    mixed = np.stack([ffn[0][:turns], ada[8:]], 1)
    stream = np.concatenate([
        ada[:8], mixed.reshape(-1, P, CHUNK), ffn[0][turns:],
        w_form(np.concatenate([mq, mk, hq], 1)), a_form(np.concatenate([hf, mv, mo, hi, hg], 1)),
        a_form(x["w_out"][0]), ffn[1],
        w_form(np.concatenate([fq, fk, rr, rk, rv, rwa, rg], 1)), a_form(np.concatenate([fv, gates], 1)),
        a_form(x["p_fox_2"][0]), a_form(x["p_rwkv_2"][0]), a_form(x["w_o_2"][0]),
        w_form(x["peer_w_q_2"][0]), keys])
    const, const_at = pack(constants())
    mu = x["rwkv_mu_2"][0]
    cols, cols_at = pack({
        "c": columns(x["c"][0]), "conv_w": columns(x["mlstm_conv_w"][0]), "conv_b": columns(x["mlstm_conv_b"][0]),
        "w_mif": narrow(mif), "w_fox": narrow(ff), "gate_b": spread(x["mlstm_gate_b"][0]),
        "fox_b": spread(x["fox_f_bias_2"][0]), "mu": columns(mu), "w0": columns(x["rwkv_w0_2"][0]),
        "a0": columns(x["rwkv_a0_2"][0]), "k_k": columns(x["rwkv_k_k_2"][0]), "k_a": columns(x["rwkv_k_a_2"][0]),
        "r_k": columns(x["rwkv_r_k_2"][0]), "ln_g": columns(x["rwkv_ln_g_2"][0]), "ln_b": columns(x["rwkv_ln_b_2"][0])})
    lora = np.concatenate([np.concatenate([x["rwkv_w2_2"][0], x["rwkv_a2_2"][0]], 0), x["rwkv_g2_2"][0]], 1)
    mats, where = {"stream": stream, "const": const, "cols": cols, "lora": np.ascontiguousarray(lora)}, {}
    mats["gains"] = np.concatenate([x[n][0] for n in ("ffn1_pre_g", "ffn1_post_g", "mix_pre_g", "mix_post_g",
                                                      "ffn2_pre_g", "ffn2_post_g")])
    mats["norms"] = np.concatenate([x["mlstm_norm_g"][0], x["hgrn_norm_g"][0], x["hgrn_lb_logits"].reshape(-1)])
    mats["lns"] = np.concatenate([x[n][0] for n in ("ln1_g_2", "ln1_b_2", "ln2_g_2", "ln2_b_2")])
    mats["ada_b"], mats["x"] = x["ada_b"][0], x["x"]
    u = x["peer_u_2"][0].reshape(NKEY, NKEY, KT, P).transpose(1, 3, 2, 0).reshape(NKEY, P, D)
    v = x["peer_v_2"][0].reshape(NKEY, NKEY, D).transpose(1, 0, 2)
    mats["experts"] = np.concatenate([u, v])
    mats["numbers"] = np.arange(NKEY, dtype=np.float32)
    return {k: np.ascontiguousarray(v) for k, v in mats.items()}, {"const": const_at, "cols": cols_at}


def kernel(**inputs):
    import concourse.bacc as _bacc
    from concourse import mybir as _mybir
    from concourse.bass_utils import run_bass_kernel_spmd as _run

    nc = _bacc.Bacc("TRN2", target_bir_lowering=False, num_devices=1)
    arrays, where = layout(inputs)
    dram = {k: nc.dram_tensor(f"in_{k}", a.shape, _mybir.dt.from_np(a.dtype), kind="ExternalInput").ap()
            for k, a in arrays.items()}
    out = nc.dram_tensor("out_0", (1, S, D), F32, kind="ExternalOutput").ap()
    program(nc, dram, out, where)
    r = _run(nc, [{f"in_{k}": a for k, a in arrays.items()}], core_ids=[0])
    return r.results[0]["out_0"]
```
